# Optimizing a Trainium2 kernel written in Bass

```python
import jax, jax.numpy as jnp
from jax import lax
import numpy as np

D_MODEL = 1024
BATCH = 1
SEQ = 256
DEPTH = 1

CHUNK = 64
N_META = 16
HEAD_DIM = 64
Q_BLOCK = 128
POOL_WINDOWS = (2, 4, 8, 16)
N_POOL_GROUPS = 4
POOL_WIDTH = D_MODEL // 4
POOL_GROUP = POOL_WIDTH // N_POOL_GROUPS
FOX_HEADS = (3 * D_MODEL // 8) // HEAD_DIM
FOX_WIDTH = FOX_HEADS * HEAD_DIM
SB_HEADS = (3 * D_MODEL // 8) // HEAD_DIM
SB_WIDTH = SB_HEADS * HEAD_DIM
MIX_WIDTH = POOL_WIDTH + FOX_WIDTH + SB_WIDTH
IN_WIDTH = POOL_WIDTH + 3 * FOX_WIDTH + FOX_HEADS + 3 * SB_WIDTH
IN_SPLITS = (
    POOL_WIDTH,
    POOL_WIDTH + FOX_WIDTH,
    POOL_WIDTH + 2 * FOX_WIDTH,
    POOL_WIDTH + 3 * FOX_WIDTH,
    POOL_WIDTH + 3 * FOX_WIDTH + FOX_HEADS,
    POOL_WIDTH + 3 * FOX_WIDTH + FOX_HEADS + SB_WIDTH,
    POOL_WIDTH + 3 * FOX_WIDTH + FOX_HEADS + 2 * SB_WIDTH,
)
D_FF = ((8 * D_MODEL // 3 + 255) // 256) * 256
EPS = 1e-6


def rmsnorm(x, g):
    x32 = x.astype(jnp.float32)
    y = x32 * lax.rsqrt(jnp.mean(x32 * x32, axis=-1, keepdims=True) + EPS)
    return (y * g.astype(jnp.float32)).astype(x.dtype)

def head_rmsnorm(y, gain, n_heads):
    b, l, _ = y.shape
    y32 = y.reshape(b, l, n_heads, HEAD_DIM).astype(jnp.float32)
    y32 = y32 * lax.rsqrt(jnp.mean(y32 * y32, axis=-1, keepdims=True) + EPS)
    return (y32.reshape(b, l, n_heads * HEAD_DIM) * gain.astype(jnp.float32)).astype(y.dtype)

def split_heads(t, n_heads):
    b, l, _ = t.shape
    return t.reshape(b, l, n_heads, HEAD_DIM).transpose(0, 2, 1, 3)

def query_blocks(t):
    l = t.shape[2]
    t = t.reshape(t.shape[:2] + (l // Q_BLOCK, Q_BLOCK) + t.shape[3:])
    return jnp.moveaxis(t, 2, 0)

def merge_blocks(o):
    nblk, b, h, q, d = o.shape
    o = jnp.moveaxis(o, 0, 2).reshape(b, h, nblk * q, d)
    return o.transpose(0, 2, 1, 3).reshape(b, nblk * q, h * d)

def multiscale_pool_mixer(u, pool_w, pool_scale):
    b, l, _ = u.shape
    ug = u.reshape(b, l, N_POOL_GROUPS, POOL_GROUP).astype(jnp.float32)
    cs = jnp.cumsum(ug, axis=1)
    cs0 = jnp.concatenate([jnp.zeros_like(cs[:, :1]), cs], axis=1)
    t1 = jnp.arange(1, l + 1)[:, None]
    win = jnp.array(POOL_WINDOWS, dtype=jnp.int32)[None, :]
    lo = jnp.maximum(t1 - win, 0)
    window_sum = cs - cs0[:, lo, jnp.arange(N_POOL_GROUPS)[None, :]]
    mean = window_sum / (t1 - lo).astype(jnp.float32)[None, :, :, None]
    d = (mean - ug).astype(u.dtype)
    mixed = jnp.einsum('blgc,gcd->blgd', d, pool_w)
    return mixed.reshape(b, l, POOL_WIDTH) * pool_scale

def forgetting_attention(q, k, v, log_f):
    c = jnp.cumsum(log_f.astype(jnp.float32), axis=1).transpose(0, 2, 1)
    l = q.shape[2]
    pos = jnp.arange(l)
    k32 = k.astype(jnp.float32)
    scale = HEAD_DIM ** -0.5

    def block(args):
        qb, cb, tq = args
        s = jnp.einsum('bhqd,bhkd->bhqk', qb.astype(jnp.float32), k32) * scale
        s = s + cb[..., None] - c[:, :, None, :]
        s = jnp.where(pos[None, :] <= tq[:, None], s, -jnp.inf)
        p = jax.nn.softmax(s, axis=-1)
        return jnp.einsum('bhqk,bhkd->bhqd', p.astype(v.dtype), v)

    o = lax.map(block, (query_blocks(q), query_blocks(c), pos.reshape(-1, Q_BLOCK)))
    return merge_blocks(o)

def stick_breaking_attention(q, k, v):
    l = q.shape[2]
    pos = jnp.arange(l)
    k32 = k.astype(jnp.float32)
    scale = HEAD_DIM ** -0.5

    def block(args):
        qb, tq = args
        z = jnp.einsum('bhqd,bhkd->bhqk', qb.astype(jnp.float32), k32) * scale
        strict = pos[None, :] < tq[:, None]
        log_beta = jax.nn.log_sigmoid(z)
        log_1m = jnp.where(strict, jax.nn.log_sigmoid(-z), 0.0)
        later = lax.cumsum(log_1m, axis=3, reverse=True) - log_1m
        a = jnp.where(strict, jnp.exp(log_beta + later), 0.0)
        return jnp.einsum('bhqk,bhkd->bhqd', a.astype(v.dtype), v)

    o = lax.map(block, (query_blocks(q), pos.reshape(-1, Q_BLOCK)))
    return merge_blocks(o)

def first_inputs(seed: int = 0) -> dict:
    key = jax.random.key(seed)
    ks = jax.random.split(key, 15)
    f32 = jnp.float32
    n = jax.random.normal
    return {
        'x': n(ks[0], (BATCH, SEQ, D_MODEL), f32),
        'meta_tokens': n(ks[1], (N_META, D_MODEL), f32),
        'norm1': 1.0 + 0.05 * n(ks[2], (DEPTH, D_MODEL), f32),
        'w_in': n(ks[3], (DEPTH, D_MODEL, IN_WIDTH), f32) * D_MODEL ** -0.5,
        'forget_bias': jax.random.uniform(ks[4], (DEPTH, FOX_HEADS), f32, 1.0, 4.0),
        'pool_w': n(ks[5], (DEPTH, N_POOL_GROUPS, POOL_GROUP, POOL_GROUP), f32) * POOL_GROUP ** -0.5,
        'pool_scale': 1.0 + 0.1 * n(ks[6], (DEPTH, POOL_WIDTH), f32),
        'fox_out_gain': 1.0 + 0.05 * n(ks[7], (DEPTH, FOX_WIDTH), f32),
        'sb_out_gain': 1.0 + 0.05 * n(ks[8], (DEPTH, SB_WIDTH), f32),
        'w_out': n(ks[9], (DEPTH, MIX_WIDTH, D_MODEL), f32) * MIX_WIDTH ** -0.5,
        'norm2': 1.0 + 0.05 * n(ks[10], (DEPTH, D_MODEL), f32),
        'w_gate': n(ks[11], (DEPTH, D_MODEL, D_FF), f32) * D_MODEL ** -0.5,
        'w_up': n(ks[12], (DEPTH, D_MODEL, D_FF), f32) * D_MODEL ** -0.5,
        'w_down': n(ks[13], (DEPTH, D_FF, D_MODEL), f32) * D_FF ** -0.5,
        'final_norm': 1.0 + 0.05 * n(ks[14], (D_MODEL,), f32),
    }

def first_block(x, meta_tokens, norm1, w_in, forget_bias, pool_w, pool_scale, fox_out_gain,
              sb_out_gain, w_out, norm2, w_gate, w_up, w_down, final_norm):
    b, s_len, _ = x.shape
    l = N_META + s_len
    l_pad = -(-l // Q_BLOCK) * Q_BLOCK
    meta = jnp.broadcast_to(meta_tokens[None].astype(x.dtype), (b, N_META, D_MODEL))
    h = jnp.concatenate([meta, x, jnp.zeros((b, l_pad - l, D_MODEL), x.dtype)], axis=1)

    for i in range(DEPTH):
        a = rmsnorm(h, norm1[i])
        proj = a @ w_in[i]
        u, qf, kf, vf, fl, qs, ks_, vs = jnp.split(proj, IN_SPLITS, axis=-1)
        y_pool = multiscale_pool_mixer(u, pool_w[i], pool_scale[i])
        log_f = jax.nn.log_sigmoid(fl.astype(jnp.float32) + forget_bias[i].astype(jnp.float32))
        y_fox = forgetting_attention(split_heads(qf, FOX_HEADS), split_heads(kf, FOX_HEADS),
                                     split_heads(vf, FOX_HEADS), log_f)
        y_fox = head_rmsnorm(y_fox, fox_out_gain[i], FOX_HEADS)
        y_sb = stick_breaking_attention(split_heads(qs, SB_HEADS), split_heads(ks_, SB_HEADS),
                                        split_heads(vs, SB_HEADS))
        y_sb = head_rmsnorm(y_sb, sb_out_gain[i], SB_HEADS)
        h = h + jnp.concatenate([y_pool, y_fox, y_sb], axis=-1) @ w_out[i]
        a = rmsnorm(h, norm2[i])
        h = h + (jax.nn.silu(a @ w_gate[i]) * (a @ w_up[i])) @ w_down[i]

    h = rmsnorm(h, final_norm)
    return h[:, N_META:N_META + s_len]


D_MIX = D_MODEL
D_RWKV = D_MIX // 2
D_NSA = D_MIX - D_RWKV
RWKV_HEADS = D_RWKV // HEAD_DIM
NSA_Q_HEADS = D_NSA // HEAD_DIM
NSA_KV_HEADS = 2
NSA_GROUP = NSA_Q_HEADS // NSA_KV_HEADS
D_KV = NSA_KV_HEADS * HEAD_DIM
LORA_W = 64
LORA_A = 64
LORA_G = 128
RWKV_SIZES = (D_RWKV, D_RWKV, D_RWKV, LORA_W, LORA_A, LORA_G)
N_RWKV_COLS = sum(RWKV_SIZES)
CMP_BLOCK = 32
CMP_STRIDE = 16
CMP_HIDDEN = 256
SEL_BLOCK = 64
SEL_TOPK = 16
WINDOW = 512
NSA_SIZES = (D_NSA, D_KV, D_KV, D_KV, D_KV, D_KV, D_KV, 3 * NSA_Q_HEADS)
N_NSA_COLS = sum(NSA_SIZES)
N_IN = N_RWKV_COLS + N_NSA_COLS
D_FF_2 = -(-8 * D_MODEL // (3 * 256)) * 256
NORM_EPS = 1e-6
GN_EPS = 64e-5
NEG = -1e30
BIG = 1e30


def _split(z, sizes):
    return jnp.split(z, [int(c) for c in np.cumsum(sizes)[:-1]], axis=-1)

def rms_norm(x, g):
    xf = x.astype(jnp.float32)
    y = xf * lax.rsqrt(jnp.mean(xf * xf, axis=-1, keepdims=True) + NORM_EPS)
    return (y * g).astype(x.dtype)

def alibi_slopes(n_heads):
    return 2.0 ** (-8.0 * jnp.arange(1, n_heads + 1, dtype=jnp.float32) / n_heads)

def swiglu(x, w_gate, w_up, w_down):
    return (jax.nn.silu(x @ w_gate) * (x @ w_up)) @ w_down

def rwkv7_time_mix(p, mu, w0, w2, a0, a2, g2, k_k, k_a, r_k, lnx_w, lnx_b):
    B, T, _ = p.shape
    H, N = RWKV_HEADS, HEAD_DIM
    p = p.astype(jnp.float32)
    p_prev = jnp.pad(p, ((0, 0), (1, 0), (0, 0)))[:, :-1]
    p = p + mu * (p_prev - p)
    r, k, v, dw, da, dg = _split(p, RWKV_SIZES)
    w_log = -jax.nn.softplus(-(w0 + jnp.tanh(dw) @ w2)) - 0.5
    decay = jnp.exp(-jnp.exp(w_log))
    a = jax.nn.sigmoid(a0 + da @ a2)
    g = jax.nn.sigmoid(dg) @ g2
    heads = lambda z: z.reshape(B, T, H, N)
    kk = heads(k * k_k)
    kk = kk / jnp.maximum(jnp.sqrt(jnp.sum(kk * kk, axis=-1, keepdims=True)), 1e-12)
    k = k * (1.0 + (a - 1.0) * k_a)
    r, k, v, decay, a = map(heads, (r, k, v, decay, a))
    xs = tuple(jnp.moveaxis(z, 1, 0) for z in (r, decay, k, v, -kk, kk * a))

    def step(S, inp):
        r_t, w_t, k_t, v_t, a_t, b_t = inp
        sa = jnp.einsum('bhvk,bhk->bhv', S, a_t)
        S = S * w_t[:, :, None, :] + sa[..., None] * b_t[:, :, None, :] + v_t[..., None] * k_t[:, :, None, :]
        return S, jnp.einsum('bhvk,bhk->bhv', S, r_t)

    S0 = jnp.zeros((B, H, N, N), jnp.float32)
    _, y = lax.scan(step, S0, xs)
    y = jnp.moveaxis(y, 0, 1)
    mean = jnp.mean(y, axis=-1, keepdims=True)
    var = jnp.mean(jnp.square(y - mean), axis=-1, keepdims=True)
    y = ((y - mean) * lax.rsqrt(var + GN_EPS)).reshape(B, T, D_RWKV) * lnx_w + lnx_b
    bonus = jnp.sum(r * k * r_k, axis=-1, keepdims=True) * v
    return (y + bonus.reshape(B, T, D_RWKV)) * g

def nsa_attention(p, pe_k, pe_v, ck1, ck2, cv1, cv2):
    B, T, _ = p.shape
    Hk, G, dk = NSA_KV_HEADS, NSA_GROUP, HEAD_DIM
    p = p.astype(jnp.float32)
    q, kc, vc, ks, vs, kw, vw, gl = _split(p, NSA_SIZES)
    q = q.reshape(B, T, Hk, G, dk) * (dk ** -0.5)
    gates = jax.nn.sigmoid(gl).reshape(B, T, Hk, G, 3)
    kv_heads = lambda z: z.reshape(B, T, Hk, dk)

    n_cmp = (T - CMP_BLOCK) // CMP_STRIDE + 1
    cmp_idx = np.arange(n_cmp)[:, None] * CMP_STRIDE + np.arange(CMP_BLOCK)[None, :]

    def compress(z, pe, w1, w2):
        blk = kv_heads(z)[:, cmp_idx] + pe[None, None, :, None, :]
        blk = jnp.transpose(blk, (0, 3, 1, 2, 4)).reshape(B, Hk, n_cmp, CMP_BLOCK * dk)
        return jax.nn.gelu(blk @ w1) @ w2

    k_cmp = compress(kc, pe_k, ck1, ck2)
    v_cmp = compress(vc, pe_v, cv1, cv2)
    cmp_start = np.arange(n_cmp) * CMP_STRIDE
    cmp_end = jnp.asarray(cmp_start + CMP_BLOCK - 1)

    n_sel = T // SEL_BLOCK
    top_k = min(SEL_TOPK, n_sel)
    sel_start = np.arange(n_sel) * SEL_BLOCK
    ov = np.clip(np.minimum(cmp_start[:, None] + CMP_BLOCK, sel_start[None, :] + SEL_BLOCK)
                 - np.maximum(cmp_start[:, None], sel_start[None, :]), 0, None) / CMP_STRIDE
    ov = jnp.asarray(ov, jnp.float32)
    k_sel = kv_heads(ks).reshape(B, n_sel, SEL_BLOCK, Hk, dk).transpose(0, 3, 1, 2, 4)
    v_sel = kv_heads(vs).reshape(B, n_sel, SEL_BLOCK, Hk, dk).transpose(0, 3, 1, 2, 4)

    pad = ((0, 0), (WINDOW, 0), (0, 0), (0, 0))
    k_win = jnp.pad(kv_heads(kw), pad)
    v_win = jnp.pad(kv_heads(vw), pad)

    slopes = alibi_slopes(NSA_Q_HEADS).reshape(Hk, G)
    b_ix = jnp.arange(B)[:, None, None, None]
    h_ix = jnp.arange(Hk)[None, :, None, None]
    blk_ids = jnp.arange(n_sel)

    def query_block(qi):
        q0 = qi * Q_BLOCK
        t = q0 + jnp.arange(Q_BLOCK)
        qb = lax.dynamic_slice_in_dim(q, q0, Q_BLOCK, 1)
        gb = lax.dynamic_slice_in_dim(gates, q0, Q_BLOCK, 1)

        s = jnp.einsum('bqhgd,bhcd->bhgqc', qb, k_cmp)
        s = s - slopes[None, :, :, None, None] * jnp.abs(t[:, None] - cmp_end[None, :])
        ok_c = cmp_end[None, :] <= t[:, None]
        p_c = jax.nn.softmax(jnp.where(ok_c, s, NEG), axis=-1) * jnp.any(ok_c, axis=-1)[:, None]
        o_c = jnp.einsum('bhgqc,bhcd->bqhgd', p_c, v_cmp)

        imp = jnp.einsum('bhgqc,cn->bhqn', p_c, ov)
        cur = t // SEL_BLOCK
        valid = blk_ids[None, :] <= cur[:, None]
        forced = (blk_ids[None, :] == 0) | (blk_ids[None, :] == cur[:, None]) | (blk_ids[None, :] == cur[:, None] - 1)
        imp = jnp.where(valid, jnp.where(forced, BIG, imp), NEG)
        top_v, top_i = lax.top_k(imp, top_k)
        kg = k_sel[b_ix, h_ix, top_i]
        vg = v_sel[b_ix, h_ix, top_i]
        pos = top_i[..., None] * SEL_BLOCK + jnp.arange(SEL_BLOCK)
        s = jnp.einsum('bqhgd,bhqnjd->bhgqnj', qb, kg)
        s = s - slopes[None, :, :, None, None, None] * jnp.abs(t[:, None, None] - pos)[:, :, None]
        ok_s = ((top_v > 0.5 * NEG)[..., None] & (pos <= t[:, None, None]))[:, :, None]
        s = jnp.where(ok_s, s, NEG).reshape(B, Hk, G, Q_BLOCK, top_k * SEL_BLOCK)
        p_s = jax.nn.softmax(s, axis=-1)
        o_s = jnp.einsum('bhgqm,bhqmd->bqhgd', p_s, vg.reshape(B, Hk, Q_BLOCK, top_k * SEL_BLOCK, dk))

        kwb = lax.dynamic_slice_in_dim(k_win, q0, Q_BLOCK + WINDOW, 1)
        vwb = lax.dynamic_slice_in_dim(v_win, q0, Q_BLOCK + WINDOW, 1)
        pos_w = q0 - WINDOW + jnp.arange(Q_BLOCK + WINDOW)
        dist = t[:, None] - pos_w[None, :]
        s = jnp.einsum('bqhgd,bkhd->bhgqk', qb, kwb) - slopes[None, :, :, None, None] * jnp.abs(dist)
        ok_w = (pos_w[None, :] >= 0) & (dist >= 0) & (dist < WINDOW)
        p_w = jax.nn.softmax(jnp.where(ok_w, s, NEG), axis=-1)
        o_w = jnp.einsum('bhgqk,bkhd->bqhgd', p_w, vwb)

        return gb[..., 0:1] * o_c + gb[..., 1:2] * o_s + gb[..., 2:3] * o_w

    out = lax.map(query_block, jnp.arange(T // Q_BLOCK))
    return jnp.moveaxis(out, 0, 1).reshape(B, T, D_NSA)

def second_inputs(seed: int = 0) -> dict:
    key = jax.random.key(seed)
    ks = jax.random.split(key, 26)
    f32 = jnp.float32
    L = DEPTH

    def nrm(k, shape, scale):
        return jax.random.normal(k, shape, f32) * scale

    def gain(k, shape):
        return 1.0 + 0.02 * jax.random.normal(k, shape, f32)

    return {
        'x': nrm(ks[0], (BATCH, SEQ, D_MODEL), 1.0),
        'norm1_g': gain(ks[1], (L, D_MODEL)),
        'w_in': nrm(ks[2], (L, D_MODEL, N_IN), D_MODEL ** -0.5),
        'mu_shift': jax.random.uniform(ks[3], (L, N_RWKV_COLS), f32),
        'rwkv_w0': jax.random.uniform(ks[4], (L, D_RWKV), f32, -4.0, 1.0),
        'rwkv_w2': nrm(ks[5], (L, LORA_W, D_RWKV), 0.1),
        'rwkv_a0': nrm(ks[6], (L, D_RWKV), 0.5),
        'rwkv_a2': nrm(ks[7], (L, LORA_A, D_RWKV), 0.1),
        'rwkv_g2': nrm(ks[8], (L, LORA_G, D_RWKV), LORA_G ** -0.5),
        'rwkv_k_k': 0.85 + 0.05 * jax.random.normal(ks[9], (L, D_RWKV), f32),
        'rwkv_k_a': gain(ks[10], (L, D_RWKV)),
        'rwkv_r_k': nrm(ks[11], (L, RWKV_HEADS, HEAD_DIM), 0.1),
        'rwkv_lnx_w': gain(ks[12], (L, D_RWKV)),
        'rwkv_lnx_b': nrm(ks[13], (L, D_RWKV), 0.01),
        'nsa_pe_k': nrm(ks[14], (L, CMP_BLOCK, HEAD_DIM), 0.1),
        'nsa_pe_v': nrm(ks[15], (L, CMP_BLOCK, HEAD_DIM), 0.1),
        'nsa_cmp_k_w1': nrm(ks[16], (L, CMP_BLOCK * HEAD_DIM, CMP_HIDDEN), (CMP_BLOCK * HEAD_DIM) ** -0.5),
        'nsa_cmp_k_w2': nrm(ks[17], (L, CMP_HIDDEN, HEAD_DIM), CMP_HIDDEN ** -0.5),
        'nsa_cmp_v_w1': nrm(ks[18], (L, CMP_BLOCK * HEAD_DIM, CMP_HIDDEN), (CMP_BLOCK * HEAD_DIM) ** -0.5),
        'nsa_cmp_v_w2': nrm(ks[19], (L, CMP_HIDDEN, HEAD_DIM), CMP_HIDDEN ** -0.5),
        'w_out': nrm(ks[20], (L, D_MIX, D_MODEL), D_MIX ** -0.5),
        'norm2_g': gain(ks[21], (L, D_MODEL)),
        'ffn_w_gate': nrm(ks[22], (L, D_MODEL, D_FF_2), D_MODEL ** -0.5),
        'ffn_w_up': nrm(ks[23], (L, D_MODEL, D_FF_2), D_MODEL ** -0.5),
        'ffn_w_down': nrm(ks[24], (L, D_FF_2, D_MODEL), D_FF_2 ** -0.5),
        'norm_f_g': gain(ks[25], (D_MODEL,)),
    }

def second_block(x, norm1_g, w_in, mu_shift, rwkv_w0, rwkv_w2, rwkv_a0, rwkv_a2, rwkv_g2,
              rwkv_k_k, rwkv_k_a, rwkv_r_k, rwkv_lnx_w, rwkv_lnx_b, nsa_pe_k, nsa_pe_v,
              nsa_cmp_k_w1, nsa_cmp_k_w2, nsa_cmp_v_w1, nsa_cmp_v_w2, w_out, norm2_g,
              ffn_w_gate, ffn_w_up, ffn_w_down, norm_f_g):
    h = x
    for i in range(DEPTH):
        u = rms_norm(h, norm1_g[i])
        p_rwkv, p_nsa = jnp.split(u @ w_in[i], [N_RWKV_COLS], axis=-1)
        y_rwkv = rwkv7_time_mix(p_rwkv, mu_shift[i], rwkv_w0[i], rwkv_w2[i], rwkv_a0[i], rwkv_a2[i],
                                rwkv_g2[i], rwkv_k_k[i], rwkv_k_a[i], rwkv_r_k[i],
                                rwkv_lnx_w[i], rwkv_lnx_b[i])
        y_nsa = nsa_attention(p_nsa, nsa_pe_k[i], nsa_pe_v[i], nsa_cmp_k_w1[i], nsa_cmp_k_w2[i],
                              nsa_cmp_v_w1[i], nsa_cmp_v_w2[i])
        y = jnp.concatenate([y_rwkv, y_nsa], axis=-1).astype(h.dtype)
        h = h + y @ w_out[i]
        h = h + swiglu(rms_norm(h, norm2_g[i]), ffn_w_gate[i], ffn_w_up[i], ffn_w_down[i])
    return rms_norm(h, norm_f_g)


def setup_inputs(seed=0):
    out = dict(first_inputs(seed))
    for name, value in second_inputs(seed + 1).items():
        if name != "x":
            out[name + "_2"] = value
    return out


def reference(
    x, meta_tokens, norm1, w_in, forget_bias, pool_w, pool_scale, fox_out_gain, sb_out_gain,
    w_out, norm2, w_gate, w_up, w_down, final_norm, norm1_g_2, w_in_2, mu_shift_2, rwkv_w0_2,
    rwkv_w2_2, rwkv_a0_2, rwkv_a2_2, rwkv_g2_2, rwkv_k_k_2, rwkv_k_a_2, rwkv_r_k_2,
    rwkv_lnx_w_2, rwkv_lnx_b_2, nsa_pe_k_2, nsa_pe_v_2, nsa_cmp_k_w1_2, nsa_cmp_k_w2_2,
    nsa_cmp_v_w1_2, nsa_cmp_v_w2_2, w_out_2, norm2_g_2, ffn_w_gate_2, ffn_w_up_2, ffn_w_down_2,
    norm_f_g_2,
):
    x = first_block(
        x, meta_tokens, norm1, w_in, forget_bias, pool_w, pool_scale, fox_out_gain, sb_out_gain,
        w_out, norm2, w_gate, w_up, w_down, final_norm,
    )
    return second_block(
        x, norm1_g_2, w_in_2, mu_shift_2, rwkv_w0_2, rwkv_w2_2, rwkv_a0_2, rwkv_a2_2, rwkv_g2_2,
        rwkv_k_k_2, rwkv_k_a_2, rwkv_r_k_2, rwkv_lnx_w_2, rwkv_lnx_b_2, nsa_pe_k_2, nsa_pe_v_2,
        nsa_cmp_k_w1_2, nsa_cmp_k_w2_2, nsa_cmp_v_w1_2, nsa_cmp_v_w2_2, w_out_2, norm2_g_2,
        ffn_w_gate_2, ffn_w_up_2, ffn_w_down_2, norm_f_g_2,
    )


_drawn_inputs = setup_inputs


def setup_inputs(seed=0):
    import zlib

    import numpy as np

    out = dict(_drawn_inputs(seed))
    spreads = {}
    factors = {'norm1_g_2': 3.236,
     'rwkv_k_k_2': 46.632,
     'rwkv_k_a_2': 4.785,
     'rwkv_lnx_w_2': 55.032,
     'rwkv_lnx_b_2': 200.0,
     'nsa_pe_k_2': 92.756,
     'nsa_pe_v_2': 24.672,
     'norm2_g_2': 13.166,
     'norm_f_g_2': 22.39}
    for name, (base, spread) in spreads.items():
        noise = np.random.default_rng([zlib.crc32(name.encode()), seed]).standard_normal(out[name].shape)
        drawn = base * np.exp(spread * noise) if base else spread * noise
        out[name] = __import__('jax').numpy.asarray(drawn.astype(out[name].dtype))
    for name, factor in factors.items():
        out[name] = (out[name] * factor).astype(out[name].dtype)
    return out
```

```python
from contextlib import ExitStack

import numpy as np

import concourse.bass as bass
from concourse import mybir

P = 128
ALU = mybir.AluOpType
ACT = mybir.ActivationFunctionType
AX = mybir.AxisListType
F32 = mybir.dt.float32

D = 1024
KT = D // P
SEQ = 256
META = 16
CTX = META + SEQ
HD = 64
EPS = 1e-6
NEG = -1e30
DFF = 2816
FT = DFF // P

HEADS1 = 6
KS0, QS0, VS0, VF0, KF0, QF0, U0, FL0 = 0, 3, 6, 9, 12, 15, 18, 20
TILES1 = 21
POOL_WINDOWS = (2, 4, 8, 16)
META_SLOT = (0, 2, 1)

R0, K0, V0, WA0, G0, Q0, KC0, VC0, KS1, VS1, KW1, VW1, GL0 = 0, 4, 8, 12, 13, 14, 18, 19, 20, 21, 22, 23, 24
SHIFTED = 14
TILES2 = 25
PAIRS = 4
CHUNK = 64
CHUNKS = SEQ // CHUNK
PACKS = PAIRS * CHUNKS
LEVELS = 6
DECAY = float(np.exp(-0.5))
GN_EPS = 64e-5
GQA, KVH = 4, 2
NQH = GQA * KVH
CMP_BLOCK, CMP_STRIDE = 32, 16
N_CMP = (SEQ - CMP_BLOCK) // CMP_STRIDE + 1
CMP_PAD = 16
CMP_PAIRS = CMP_BLOCK // 2
CMP_HIDDEN = 256
EXP_MAX = 43.0
GELU = 2.0 * float(np.sqrt(2.0 / np.pi))

TILE = KT * P
BLOCK = 2 * TILE
RING = 4


def blocks_of(tiles):
    return -(-tiles // 2)


B_IN1 = 0
B_OUT1 = B_IN1 + blocks_of(TILES1)
B_UP1 = B_OUT1 + KT // 2
B_DOWN1 = B_UP1 + FT
B_IN2 = B_DOWN1 + FT // 2
B_CMP = B_IN2 + blocks_of(TILES2)
B_OUT2 = B_CMP + 4
B_UP2 = B_OUT2 + KT // 2
B_DOWN2 = B_UP2 + FT

NORMS = ("norm1", "norm_ff1", "norm3", "norm4", "norm_ff2", "norm6")
FEEDING = ("norm1", "norm_ff1", "norm4", "norm_ff2")


def nth(name):
    return NORMS.index(name) + 1


def normed(name, k):
    return FEEDING.index(name) * KT + k + 1




def constant_tables():
    i = np.arange(P)
    c = {}
    c["ident"] = np.eye(P)
    c["ones"] = np.ones((P, P))
    c["neg_ones"] = -np.ones((P, P))
    c["neg_from"] = -(i[:, None] >= i[None, :]).astype(float)
    strict = i[:, None] < i[None, :]
    c["strict"] = strict.astype(float)
    c["strict_add"] = np.where(strict, 0.0, NEG)
    a = np.where(np.arange(META + P)[None, :] <= META + i[:, None], 0.0, NEG)
    b = np.where(np.arange(CTX)[None, :] <= META + P + i[:, None], 0.0, NEG)
    c["causal1"] = np.concatenate([a, b], 1)
    c["head_ones"] = np.kron(np.eye(2), np.ones((HD, HD)))
    sel = np.zeros((P, HEADS1, P))
    for h in range(HEADS1):
        sel[h, h] = 1.0
    c["pick_head"] = sel.reshape(P, -1)
    c["eps"] = np.full((P, 1), EPS)
    c["one"] = np.ones((P, 1))
    slopes = 2.0 ** (-8.0 * np.arange(1, NQH + 1) / NQH)
    k = np.arange(SEQ)
    dist = (P + i[:, None]) - k[None, :]
    c["alibi"] = np.where(dist[:, None, :] >= 0, -slopes[None, :, None] * dist[:, None, :], NEG).reshape(P, -1)
    end = np.arange(CMP_PAD) * CMP_STRIDE + CMP_BLOCK - 1
    t = i[:, None] + P * np.arange(2)[None, :]
    dist = t[:, :, None] - end
    ok = (dist >= 0) & (np.arange(CMP_PAD) < N_CMP)
    c["cmp_bias"] = np.where(ok[:, :, None, :], -slopes[None, None, :, None] * dist[:, :, None, :], NEG).reshape(P, -1)
    c["cmp_any"] = ok.any(-1).astype(float)
    rows = np.arange(P)
    c["cmp_spread"] = ((rows[None, :] % CMP_PAD == i[:, None]) & (i[:, None] < N_CMP)).astype(float)
    m = np.zeros((P, GQA, P))
    for r in rows:
        head = r // CMP_PAD
        m[r, head % GQA, HD * (head // GQA):HD * (head // GQA) + HD] = 1.0
    c["cmp_own"] = m.reshape(P, -1)
    same = i[:, None] // CHUNK == i[None, :] // CHUNK
    before = same & (i[:, None] < i[None, :])
    upto = same & (i[:, None] <= i[None, :])
    c["pack_masks"] = np.concatenate([before, upto, before, upto], 1).astype(float)
    lv = []
    for level in range(LEVELS):
        w = 2 << level
        lv.append((i[:, None] // w == i[None, :] // w) & (i[:, None] % w < w // 2) & (i[None, :] % w >= w // 2))
    c["join"] = np.concatenate(lv, 1).astype(float)
    c["join0_t"] = lv[0].T.astype(float)
    c["gn_eps"] = np.full((P, 1), GN_EPS)
    return {k: np.ascontiguousarray(v, np.float32) for k, v in c.items()}


def columns(widths):
    at, out = 0, {}
    for k, w in widths.items():
        out[k] = (at, w)
        at += w
    return out, at


CONST_AT, CONST_W = columns({k: v.shape[1] for k, v in constant_tables().items()})

VEC_WIDTHS = {
    "norm1": KT, "norm2": KT, "norm3": KT,
    "norm4": KT, "norm5": KT, "norm6": KT, "mu": SHIFTED, "w0": PAIRS, "a0": PAIRS, "k_k": PAIRS, "k_a": PAIRS,
    "r_k": PAIRS, "w2a2": PAIRS * P, "g2": PAIRS * P, "lnx_w": PAIRS * HD, "lnx_b": PAIRS * HD,
    "pe_k": CMP_PAIRS, "pe_v": CMP_PAIRS, "cmp_w2k": 2 * HD, "cmp_w2v": 2 * HD,
    "fox_gain": 3, "sb_gain": 3, "pool_scale": 2, "forget_bias": 1, "pool_w": 2 * P,
}
VEC_AT, VEC_W = columns(VEC_WIDTHS)


def build_program(nc, xT, weights, consts, vecs, out):
    ctx = ExitStack()
    sems = {}

    def S(name):
        if name not in sems:
            sems[name] = ctx.enter_context(nc.semaphore(name))
        return sems[name]

    def sb(name, shape):
        return ctx.enter_context(nc.sbuf_tensor(name, shape, F32))

    with ctx:
        ring = sb("ring", [P, RING, 2, KT, P])
        cst = sb("cst", [P, CONST_W])
        vec = sb("vec", [P, VEC_W])
        res = sb("res", [P, KT, CTX])
        act_in = sb("act_in", [P, KT, CTX])
        proj = sb("proj", [P, 25, CTX])
        yT = sb("yT", [P, KT, SEQ])
        hid = sb("hid", [P, FT, SEQ])
        nrm = sb("nrm", [P, 2, CTX])
        sig = sb("sig", [P, 2, SEQ])
        sig2 = sb("sig2", [P, 2, SEQ])
        vtok = sb("vtok", [P, 3, 12, HD])
        ps = ctx.enter_context(nc.psum_tensor("ps", [P, 8, 512], F32))

        def C(name, parts=P):
            at, w = CONST_AT[name]
            return cst[0:parts, at:at + w]

        def V(name, j=0, n=1):
            at, _ = VEC_AT[name]
            return vec[:, at + j:at + j + n]

        landed = [S(f"weights_landed_{r}") for r in range(RING)]

        class Steps:

            def __init__(self, eng, name):
                self.eng, self.sem, self.n = eng, S(name), 0

            def __call__(self, ins):
                self.n += 1
                ins.then_inc(self.sem, 1)
                self.eng.wait_ge(self.sem, self.n)

        def signal(eng, ins, name, n=1):
            ins.then_inc(S(name), 1)
            eng.wait_ge(S(name), n)

        sq = hid[:, :, :].rearrange("p a b -> p (a b)")[:, 0:KT * CTX].rearrange("p (k t) -> p k t", k=KT)
        flat = hid[:, :, :].rearrange("p a b -> p (a b)")
        sb_nl = flat[:, 0:1152].rearrange("p (h c) -> p h c", h=3)
        sb_nlm = flat[0:META, 1152:1920].rearrange("p (h c) -> p h c", h=3)
        pT = flat[:, 1920:3072].rearrange("p (h c) -> p h c", h=3)
        pTm = flat[0:META, 3072:3840].rearrange("p (h c) -> p h c", h=3)
        s_row = flat[:, 3840:3840 + 1248].rearrange("p (h c) -> p h c", h=3)
        mx = flat[:, 5100:5106].rearrange("p (t h) -> p t h", t=2)
        den = flat[:, 5106:5112].rearrange("p (t h) -> p t h", t=2)
        rden = flat[:, 5112:5118].rearrange("p (t h) -> p t h", t=2)
        heads_out = act_in[:, :, :].rearrange("p a b -> p (a b)")[:, 0:6 * SEQ].rearrange("p (t q) -> p t q", t=6)
        arena = sb("arena", [P, 12288])

        def carve(at, *shape, parts=P):
            n = int(np.prod(shape))
            names = " ".join("abcd"[:len(shape)])
            return arena[0:parts, at:at + n].rearrange(f"p ({names}) -> p {names}",
                                                       **dict(zip("abcd", shape))), at + n

        negc, at = carve(0, 1, CTX, parts=8)
        negc = negc[:, 0, :]
        fl_t, at = carve(at, 2, CTX, parts=8)
        pool_s, at = carve(at, 2, 2, CTX)
        hsq, at = carve(at, 3, SEQ)
        hr, at = carve(at, 3, SEQ)
        ar, at = carve(0, 2, PAIRS, 2, P)
        ar = arena[:, 0:2048].rearrange("p (m j x c) -> p m j x c", m=2, j=PAIRS, x=2)
        bf, at = carve(2048, 2, PAIRS, P)
        kf, at = carve(at, 2, PAIRS, P)
        wt, at = carve(at, 2, PAIRS, 4 * P)
        xi, at = carve(at, 2, PAIRS, P)
        xt, at = carve(at, 2, PAIRS, P)
        pb, at = carve(at, 2, PAIRS, P)
        nl, at = carve(at, 2, PAIRS, P)
        def feat(t, at):
            return t[:, at:at + PAIRS * SEQ].rearrange("p (j t) -> p j t", j=PAIRS)
        act_flat = act_in[:, :, :].rearrange("p a b -> p (a b)")
        vtok_flat = vtok[:, :, :, :].rearrange("p a b c -> p (a b c)")
        sigw, lsum, avec, kkn, scr = (feat(flat, 1024 * n) for n in range(5))
        sdg, lora_w = flat[:, 5120:5376], flat[0:HD, 5376:5632]
        p_inc, p_inv = feat(act_flat, 0), feat(act_flat, 1024)
        p_exc = yT[:, 4:8, :]
        reset = yT[:, 0:4, :]
        y_all = vtok_flat[:, 0:1024].rearrange("p (n v) -> p n v", n=PACKS)
        v_st = vtok_flat[:, 1024:2048].rearrange("p (n v) -> p n v", n=PACKS)
        state = sb("state", [P, PAIRS, HD])
        rhs_sa = sb("rhs_sa", [P, 2, PAIRS, HD])
        small = sb("small", [P, 8, 16])
        s_nsa, at = carve(0, 4, P + SEQ)
        pt_nsa, at = carve(at, 4, P + SEQ)
        vt_nsa, at = carve(at, 2, 2, P)
        blk, at = carve(at, 2, CMP_PAIRS, 32)
        hid_c, at = carve(at, 2, CMP_HIDDEN, parts=32)
        gel, at = carve(at, 2, CMP_HIDDEN, parts=32)
        hid_t, at = carve(at, 2, 2, 32)
        kcmp, at = carve(at, 1, 32)
        vcmp, at = carve(at, 1, P, parts=CMP_PAD)
        vown, at = carve(at, GQA, P)
        s_cmp, at = carve(at, 2, NQH, CMP_PAD)
        pt_cmp, at = carve(at, 2, P)
        gates, at = carve(at, 2, 24)
        gl_t, at = carve(at, 1, SEQ, parts=24)
        coef, at = carve(at, 2, 3, NQH)
        vown_src, at = carve(at, 1, P)
        vown_src = vown_src[:, 0]
        mx_n, at = carve(at, 2, 4)
        den_n, at = carve(at, 2, 4)
        mx_c, at = carve(at, 2, NQH)
        den_c, at = carve(at, 2, NQH)

        block = ctx.enter_context(nc.Block())

        @block.sync
        def _(sp):
            sp.dma_start(cst[:], consts).then_inc(S("consts_landed"), 16)
            sp.dma_start(vec[:], vecs).then_inc(S("vecs_landed"), 16)

            def load(b, used=None, n=0):
                if used is not None:
                    sp.wait_ge(S(used), n)
                sp.dma_start(ring[:, b % RING].rearrange("p a k c -> p (a k c)"), weights[b])\
                    .then_inc(landed[b % RING], 16)

            def load_ffn(layer, b_up, before):
                b_down = b_up + FT
                for j in range(RING):
                    load(b_up + j, *before[j])
                for j in range(RING, RING + 2):
                    load(b_up + j, "up_ready", (layer - 1) * FT + j - RING + 1)
                with sp.Fori(0, (FT - RING - 2) // RING) as i:
                    for u in range(RING):
                        j0 = RING + 2 + u
                        sp.wait_ge(S("up_ready"), (layer - 1) * FT + i * RING + (j0 - RING + 1))
                        sp.dma_start(ring[:, (b_up + j0) % RING].rearrange("p a k c -> p (a k c)"),
                                     weights[bass.ds(i * RING + (b_up + j0), 1)].rearrange("o p c -> (o p) c"))\
                            .then_inc(landed[(b_up + j0) % RING], 16)
                for j in range(FT // 2):
                    if j < RING:
                        load(b_down + j, "up_ready", (layer - 1) * FT + FT - RING + j + 1)
                    else:
                        load(b_down + j, "down_used", (layer - 1) * (FT // 2 - 1) + j - RING + 1)

            for b in range(B_IN1, B_OUT1):
                if b < RING:
                    load(b)
                else:
                    load(b, "proj1_ready", 2 * (b - RING + 1))
            for b in range(B_OUT1, B_UP1):
                load(b, "proj1_ready", min(2 * (b - RING + 1), TILES1))
            load_ffn(1, B_UP1, [("out_ready", 2 * (j + 1)) for j in range(RING)])
            last = FT // 2 - 1
            for b in range(B_IN2, B_OUT2):
                n = b - B_IN2
                if n < RING:
                    j = FT // 2 - RING + n
                    load(b, *(("down_used", j + 1) if j < last else ("down_ready", KT)))
                elif b < B_CMP + RING:
                    load(b, "proj2_ready", min(2 * (n - RING + 1), TILES2))
            for b in range(B_OUT2, B_UP2):
                load(b, "cmp_hidden", 1 if b < B_OUT2 + 2 else 2)
            load_ffn(2, B_UP2, [("out_ready", KT + 2 * (j + 1)) for j in range(RING)])

        @block.gpsimd
        def _(pool):
            pool.dma_start(res[:].rearrange("p k t -> p (k t)"), xT).then_inc(S("x_landed"), 16)
            pool.wait_ge(S("normed"), normed("norm4", KT - 1))
            signal(pool, pool.memset(arena[:, 0:4096], 0.0), "packs_zeroed")
            signal(pool, pool.memset(state[:], 0.0), "state_zeroed")
            pool.memset(reset, 1.0).then_inc(S("reset_ones"), 1)
            pool.wait_ge(S("reset_ones"), 1)
            signal(pool, pool.memset(reset.rearrange("p j (c t) -> p j c t", c=CHUNKS)[:, :, :, 0:1], 0.0),
                   "reset_ready")
            for cp in range(0, CHUNKS, 2):
                for level in range(1, LEVELS):
                    for m in range(2):
                        c = cp + m
                        if level == 1:
                            pool.wait_ge(S("products_masked"), c + 1)
                        if level > 1:
                            pool.wait_ge(S(f"join_products_{m}"), (cp // 2) * (LEVELS - 1) + level - 1)
                        elif cp > 0:
                            pool.wait_ge(S("chunk_done"), c - 1)
                        pool.tensor_tensor(nl[:, m], wt[:, m, :, 0:P],
                                           C("join")[:, level * P:(level + 1) * P].unsqueeze(1)
                                           .to_broadcast([P, PAIRS, P]), ALU.mult)\
                            .then_inc(S(f"joins_{m}"), 1)
            pool.wait_ge(S("final_ready"), KT)
            pool.dma_start(out, yT[:].rearrange("p k t -> p (k t)")).then_inc(S("stored"), 16)
            pool.wait_ge(S("stored"), 16)

        @block.tensor
        def _(pe):
            def tile_products(dst, b, half, rhs, n, first=None):
                for k in range(KT):
                    if first is not None:
                        pe.wait_ge(S("normed"), normed(first, k))
                    mm = pe.matmul(dst, ring[:, b % RING, half, k, :], rhs[:, k, 0:n],
                                   start=(k == 0), stop=(k == KT - 1))
                return mm

            def have(b):
                pe.wait_ge(landed[b % RING], 16 * (b // RING + 1))

            def sum_squares(name, tokens):
                pe.wait_ge(S("norm_squares"), nth(name))
                for k in range(KT):
                    mm = pe.matmul(ps[:, 7, 0:tokens], C("ones"), sq[:, k, 0:tokens],
                                   start=(k == 0), stop=(k == KT - 1))
                mm.then_inc(S("norm_sums"), 1)

            def feed_forward(layer, b_up):
                b_down = b_up + FT

                def up(j, i=None):
                    b = b_up + j
                    step = 0 if i is None else i * RING
                    pe.wait_ge(landed[b % RING], 16 * ((0 if i is None else i) + (b // RING + 1)))
                    if j >= 2 or i is not None:
                        pe.wait_ge(S("hid_ready"), (layer - 1) * FT + step + (j - 1))
                    first = f"norm_ff{layer}" if j == 0 else None
                    tile_products(ps[:, 2 * (j % 2), 0:SEQ], b, 0, act_in, SEQ, first)
                    tile_products(ps[:, 2 * (j % 2) + 1, 0:SEQ], b, 1, act_in, SEQ)\
                        .then_inc(S("up_ready"), 1)

                up(0)
                up(1)
                with pe.Fori(0, (FT - 2) // RING) as i:
                    for u in range(RING):
                        up(2 + u, i)

                def down(j, i=None):
                    b = b_down + j
                    pe.wait_ge(landed[b % RING], 16 * ((0 if i is None else i) + (b // RING + 1)))
                    pe.wait_ge(S("hid_ready"), (layer - 1) * FT + (0 if i is None else i * (2 * RING)) + (2 * j + 2))
                    last = i is None and j == FT // 2 - 1
                    for f in range(KT):
                        for half in range(2):
                            if i is None:
                                rhs = hid[:, 2 * j + half, :]
                            else:
                                rhs = hid[:, bass.ds(i * (2 * RING) + (2 * j + half), 1), :]\
                                    .rearrange("p o t -> p (o t)")
                            mm = pe.matmul(ps[:, 4 + f // 2, (f % 2) * SEQ:(f % 2 + 1) * SEQ],
                                           ring[:, b % RING, half, f, :], rhs,
                                           start=(i is None and j == 0 and half == 0 and f % 2 == 0),
                                           stop=(last and half == 1), skip_group_check=True)
                        if last:
                            mm.then_inc(S("down_ready"), 1)
                    if not last:
                        mm.then_inc(S("down_used"), 1)

                down(0)
                with pe.Fori(0, (FT // 2 - 3) // RING) as i:
                    for u in range(RING):
                        down(1 + u, i)
                down(FT // 2 - 2)
                down(FT // 2 - 1)

            pe.wait_ge(S("consts_landed"), 16)
            sum_squares("norm1", CTX)
            for t in range(TILES1):
                if t % 2 == 0:
                    have(B_IN1 + t // 2)
                if t >= 2:
                    pe.wait_ge(S("proj1_copied_" + "ab"[t % 2]), (t - 2) // 2 + 1)
                tile_products(ps[:, t % 2, 0:CTX], B_IN1 + t // 2, t % 2, act_in, CTX,
                              "norm1" if t == 0 else None).then_inc(S("proj1_ready"), 1)

            pe.wait_ge(S("proj1_copied_a"), 11)
            pe.wait_ge(S("proj1_copied_b"), 10)
            for kt, (t0, nt) in enumerate(((META, P), (META + P, P), (0, META))):
                for f in range(6):
                    mm = pe.transpose(ps[0:nt, 2 * kt + f // 4, (f % 4) * P:(f % 4 + 1) * P],
                                      proj[:, VS0 + f, t0:t0 + nt], C("ident"))
                mm.then_inc(S("v1_turned"), 1)

            def meta_dst(j):
                return ps[0:META, 3 + j % 2, (j // 2) * SEQ:(j // 2 + 1) * SEQ]

            def half_of(h):
                return slice(HD * (h % 2), HD * (h % 2) + HD)

            def weighted_values(src, srcm, g, v0, ready, done):
                pe.wait_ge(S(ready), g + 1)
                for j in range(3):
                    h = 3 * g + j
                    dst = ps[half_of(h), 5 + h // 2 - (3 * g) // 2, 0:SEQ]
                    vh = v0 + h
                    pe.matmul(dst, vtok[:, 0, vh, :], src[:, j, 0:SEQ], start=True, stop=False)
                    pe.matmul(dst, vtok[0:META, 2, vh, :], srcm[:, META_SLOT[j], :], start=False, stop=False)
                    mm = pe.matmul(dst[:, P:SEQ], vtok[:, 1, vh, :], src[:, j, SEQ:SEQ + P],
                                   start=False, stop=True)
                mm.then_inc(S(done), 1)

            pe.wait_ge(S("v1_copied"), 3)
            for g in range(2):
                if g == 1:
                    pe.wait_ge(S("sb_weights"), 1)
                for j in range(3):
                    h = 3 * g + j
                    hs = half_of(h)
                    q = proj[hs, QS0 + h // 2, META:CTX]
                    k = proj[hs, KS0 + h // 2, :]
                    pe.matmul(ps[:, j, 0:SEQ], k[:, META:META + P], q, start=True, stop=True,
                              skip_group_check=True)
                    pe.matmul(ps[:, j, SEQ:SEQ + P], k[:, META + P:CTX], q[:, P:SEQ], start=False, stop=True,
                              skip_group_check=True)
                    mm = pe.matmul(meta_dst(j), k[:, 0:META], q,
                                   start=(j < 2), stop=True, skip_group_check=True)
                mm.then_inc(S("sb_logits"), 1)
                pe.wait_ge(S("sb_logs"), g + 1)
                for j in range(3):
                    a_all = ps[:, j, 0:SEQ]
                    b_all = ps[:, j, SEQ:SEQ + P]
                    m_all = meta_dst(j)
                    nl_a, nl_b, nl_m = sb_nl[:, j, 0:SEQ], sb_nl[:, j, SEQ:SEQ + P], sb_nlm[:, META_SLOT[j], :]
                    kw = dict(start=False, stop=True, skip_group_check=True)
                    pe.matmul(a_all, C("neg_from"), nl_a, **kw)
                    pe.matmul(a_all[:, P:SEQ], C("neg_ones"), nl_b, **kw)
                    pe.matmul(a_all[:, 0:P], C("ident"), C("strict_add"), **kw)
                    pe.matmul(b_all, C("neg_from"), nl_b, **kw)
                    pe.matmul(b_all, C("ident"), C("strict_add"), **kw)
                    pe.matmul(m_all, C("neg_from")[0:META, 0:META], nl_m, **kw)
                    pe.matmul(m_all, C("neg_ones")[:, 0:META], nl_a, **kw)
                    mm = pe.matmul(m_all[:, P:SEQ], C("neg_ones")[:, 0:META], nl_b, **kw)
                mm.then_inc(S("sb_sums"), 1)
                if g == 1:
                    pe.wait_ge(S("sb_out_copied"), 1)
                weighted_values(pT, pTm, g, 0, "sb_weights", "sb_out")

            pe.wait_ge(S("sb_out_copied"), 2)
            pe.wait_ge(S("decay_sums"), 1)
            for g in range(2):
                if g == 1:
                    pe.wait_ge(S("fox_out_copied"), 1)
                for j in range(3):
                    h = 3 * g + j
                    hs = half_of(h)
                    q = proj[hs, QF0 + h // 2, META:CTX]
                    k = proj[hs, KF0 + h // 2, :]
                    for t, (c0, nk) in enumerate(((0, META + P), (META + P, CTX))):
                        pe.matmul(ps[:, 5 + j, c0:c0 + nk], q[:, t * P:(t + 1) * P], k[:, 0:nk],
                                  start=True, stop=False, skip_group_check=True)
                        mm = pe.matmul(ps[:, 5 + j, c0:c0 + nk],
                                       C("pick_head")[0:HEADS1, h * P:(h + 1) * P], negc[0:HEADS1, 0:nk],
                                       start=False, stop=True, skip_group_check=True)
                mm.then_inc(S("fox_scores"), 1)
                pe.wait_ge(S("fox_probs"), g + 1)
                if g == 1:
                    pe.wait_ge(S("fox_weights"), 1)
                for j in range(3):
                    row = s_row[:, j, :]
                    pe.transpose(ps[:, j, 0:P], row[:, META:META + P], C("ident"))
                    pe.transpose(ps[:, j, P:SEQ], row[:, P + 2 * META:2 * P + 2 * META], C("ident"))
                    pe.transpose(ps[:, j, SEQ:SEQ + P], row[:, 2 * P + 2 * META:3 * P + 2 * META], C("ident"))
                    pe.transpose(meta_dst(j)[:, 0:P], row[:, 0:META], C("ident"))
                    mm = pe.transpose(meta_dst(j)[:, P:SEQ],
                                      row[:, META + P:META + P + META], C("ident"))
                mm.then_inc(S("fox_turned"), 1)
                weighted_values(pT, pTm, g, 6, "fox_weights", "fox_out")

            for n, name in enumerate(("sb", "fox")):
                pe.wait_ge(S(f"{name}_head_squares"), 1)
                pe.matmul(ps[:, 2 * n, 0:512], C("head_ones"), hsq[:, 0:2, :].rearrange("p a b -> p (a b)"),
                          start=True, stop=True)
                pe.matmul(ps[:, 2 * n + 1, 0:SEQ], C("head_ones"), hsq[:, 2, :],
                          start=True, stop=True).then_inc(S(f"{name}_head_sums"), 1)
            pe.wait_ge(S("pool_diff"), 1)
            for t in range(2):
                mm = pe.matmul(ps[:, 4 + t, 0:SEQ], V("pool_w", t * P, P), pool_s[:, 0, t, META:CTX],
                               start=True, stop=True)
            mm.then_inc(S("pool_mixed"), 1)

            def output_product(layer, b0):
                for t in range(KT):
                    if t % 2 == 0:
                        have(b0 + t // 2)
                    if t >= 4:
                        pe.wait_ge(S("out_added"), (layer - 1) * KT + t - 3)
                    tile_products(ps[:, t % 4, 0:SEQ], b0 + t // 2, t % 2, yT, SEQ)\
                        .then_inc(S("out_ready"), 1)

            pe.wait_ge(S("y1_ready"), 1)
            output_product(1, B_OUT1)
            sum_squares("norm_ff1", SEQ)
            feed_forward(1, B_UP1)
            sum_squares("norm3", SEQ)

            sum_squares("norm4", SEQ)
            for t in range(TILES2):
                if t % 2 == 0:
                    have(B_IN2 + t // 2)
                if t >= 2:
                    pe.wait_ge(S("proj2_copied_" + "ab"[t % 2]), (t - 2) // 2 + 1)
                tile_products(ps[:, t % 2, 0:SEQ], B_IN2 + t // 2, t % 2, act_in, SEQ,
                              "norm4" if t == 0 else None).then_inc(S("proj2_ready"), 1)

            pe.wait_ge(S("lora_w_ready"), 1)
            for f in range(PAIRS):
                pe.matmul(ps[:, f // 2, (f % 2) * SEQ:(f % 2 + 1) * SEQ], V("w2a2", f * P, P)[0:HD], lora_w,
                          start=True, stop=True)
            for f in range(PAIRS):
                mm = pe.matmul(ps[:, 2 + f // 2, (f % 2) * SEQ:(f % 2 + 1) * SEQ], V("w2a2", f * P, P)[HD:P],
                               proj[HD:P, WA0, 1:1 + SEQ], start=True, stop=True)
            mm.then_inc(S("lora_ready"), 1)
            pe.wait_ge(S("key_squares"), 1)
            for f in range(2):
                mm = pe.matmul(ps[:, 4 + f, :], C("head_ones"),
                               scr[:, 2 * f:2 * f + 2, :].rearrange("p a b -> p (a b)"), start=True, stop=True)
            mm.then_inc(S("key_sums"), 1)

            def tok(c):
                return slice(CHUNK * c, CHUNK * (c + 1))

            def halves():
                return ((h, slice(HD * h, HD * (h + 1))) for h in range(2))

            for c in range(CHUNKS):
                for j in range(PAIRS):
                    n = c * PAIRS + j
                    for h, hs in halves():
                        mm = pe.matmul(ps[hs, 6 + n // 8, (n % 8) * HD:(n % 8 + 1) * HD],
                                       proj[hs, V0 + j, 1 + CHUNK * c:1 + CHUNK * (c + 1)], C("ident")[hs, hs],
                                       start=True, stop=True)
            mm.then_inc(S("v_stacked"), 1)
            pe.wait_ge(S("rk_ready"), 1)
            for c in range(CHUNKS):
                for j in range(PAIRS):
                    for h, hs in halves():
                        mm = pe.matmul(ps[hs, 4, c * PAIRS + j:c * PAIRS + j + 1], scr[hs, j, tok(c)],
                                       C("ones")[hs, 0:1], start=True, stop=True)
            mm.then_inc(S("bonus_sums"), 1)

            for cp in range(0, CHUNKS, 2):
                pe.wait_ge(S("v_st_copied"), 1)
                pe.wait_ge(S("bonus_copied"), 1)
                for m in range(2):
                    c = cp + m
                    pe.wait_ge(S("packs_ready"), c + 1)
                    if c > 0:
                        pe.wait_ge(S("products_masked"), c)
                    if cp > 0:
                        pe.wait_ge(S("chunk_done"), c - 1)
                    for j in range(PAIRS):
                        both = ar[:, m, j, :, :].rearrange("p x c -> p (x c)")
                        pe.matmul(ps[:, j, 0:2 * P], bf[:, m, j, :], both, start=True, stop=True)
                        pe.matmul(ps[:, j, 2 * P:4 * P], kf[:, m, j, :], both, start=True, stop=True)
                        mm = pe.matmul(ps[:, 4 + m, j * P:(j + 1) * P], ar[:, m, j, 0, :], bf[:, m, j, :],
                                       start=True, stop=True)
                    mm.then_inc(S("products_ready"), 1)
                for level in range(1, LEVELS):
                    n = (cp // 2) * (LEVELS - 1) + level
                    for m in range(2):
                        if level == 1:
                            pe.wait_ge(S("products_masked"), cp + 2)
                        pe.wait_ge(S(f"joins_{m}"), n)
                        pe.wait_ge(S(f"inverse_grown_{m}"), n + cp // 2)
                        for j in range(PAIRS):
                            mm = pe.matmul(ps[:, 3 * m, j * P:(j + 1) * P], nl[:, m, j, :], xi[:, m, j, :],
                                           start=True, stop=True)
                        mm.then_inc(S(f"join_products_{m}"), 1)
                    for m in range(2):
                        pe.wait_ge(S(f"join_copied_{m}"), n)
                        for j in range(PAIRS):
                            if level < LEVELS - 1:
                                pe.matmul(ps[:, 3 * m + 1, j * P:(j + 1) * P], xt[:, m, j, :], pb[:, m, j, :],
                                          start=True, stop=True)
                            mm = pe.matmul(ps[:, 3 * m + 2, j * P:(j + 1) * P], pb[:, m, j, :], xt[:, m, j, :],
                                           start=True, stop=True)
                        mm.then_inc(S(f"inverse_terms_{m}"), 1)
                for m in range(2):
                    pe.wait_ge(S(f"inverse_grown_{m}"), (cp // 2 + 1) * LEVELS)
                    for j in range(PAIRS):
                        pe.transpose(ps[:, 3 * m, j * P:(j + 1) * P], bf[:, m, j, :], C("ident"))
                        mm = pe.transpose(ps[:, 3 * m + 1, j * P:(j + 1) * P], kf[:, m, j, :], C("ident"))
                    mm.then_inc(S("bk_turned"), 1)
                for m in range(2):
                    c = cp + m
                    if c == 0:
                        pe.wait_ge(S("state_zeroed"), 1)
                    else:
                        pe.wait_ge(S("chunk_done"), c)

                    def part(bank, j):
                        return ps[:, bank, j * HD:(j + 1) * HD]

                    kw = dict(stop=True, skip_group_check=True)
                    for j in range(PAIRS):
                        pe.matmul(part(6, j), ar[:, m, j, 0, :], state[:, j, :], start=(j == 0), **kw)
                        mm = pe.matmul(part(6, j), wt[:, m, j, 2 * P:3 * P], v_st[:, c * PAIRS + j, :],
                                       start=False, **kw)
                    mm.then_inc(S("rhs_ready"), 1)
                    pe.wait_ge(S("rhs_copied"), c + 1)
                    for j in range(PAIRS):
                        mm = pe.matmul(part(7, j), xt[:, m, j, :], rhs_sa[:, 0, j, :], start=(j == 0), **kw)
                    mm.then_inc(S("sa_ready"), 1)
                    for j in range(PAIRS):
                        pe.matmul(part(6, j), ar[:, m, j, 1, :], state[:, j, :], start=(j == 0), **kw)
                        pe.matmul(part(6, j), wt[:, m, j, 3 * P:4 * P], v_st[:, c * PAIRS + j, :],
                                  start=False, **kw)
                    pe.wait_ge(S("sa_copied"), c + 1)
                    pe.wait_ge(S("bk_copied"), c + 1)
                    for j in range(PAIRS):
                        pe.matmul(part(7, j), nl[:, m, j, :], v_st[:, c * PAIRS + j, :], start=(j == 0), **kw)
                        mm = pe.matmul(part(7, j), pb[:, m, j, :], rhs_sa[:, 1, j, :], start=False, **kw)
                    mm.then_inc(S("state_terms"), 1)
                    for j in range(PAIRS):
                        mm = pe.matmul(part(6, j), wt[:, m, j, P:2 * P], rhs_sa[:, 1, j, :], start=False, **kw)
                    mm.then_inc(S("y_terms"), 1)

            pe.wait_ge(S("chunk_done"), CHUNKS)
            for c in range(CHUNKS):
                for h, hs in halves():
                    mm = pe.matmul(ps[hs, c // 2, (c % 2) * 256:(c % 2 + 1) * 256], sdg[:, tok(c)],
                                   V("g2", h * 256, 256), start=True, stop=True)
            mm.then_inc(S("gates_ready"), 1)
            pe.wait_ge(S("rwkv_y"), 1)
            for c in range(CHUNKS):
                for j in range(PAIRS):
                    for h, hs in halves():
                        at = (j % 2) * SEQ + CHUNK * c
                        mm = pe.matmul(ps[hs, 2 + j // 2, at:at + CHUNK], y_all[hs, c * PAIRS + j, :],
                                       C("ident")[hs, hs], start=True, stop=True)
            mm.then_inc(S("rwkv_turned"), 1)

            def grp(g):
                return slice(HD * g, HD * (g + 1))

            for x in range(2):
                pe.wait_ge(S("blk_ready"), x + 1)
                for q in range(2):
                    have(B_CMP + 2 * x + q)
                for jp in range(CMP_PAIRS):
                    b, r = B_CMP + 2 * x + jp // 8, jp % 8
                    w1 = ring[:, b % RING, r // 4, 2 * (r % 4):2 * (r % 4) + 2, :].rearrange("p a c -> p (a c)")
                    mm = pe.matmul(ps[0:32, 4 + x, 0:CMP_HIDDEN], blk[:, x, jp, :], w1,
                                   start=(jp == 0), stop=(jp == CMP_PAIRS - 1))
                mm.then_inc(S("cmp_hidden"), 1)
            pe.wait_ge(S("gate_sigmoids"), 1)
            for t in range(2):
                pe.transpose(ps[:, 6, t * 24:(t + 1) * 24], gl_t[:, 0, t * P:(t + 1) * P], C("ident")[0:24, 0:24])
            for br, v in enumerate((VS1, VW1)):
                for t in range(2):
                    mm = pe.transpose(ps[:, 7, (2 * br + t) * P:(2 * br + t + 1) * P],
                                      proj[:, v, 1 + t * P:1 + (t + 1) * P], C("ident"))
            mm.then_inc(S("nsa_turned"), 1)
            pe.wait_ge(S("cmp_gelu"), 1)
            for x in range(2):
                for q in range(2):
                    mm = pe.transpose(ps[:, 0, (2 * x + q) * 32:(2 * x + q + 1) * 32],
                                      hid_c[:, x, q * P:(q + 1) * P], C("ident")[0:32, 0:32])
            mm.then_inc(S("cmp_turned"), 1)
            pe.wait_ge(S("hid_t_copied"), 1)
            for g in range(KVH):
                for q in range(2):
                    pe.matmul(ps[grp(g), 1, 0:CMP_PAD], V("cmp_w2k", q * HD, HD),
                              hid_t[:, 0, q, g * CMP_PAD:(g + 1) * CMP_PAD], start=(q == 0), stop=(q == 1))
            for g in range(KVH):
                for q in range(2):
                    mm = pe.matmul(ps[0:CMP_PAD, 2, g * HD:(g + 1) * HD], hid_t[:, 1, q, g * CMP_PAD:(g + 1) * CMP_PAD],
                                   V("cmp_w2v", q * HD, HD), start=(q == 0), stop=(q == 1))
            mm.then_inc(S("cmp_kv"), 1)
            pe.wait_ge(S("cmp_kv_copied"), 1)
            for g in range(KVH):
                for t in range(2):
                    for a in range(GQA):
                        at = (t * GQA + a) * CMP_PAD
                        pe.matmul(ps[:, 4 + g, at:at + CMP_PAD], proj[grp(g), Q0 + a, 1 + t * P:1 + (t + 1) * P],
                                  kcmp[grp(g), 0, 0:CMP_PAD], start=True, stop=True)
            pe.matmul(ps[:, 3, 0:P], C("cmp_spread")[0:CMP_PAD, :], vcmp[:, 0, :], start=True, stop=True)\
                .then_inc(S("cmp_scores"), 1)
            pe.wait_ge(S("cmp_probs"), 1)
            for t in range(2):
                mm = pe.transpose(ps[:, 6, t * P:(t + 1) * P], s_cmp[:, t].rearrange("p h n -> p (h n)"), C("ident"))
            mm.then_inc(S("cmp_probs_turned"), 1)

            for a in range(GQA):
                if a > 0:
                    pe.wait_ge(S("nsa_weights"), a)
                for br, k in enumerate((KS1, KW1)):
                    for g in range(KVH):
                        q = proj[grp(g), Q0 + a, 1:1 + SEQ]
                        kk = proj[grp(g), k, 1:1 + SEQ]
                        slot = 2 * br + g
                        pe.matmul(ps[:, slot, 0:P], q[:, 0:P], kk[:, 0:P], start=True, stop=True)
                        mm = pe.matmul(ps[:, slot, P:P + SEQ], q[:, P:SEQ], kk, start=True, stop=True)
                mm.then_inc(S("nsa_scores"), 1)
                pe.wait_ge(S("nsa_probs"), a + 1)
                for slot in range(4):
                    pe.transpose(ps[:, slot, 0:P], s_nsa[:, slot, 0:P], C("ident"))
                    pe.transpose(ps[:, slot, P:SEQ], s_nsa[:, slot, P:SEQ], C("ident"))
                    mm = pe.transpose(ps[:, slot, SEQ:SEQ + P], s_nsa[:, slot, SEQ:SEQ + P], C("ident"))
                mm.then_inc(S("nsa_probs_turned"), 1)
                if a == 0:
                    pe.wait_ge(S("pt_cmp_copied"), 1)
                if a >= 2:
                    pe.wait_ge(S("nsa_out_copied"), a - 1)
                dst = ps[:, 4 + a % 2, 0:SEQ]
                pe.matmul(dst, vown[:, a, :], pt_cmp[:].rearrange("p t q -> p (t q)"), start=True, stop=False,
                          skip_group_check=True)
                pe.wait_ge(S("nsa_weights"), a + 1)
                for br in range(2):
                    for g in range(KVH):
                        slot = 2 * br + g
                        w = pt_nsa[:, slot, :]
                        pe.matmul(dst[grp(g)], vt_nsa[:, br, 0, grp(g)], w[:, 0:SEQ], start=False, stop=False,
                                  skip_group_check=True)
                        mm = pe.matmul(dst[grp(g), P:SEQ], vt_nsa[:, br, 1, grp(g)], w[:, SEQ:SEQ + P],
                                       start=False, stop=(br == 1), skip_group_check=True)
                mm.then_inc(S("nsa_out"), 1)

            pe.wait_ge(S("y2_ready"), 1)
            output_product(2, B_OUT2)
            sum_squares("norm_ff2", SEQ)
            feed_forward(2, B_UP2)
            sum_squares("norm6", SEQ)

        @block.scalar
        def _(act):
            step = Steps(act, "scalar_steps")

            def norm_root(name, src_ready, n, src, tokens):
                act.wait_ge(S(src_ready), n)
                signal(act, act.activation(sq[:, :, 0:tokens], src, ACT.Square), "norm_squares", nth(name))
                act.wait_ge(S("norm_sums"), nth(name))
                step(act.activation(nrm[:, 0, 0:tokens], ps[:, 7, 0:tokens], ACT.Ln,
                                    bias=C("eps"), scale=1.0 / D))
                signal(act, act.activation(nrm[:, 1, 0:tokens], nrm[:, 0, 0:tokens], ACT.Exp, scale=-0.5),
                       "norm_root", nth(name))

            act.wait_ge(S("consts_landed"), 16)
            norm_root("norm1", "x_landed", 16, res[:, :, 0:CTX], CTX)

            def scale_of(t):
                return HD ** -0.5 if QS0 <= t < QS0 + 3 or QF0 <= t < QF0 + 3 else 1.0

            for t in range(0, TILES1, 2):
                n = 6 if t == FL0 else P
                act.wait_ge(S("proj1_ready"), t + 1)
                act.activation(proj[0:n, t, :], ps[0:n, t % 2, 0:CTX], ACT.Copy, scale=scale_of(t))\
                    .then_inc(S("proj1_copied_a"), 1)
            act.wait_ge(S("forget_logit"), 1)
            step(act.activation(fl_t[0:6, 1, :], fl_t[0:6, 0, :], ACT.Abs))
            step(act.activation(fl_t[0:6, 1, :], fl_t[0:6, 1, :], ACT.Exp, scale=-1.0))
            signal(act, act.activation(fl_t[0:6, 1, :], fl_t[0:6, 1, :], ACT.Ln, bias=C("one", 6)),
                   "forget_log")

            for g in range(2):
                act.wait_ge(S("sb_logits"), g + 1)
                if g == 1:
                    act.wait_ge(S("sb_sums"), 1)
                zm = ps[0:META, 3:5, :].rearrange("p a b -> p (a b)")[:, 0:3 * SEQ]\
                    .rearrange("p (h q) -> p h q", h=3)
                z = ps[:, 0:3, 0:384]
                act.activation(sb_nl, z, ACT.Abs)
                step(act.activation(sb_nlm, zm, ACT.Abs))
                act.activation(sb_nl, sb_nl, ACT.Exp, scale=-1.0)
                step(act.activation(sb_nlm, sb_nlm, ACT.Exp, scale=-1.0))
                act.activation(sb_nl, sb_nl, ACT.Ln, bias=C("one"))
                signal(act, act.activation(sb_nlm, sb_nlm, ACT.Ln, bias=C("one", META)), "sb_softplus", g + 1)
                act.wait_ge(S("sb_sums"), g + 1)
                if g == 1:
                    act.wait_ge(S("sb_out"), 1)
                act.activation(pT, z, ACT.Exp)
                signal(act, act.activation(pTm, zm, ACT.Exp), "sb_weights", g + 1)

            act.wait_ge(S("sb_out_copied"), 2)
            signal(act, act.activation(hsq[:], heads_out[:, 3:6, :], ACT.Square), "sb_head_squares")

            for g in range(2):
                act.wait_ge(S("fox_max"), g + 1)
                for j in range(3):
                    for t, (c0, nk) in enumerate(((0, META + P), (META + P, CTX))):
                        ins = act.activation(s_row[:, j, c0:c0 + nk], s_row[:, j, c0:c0 + nk], ACT.Exp,
                                             bias=mx[:, t, j:j + 1], accum_out=den[:, t, j:j + 1])
                signal(act, ins, "fox_exps", g + 1)
                act.wait_ge(S("fox_turned"), g + 1)
                if g == 1:
                    act.wait_ge(S("fox_out"), 1)
                zm = ps[0:META, 3:5, :].rearrange("p a b -> p (a b)")[:, 0:3 * SEQ]\
                    .rearrange("p (h q) -> p h q", h=3)
                act.activation(pT, ps[:, 0:3, 0:384], ACT.Copy)
                signal(act, act.activation(pTm, zm, ACT.Copy), "fox_weights", g + 1)

            def head_root(name, n):
                act.wait_ge(S(f"{name}_head_sums"), 1)
                src = ps[:, 2 * n:2 * n + 2, :].rearrange("p a b -> p (a b)")[:, 0:3 * SEQ]
                dst = hr[:].rearrange("p a b -> p (a b)")
                step(act.activation(dst, src, ACT.Ln, bias=C("eps"), scale=1.0 / HD))
                signal(act, act.activation(dst, dst, ACT.Exp, scale=-0.5), f"{name}_head_root")

            head_root("sb", 0)
            act.wait_ge(S("fox_out_copied"), 2)
            signal(act, act.activation(hsq[:], heads_out[:, 0:3, :], ACT.Square), "fox_head_squares")
            act.wait_ge(S("sb_y"), 1)
            head_root("fox", 1)

            def silu_exps(layer):
                def one(j, i=None):
                    at = 0 if i is None else i * RING
                    act.wait_ge(S("up_ready"), (layer - 1) * FT + at + (j + 1))
                    if j >= 2 or i is not None:
                        act.wait_ge(S("hid_ready"), (layer - 1) * FT + at + (j - 1))
                    act.activation(sig[:, j % 2, :], ps[:, 2 * (j % 2), 0:SEQ], ACT.Exp, scale=-1.0)\
                        .then_inc(S("gate_exp"), 1)
                one(0)
                one(1)
                with act.Fori(0, (FT - 2) // RING) as i:
                    for u in range(RING):
                        one(2 + u, i)

            norm_root("norm_ff1", "out_added", KT, res[:, :, META:CTX], SEQ)
            silu_exps(1)
            norm_root("norm3", "down_added", KT, res[:, :, META:CTX], SEQ)

            norm_root("norm4", "norm3_ready", KT, res[:, :, META:CTX], SEQ)
            for t in range(0, TILES2, 2):
                n = 24 if t == GL0 else P
                act.wait_ge(S("proj2_ready"), t + 1)
                act.activation(proj[0:n, t, 1:1 + SEQ], ps[0:n, t % 2, 0:SEQ], ACT.Copy,
                               scale=HD ** -0.5 if Q0 <= t < Q0 + 4 else 1.0).then_inc(S("proj2_copied_a"), 1)

            def one_over_one_plus(dst):
                step(act.activation(dst, dst, ACT.Ln, bias=C("one", dst.shape[0])))
                return act.activation(dst, dst, ACT.Exp, scale=-1.0)

            act.wait_ge(S("shifted"), 1)
            step(act.activation(lora_w, lora_w, ACT.Exp, scale=2.0))
            signal(act, one_over_one_plus(lora_w), "lora_w_exp")
            step(act.activation(sdg, sdg, ACT.Exp, scale=-1.0))
            step(one_over_one_plus(sdg))
            act.wait_ge(S("key_scaled"), 1)
            signal(act, act.activation(scr, kkn, ACT.Square), "key_squares")
            for n, dst in enumerate((sigw, avec)):
                act.wait_ge(S("lora_biased"), n + 1)
                step(act.activation(dst, dst, ACT.Exp, scale=-1.0))
                signal(act, one_over_one_plus(dst), "decay_a_sigmoids", n + 1)
            act.wait_ge(S("key_sums_kept"), 1)
            step(act.activation(scr, scr, ACT.Ln))
            signal(act, act.activation(scr, scr, ACT.Exp, scale=-0.5), "key_root")
            act.wait_ge(S("decay_scanned"), 2)
            act.activation(p_exc, sigw, ACT.Exp, scale=-DECAY)
            act.activation(p_inc, lsum, ACT.Exp, scale=-DECAY)
            signal(act, act.activation(p_inv, lsum, ACT.Exp, scale=DECAY), "decay_powers")

            for cp in range(0, CHUNKS, 2):
                for level in range(1, LEVELS):
                    n = (cp // 2) * (LEVELS - 1) + level
                    for m in range(2):
                        if level == 1 and cp > 0:
                            act.wait_ge(S("chunk_done"), cp)
                        act.wait_ge(S(f"join_products_{m}"), n)
                        if level > 1:
                            act.wait_ge(S(f"inverse_terms_{m}"), n - 1)
                        act.activation(pb[:, m].rearrange("p j c -> p (j c)"), ps[:, 3 * m, :], ACT.Copy)\
                            .then_inc(S(f"join_copied_{m}"), 1)
                for m in range(2):
                    act.wait_ge(S("bk_turned"), cp + m + 1)
                    act.activation(pb[:, m].rearrange("p j c -> p (j c)"), ps[:, 3 * m, :], ACT.Copy)
                    signal(act, act.activation(nl[:, m].rearrange("p j c -> p (j c)"), ps[:, 3 * m + 1, :],
                                               ACT.Copy), "bk_copied", cp + m + 1)
                for m in range(2):
                    c = cp + m
                    act.wait_ge(S("rhs_ready"), c + 1)
                    signal(act, act.activation(rhs_sa[:, 0].rearrange("p j c -> p (j c)"), ps[:, 6, 0:256],
                                               ACT.Copy), "rhs_copied", c + 1)
                    act.wait_ge(S("sa_ready"), c + 1)
                    if c > 0:
                        act.wait_ge(S("y_terms"), c)
                    signal(act, act.activation(rhs_sa[:, 1].rearrange("p j c -> p (j c)"), ps[:, 7, 0:256],
                                               ACT.Copy), "sa_copied", c + 1)
            act.wait_ge(S("y_centred"), 1)
            signal(act, act.activation(scr.rearrange("p j t -> p (j t)"), y_all.rearrange("p n v -> p (n v)"),
                                       ACT.Square), "y_squares")
            act.wait_ge(S("y_vars"), 1)
            step(act.activation(small[:, 2], small[:, 2], ACT.Ln, bias=C("gn_eps"), scale=1.0 / HD))
            signal(act, act.activation(small[:, 2], small[:, 2], ACT.Exp, scale=-0.5), "y_root")
            act.wait_ge(S("rwkv_turned"), 1)
            signal(act, act.activation(yT[:, 0:4, :].rearrange("p j t -> p (j t)"),
                                       ps[:, 2:4, :].rearrange("p a b -> p (a b)"), ACT.Copy), "rwkv_out")

            act.wait_ge(S("blk_zeroed"), 1)
            for x, src in enumerate((KC0, VC0)):
                for g in range(KVH):
                    for q in range(2):
                        full = proj[HD * g:HD * (g + 1), src, 1 + q:1 + q + 255]
                        view = bass.AP(full.tensor, full.offset, [full.ap[0], [2, CMP_PAIRS], [CMP_STRIDE, N_CMP]])
                        ins = act.activation(blk[HD * q:HD * (q + 1), x, :, g * CMP_PAD:g * CMP_PAD + N_CMP],
                                             view, ACT.Copy)
                signal(act, ins, "blk_gathered", x + 1)
            step(act.activation(gl_t[:, 0], proj[0:24, GL0, 1:1 + SEQ], ACT.Exp, scale=-1.0))
            signal(act, one_over_one_plus(gl_t[:, 0]), "gate_sigmoids")
            act.wait_ge(S("cmp_gelu_arg"), 1)
            step(act.activation(gel[:], gel[:], ACT.Exp, scale=-GELU))
            signal(act, one_over_one_plus(gel[:]), "cmp_gelu_sigmoid")
            act.wait_ge(S("nsa_turned"), 1)
            act.activation(gates[:].rearrange("p t n -> p (t n)"), ps[:, 6, 0:48], ACT.Copy)
            signal(act, act.activation(vt_nsa[:].rearrange("p b t c -> p (b t c)"), ps[:, 7, :], ACT.Copy),
                   "nsa_values")
            act.wait_ge(S("cmp_turned"), 1)
            signal(act, act.activation(hid_t[:].rearrange("p a b c -> p (a b c)"), ps[:, 0, 0:128], ACT.Copy),
                   "hid_t_copied")
            act.wait_ge(S("cmp_kv"), 1)
            act.activation(kcmp[:, 0, 0:CMP_PAD], ps[:, 1, 0:CMP_PAD], ACT.Copy)
            signal(act, act.activation(vcmp[:, 0], ps[0:CMP_PAD, 2, 0:P], ACT.Copy), "cmp_kv_copied")
            act.wait_ge(S("cmp_centred"), 1)
            signal(act, act.activation(s_cmp[:], s_cmp[:], ACT.Exp), "cmp_exps")
            act.wait_ge(S("cmp_probs_turned"), 1)
            signal(act, act.activation(pt_cmp[:].rearrange("p t q -> p (t q)"), ps[:, 6, 0:SEQ], ACT.Copy),
                   "pt_cmp_copied")
            for a in range(GQA):
                act.wait_ge(S("nsa_max"), a + 1)
                for slot in range(4):
                    for t, (c0, n) in enumerate(((0, P), (P, SEQ))):
                        ins = act.activation(s_nsa[:, slot, c0:c0 + n], s_nsa[:, slot, c0:c0 + n], ACT.Exp,
                                             bias=mx_n[:, t, slot:slot + 1], accum_out=den_n[:, t, slot:slot + 1])
                signal(act, ins, "nsa_exps", a + 1)
                act.wait_ge(S("nsa_probs_turned"), a + 1)
                if a > 0:
                    act.wait_ge(S("nsa_out"), a)
                signal(act, act.activation(pt_nsa[:], ps[:, 0:4, 0:P + SEQ], ACT.Copy), "nsa_weights", a + 1)

            norm_root("norm_ff2", "out_added", 2 * KT, res[:, :, META:CTX], SEQ)
            silu_exps(2)
            norm_root("norm6", "down_added", 2 * KT, res[:, :, META:CTX], SEQ)

        @block.vector
        def _(dve):
            step = Steps(dve, "vector_steps")

            def normalise(name, gain, t0, tokens, dst=None):
                dst = act_in if dst is None else dst
                dve.wait_ge(S("norm_root"), nth(name))
                for k in range(KT):
                    dve.scalar_tensor_tensor(dst[:, k, 0:tokens], res[:, k, t0:t0 + tokens],
                                             V(gain, k), nrm[:, 1, 0:tokens], ALU.mult, ALU.mult)\
                        .then_inc(S("normed"), 1)

            dve.wait_ge(S("vecs_landed"), 16)
            normalise("norm1", "norm1", 0, CTX)

            for t in range(1, TILES1, 2):
                dve.wait_ge(S("proj1_ready"), t + 1)
                scale = HD ** -0.5 if QS0 <= t < QS0 + 3 or QF0 <= t < QF0 + 3 else 1.0
                dve.tensor_scalar(proj[:, t, :], ps[:, t % 2, 0:CTX], scale, None, ALU.mult)\
                    .then_inc(S("proj1_copied_b"), 1)
            for kt, nt in enumerate((P, P, META)):
                dve.wait_ge(S("v1_turned"), kt + 1)
                src = ps[0:nt, 2 * kt:2 * kt + 2, :].rearrange("p a b -> p (a b)")[:, 0:12 * HD]
                dve.tensor_copy(vtok[0:nt, kt].rearrange("p h d -> p (h d)"), src).then_inc(S("v1_copied"), 1)

            dve.wait_ge(S("proj1_copied_a"), 11)
            signal(dve, dve.tensor_scalar(fl_t[0:6, 0, :], proj[0:6, FL0, :], V("forget_bias")[0:6], None, ALU.add),
                   "forget_logit")
            dve.wait_ge(S("forget_log"), 1)
            step(dve.scalar_tensor_tensor(fl_t[0:6, 0, :], fl_t[0:6, 0, :], 0.0, fl_t[0:6, 1, :],
                                          ALU.min, ALU.subtract))
            step(dve.memset(fl_t[0:6, 1, :], 1.0))
            signal(dve, dve.tensor_tensor_scan(negc[0:6, :], fl_t[0:6, 1, :], fl_t[0:6, 0, :], 0.0,
                                               ALU.mult, ALU.subtract), "decay_sums")

            dve.wait_ge(S("proj1_copied_b"), 10)
            u = proj[:, U0:U0 + 2, :]
            lo, hi = slice(0, HD), slice(HD, P)
            a, b = pool_s[:, 0], pool_s[:, 1]
            step(dve.tensor_tensor(a[:, :, 1:CTX], u[:, :, 1:CTX], u[:, :, 0:CTX - 1], ALU.add))
            step(dve.tensor_tensor(b[:, :, 3:CTX], a[:, :, 3:CTX], a[:, :, 1:CTX - 2], ALU.add))
            step(dve.scalar_tensor_tensor(a[lo, 0, META:CTX], a[lo, 0, META:CTX], 1 / 2, u[lo, 0, META:CTX],
                                          ALU.mult, ALU.subtract))
            step(dve.scalar_tensor_tensor(a[hi, 0, META:CTX], b[hi, 0, META:CTX], 1 / 4, u[hi, 0, META:CTX],
                                          ALU.mult, ALU.subtract))
            step(dve.tensor_tensor(a[:, 1, 7:CTX], b[:, 1, 7:CTX], b[:, 1, 3:CTX - 4], ALU.add))
            step(dve.tensor_tensor(b[:, 1, 15:CTX], a[:, 1, 15:CTX], a[:, 1, 7:CTX - 8], ALU.add))
            step(dve.scalar_tensor_tensor(a[lo, 1, META:CTX], a[lo, 1, META:CTX], 1 / 8, u[lo, 1, META:CTX],
                                          ALU.mult, ALU.subtract))
            signal(dve, dve.scalar_tensor_tensor(a[hi, 1, META:CTX], b[hi, 1, META:CTX], 1 / 16,
                                                 u[hi, 1, META:CTX], ALU.mult, ALU.subtract), "pool_diff")

            def copy_heads(g, t0, done):
                if g == 0:
                    dve.tensor_copy(heads_out[:, t0, :], ps[:, 5, 0:SEQ])
                    ins = dve.tensor_copy(heads_out[0:HD, t0 + 1, :], ps[0:HD, 6, 0:SEQ])
                else:
                    dve.tensor_copy(heads_out[HD:P, t0 + 1, :], ps[HD:P, 5, 0:SEQ])
                    ins = dve.tensor_copy(heads_out[:, t0 + 2, :], ps[:, 6, 0:SEQ])
                signal(dve, ins, done, g + 1)

            strict = C("strict").unsqueeze(1).to_broadcast([P, 3, P])
            for g in range(2):
                dve.wait_ge(S("sb_softplus"), g + 1)
                zm = ps[0:META, 3:5, :].rearrange("p a b -> p (a b)")[:, 0:3 * SEQ]\
                    .rearrange("p (h q) -> p h q", h=3)
                step(dve.scalar_tensor_tensor(sb_nl, ps[:, 0:3, 0:384], 0.0, sb_nl, ALU.max, ALU.add))
                dve.tensor_tensor(sb_nl[:, :, 0:P], sb_nl[:, :, 0:P], strict, ALU.mult)
                dve.tensor_tensor(sb_nl[:, :, SEQ:SEQ + P], sb_nl[:, :, SEQ:SEQ + P], strict, ALU.mult)
                signal(dve, dve.scalar_tensor_tensor(sb_nlm, zm, 0.0, sb_nlm, ALU.max, ALU.add),
                       "sb_logs", g + 1)
                dve.wait_ge(S("sb_out"), g + 1)
                copy_heads(g, 3, "sb_out_copied")

            causal = C("causal1").unsqueeze(1).to_broadcast([P, 3, META + P + CTX])
            for g in range(2):
                dve.wait_ge(S("fox_scores"), g + 1)
                step(dve.tensor_tensor(s_row, ps[:, 5:8, 0:META + P + CTX], causal, ALU.add))
                dve.tensor_reduce(mx[:, 0, :], s_row[:, :, 0:META + P], AX.X, ALU.max, negate=True)
                signal(dve, dve.tensor_reduce(mx[:, 1, :], s_row[:, :, META + P:META + P + CTX], AX.X, ALU.max,
                                              negate=True), "fox_max", g + 1)
                dve.wait_ge(S("fox_exps"), g + 1)
                step(dve.reciprocal(rden, den))
                for j in range(3):
                    for t, (c0, nk) in enumerate(((0, META + P), (META + P, CTX))):
                        ins = dve.tensor_scalar(s_row[:, j, c0:c0 + nk], s_row[:, j, c0:c0 + nk],
                                                rden[:, t, j:j + 1], None, ALU.mult)
                signal(dve, ins, "fox_probs", g + 1)
                dve.wait_ge(S("fox_out"), g + 1)
                copy_heads(g, 0, "fox_out_copied")

            for name, t0, y0, gain in (("sb", 3, 5, "sb_gain"), ("fox", 0, 2, "fox_gain")):
                dve.wait_ge(S(f"{name}_head_root"), 1)
                for t in range(3):
                    ins = dve.scalar_tensor_tensor(yT[:, y0 + t, :], heads_out[:, t0 + t, :], V(gain, t),
                                                   hr[:, t, :], ALU.mult, ALU.mult)
                signal(dve, ins, f"{name}_y")
            dve.wait_ge(S("pool_mixed"), 1)
            for t in range(2):
                ins = dve.tensor_scalar(yT[:, t, :], ps[:, 4 + t, 0:SEQ], V("pool_scale", t), None, ALU.mult)
            signal(dve, ins, "y1_ready")

            def add_output(layer):
                for t in range(KT):
                    dve.wait_ge(S("out_ready"), (layer - 1) * KT + t + 1)
                    dve.tensor_tensor(res[:, t, META:CTX], ps[:, t % 4, 0:SEQ], res[:, t, META:CTX], ALU.add)\
                        .then_inc(S("out_added"), 1)

            def silu(layer):
                def one(j, i=None):
                    at = 0 if i is None else i * RING
                    own, first = S("silu_steps"), (layer - 1) * 3 * FT
                    m = j % 2
                    dve.wait_ge(S("gate_exp"), (layer - 1) * FT + at + (j + 1))
                    dve.tensor_scalar(sig2[:, m, :], sig[:, m, :], 1.0, None, ALU.add).then_inc(own, 1)
                    dve.wait_ge(own, at * 3 + (first + 3 * j + 1))
                    dve.reciprocal(sig2[:, m, :], sig2[:, m, :]).then_inc(own, 1)
                    dve.wait_ge(own, at * 3 + (first + 3 * j + 2))
                    dve.tensor_tensor(sig2[:, m, :], ps[:, 2 * m, 0:SEQ], sig2[:, m, :], ALU.mult).then_inc(own, 1)
                    dve.wait_ge(own, at * 3 + (first + 3 * j + 3))
                    if i is None:
                        dst = hid[:, j, :]
                    else:
                        dst = hid[:, bass.ds(i * RING + j, 1), :].rearrange("p o t -> p (o t)")
                    dve.tensor_tensor(dst, ps[:, 2 * m + 1, 0:SEQ], sig2[:, m, :], ALU.mult)\
                        .then_inc(S("hid_ready"), 1)
                    dve.wait_ge(S("hid_ready"), (layer - 1) * FT + at + (j + 1))
                one(0)
                one(1)
                with dve.Fori(0, (FT - 2) // RING) as i:
                    for u in range(RING):
                        one(2 + u, i)

            def add_down(layer):
                dve.wait_ge(S("down_ready"), (layer - 1) * KT + KT)
                for t in range(KT):
                    dve.tensor_tensor(res[:, t, META:CTX], ps[:, 4 + t // 2, (t % 2) * SEQ:(t % 2 + 1) * SEQ],
                                      res[:, t, META:CTX], ALU.add).then_inc(S("down_added"), 1)

            add_output(1)
            normalise("norm_ff1", "norm2", META, SEQ)
            silu(1)
            add_down(1)
            dve.wait_ge(S("norm_root"), nth("norm3"))
            for k in range(KT):
                dve.scalar_tensor_tensor(res[:, k, META:CTX], res[:, k, META:CTX], V("norm3", k), nrm[:, 1, 0:SEQ],
                                         ALU.mult, ALU.mult).then_inc(S("norm3_ready"), 1)

            normalise("norm4", "norm4", META, SEQ)
            dve.wait_ge(S("normed"), normed("norm4", KT - 1))
            step(dve.memset(proj[:, 0:SHIFTED, 0:1], 0.0))
            for t in range(1, TILES2, 2):
                dve.wait_ge(S("proj2_ready"), t + 1)
                scale = HD ** -0.5 if Q0 <= t < Q0 + 4 else 1.0
                dve.tensor_scalar(proj[:, t, 1:1 + SEQ], ps[:, t % 2, 0:SEQ], scale, None, ALU.mult)\
                    .then_inc(S("proj2_copied_b"), 1)
            dve.wait_ge(S("proj2_copied_a"), 13)
            dve.wait_ge(S("proj2_copied_b"), 12)
            dve.wait_ge(S("norm_root"), nth("norm4"))
            diff = flat[:, 0:SHIFTED * SEQ].rearrange("p (a b) -> p a b", a=SHIFTED)
            step(dve.tensor_tensor(diff, proj[:, 0:SHIFTED, 0:SEQ], proj[:, 0:SHIFTED, 1:1 + SEQ], ALU.subtract))
            for t in range(SHIFTED):
                ins = dve.scalar_tensor_tensor(proj[:, t, 1:1 + SEQ], diff[:, t, :], V("mu", t),
                                               proj[:, t, 1:1 + SEQ], ALU.mult, ALU.add)
            step(ins)
            dve.tensor_scalar(lora_w, proj[0:HD, WA0, 1:1 + SEQ], EXP_MAX / 2, None, ALU.min)
            signal(dve, dve.tensor_scalar(sdg, proj[:, G0, 1:1 + SEQ], -EXP_MAX, None, ALU.max), "shifted")

            def per_pair(name):
                return V(name, 0, PAIRS).unsqueeze(2).to_broadcast([P, PAIRS, SEQ])

            rv, kv = proj[:, R0:R0 + 4, 1:1 + SEQ], proj[:, K0:K0 + 4, 1:1 + SEQ]
            signal(dve, dve.tensor_tensor(kkn, kv, per_pair("k_k"), ALU.mult), "key_scaled")
            dve.wait_ge(S("lora_w_exp"), 1)
            signal(dve, dve.tensor_scalar(lora_w, lora_w, -2.0, 1.0, ALU.mult, ALU.add), "lora_w_ready")
            dve.wait_ge(S("v_stacked"), 1)
            signal(dve, dve.tensor_copy(v_st.rearrange("p n v -> p (n v)"),
                                        ps[:, 6:8, :].rearrange("p a b -> p (a b)")), "v_st_copied")
            dve.wait_ge(S("key_sums"), 1)
            signal(dve, dve.tensor_scalar(scr.rearrange("p j t -> p (j t)"),
                                          ps[:, 4:6, :].rearrange("p a b -> p (a b)"), 1e-24, None, ALU.max),
                   "key_sums_kept")
            dve.wait_ge(S("lora_ready"), 1)
            for n, (name, dst) in enumerate((("w0", sigw), ("a0", avec))):
                for f in range(PAIRS):
                    ins = dve.tensor_scalar(dst[:, f, :],
                                            ps[:, 2 * n + f // 2, (f % 2) * SEQ:(f % 2 + 1) * SEQ],
                                            V(name, f), -EXP_MAX, ALU.add, ALU.max)
                signal(dve, ins, "lora_biased", n + 1)
            dve.wait_ge(S("reset_ready"), 1)
            dve.wait_ge(S("decay_a_sigmoids"), 1)
            one = "p j t -> p (j t)"
            signal(dve, dve.tensor_tensor_scan(lsum.rearrange(one), reset.rearrange(one), sigw.rearrange(one), 0.0,
                                               ALU.mult, ALU.add), "decay_scanned", 1)
            signal(dve, dve.tensor_tensor(sigw, lsum, sigw, ALU.subtract), "decay_scanned", 2)
            dve.wait_ge(S("key_root"), 1)
            step(dve.scalar_tensor_tensor(kkn, kkn, -1.0, scr, ALU.mult, ALU.mult))
            dve.wait_ge(S("decay_a_sigmoids"), 2)
            step(dve.scalar_tensor_tensor(scr, avec, -1.0, kv, ALU.add, ALU.mult))
            step(dve.tensor_tensor(scr, scr, per_pair("k_a"), ALU.mult))
            step(dve.tensor_tensor(kv, kv, scr, ALU.add))
            step(dve.scalar_tensor_tensor(avec, kkn, -1.0, avec, ALU.mult, ALU.mult))
            step(dve.tensor_tensor(scr, rv, kv, ALU.mult))
            signal(dve, dve.tensor_tensor(scr, scr, per_pair("r_k"), ALU.mult), "rk_ready")
            dve.wait_ge(S("bonus_sums"), 1)
            signal(dve, dve.tensor_copy(small[:, 0], ps[:, 4, 0:PACKS]), "bonus_copied")
            dve.wait_ge(S("decay_powers"), 1)
            dve.wait_ge(S("packs_zeroed"), 1)

            for cp in range(0, CHUNKS, 2):
                for m in range(2):
                    c = cp + m
                    if cp > 0:
                        dve.wait_ge(S("chunk_done"), c - 1)
                        dve.wait_ge(S("y_kept"), c - 1)
                    ts = slice(c * CHUNK, (c + 1) * CHUNK)
                    for dst, x, y in ((ar[:, m, :, 0], kkn, p_exc), (ar[:, m, :, 1], rv, p_inc),
                                      (bf[:, m], avec, p_inv), (kf[:, m], kv, p_inv)):
                        for h in range(2):
                            hs = slice(HD * h, HD * (h + 1))
                            ins = dve.tensor_tensor(dst[hs, :, CHUNK * h:CHUNK * (h + 1)], x[hs, :, ts],
                                                    y[hs, :, ts], ALU.mult)
                    signal(dve, ins, "packs_ready", c + 1)
                for m in range(2):
                    c = cp + m
                    dve.wait_ge(S("products_ready"), c + 1)
                    for j in range(PAIRS):
                        dve.tensor_tensor(wt[:, m, j], ps[:, j, :], C("pack_masks"), ALU.mult)
                    join0 = C("join")[:, 0:P].unsqueeze(1).to_broadcast([P, PAIRS, P])
                    join0_t = C("join0_t").unsqueeze(1).to_broadcast([P, PAIRS, P])
                    eye = C("ident").unsqueeze(1).to_broadcast([P, PAIRS, P])
                    ab = ps[:, 4 + m, :].rearrange("p (j c) -> p j c", j=PAIRS)
                    signal(dve, dve.tensor_tensor(xi[:, m], ab, join0_t, ALU.mult), "products_masked", c + 1)
                    step(dve.tensor_tensor(xt[:, m], wt[:, m, :, 0:P], join0, ALU.mult))
                    step(dve.tensor_tensor(xt[:, m], xt[:, m], eye, ALU.add))
                    signal(dve, dve.tensor_tensor(xi[:, m], xi[:, m], eye, ALU.add),
                           f"inverse_grown_{m}", (cp // 2) * LEVELS + 1)
                for level in range(1, LEVELS):
                    n = (cp // 2) * (LEVELS - 1) + level
                    for m in range(2):
                        dve.wait_ge(S(f"inverse_terms_{m}"), n)
                        flat2 = "p j c -> p (j c)"
                        if level < LEVELS - 1:
                            dve.tensor_tensor(xi[:, m].rearrange(flat2), ps[:, 3 * m + 1, :],
                                              xi[:, m].rearrange(flat2), ALU.add)
                        signal(dve, dve.tensor_tensor(xt[:, m].rearrange(flat2), ps[:, 3 * m + 2, :],
                                                      xt[:, m].rearrange(flat2), ALU.add),
                               f"inverse_grown_{m}", (cp // 2) * LEVELS + level + 1)
                for m in range(2):
                    c = cp + m
                    dve.wait_ge(S("state_terms"), c + 1)
                    st = "p j v -> p (j v)"
                    step(dve.tensor_tensor(state[:].rearrange(st), ps[:, 7, 0:256], state[:].rearrange(st), ALU.add))
                    end = p_inc[:, :, (c + 1) * CHUNK - 1:(c + 1) * CHUNK].to_broadcast([P, PAIRS, HD])
                    dve.wait_ge(S("y_terms"), c + 1)
                    signal(dve, dve.tensor_copy(y_all[:, c * PAIRS:(c + 1) * PAIRS, :].rearrange("p n v -> p (n v)"),
                                                ps[:, 6, 0:256]), "y_kept", c + 1)
                    signal(dve, dve.tensor_tensor(state[:], state[:], end, ALU.mult), "chunk_done", c + 1)

            def each(name):
                return small[:, name].unsqueeze(2).to_broadcast([P, PACKS, HD])

            def table(name):
                at, w = VEC_AT[name]
                return vec[:, at:at + w].unsqueeze(1).to_broadcast([P, CHUNKS, PAIRS * HD])

            by_chunk = y_all.rearrange("p (c j) v -> p c (j v)", c=CHUNKS)
            step(dve.tensor_reduce(small[:, 1], y_all, AX.X, ALU.add))
            step(dve.tensor_scalar(small[:, 1], small[:, 1], 1.0 / HD, None, ALU.mult))
            signal(dve, dve.tensor_tensor(y_all, y_all, each(1), ALU.subtract), "y_centred")
            dve.wait_ge(S("y_squares"), 1)
            signal(dve, dve.tensor_reduce(small[:, 2], scr.rearrange("p j t -> p (j t)")
                                          .rearrange("p (n v) -> p n v", n=PACKS), AX.X, ALU.add), "y_vars")
            dve.wait_ge(S("y_root"), 1)
            step(dve.tensor_tensor(y_all, y_all, each(2), ALU.mult))
            step(dve.tensor_tensor(by_chunk, by_chunk, table("lnx_w"), ALU.mult))
            step(dve.tensor_tensor(by_chunk, by_chunk, table("lnx_b"), ALU.add))
            step(dve.tensor_tensor(v_st, v_st, each(0), ALU.mult))
            step(dve.tensor_tensor(y_all, y_all, v_st, ALU.add))
            dve.wait_ge(S("gates_ready"), 1)
            signal(dve, dve.tensor_tensor(y_all.rearrange("p n v -> p (n v)"),
                                          ps[:, 0:2, :].rearrange("p a b -> p (a b)"),
                                          y_all.rearrange("p n v -> p (n v)"), ALU.mult), "rwkv_y")

            step(dve.memset(blk[:], 0.0))
            signal(dve, dve.memset(blk[:], 0.0), "blk_zeroed")
            for x in range(2):
                dve.wait_ge(S("blk_gathered"), x + 1)
                pe_add = V(("pe_k", "pe_v")[x], 0, CMP_PAIRS).unsqueeze(2).to_broadcast([P, CMP_PAIRS, 32])
                signal(dve, dve.tensor_tensor(blk[:, x], blk[:, x], pe_add, ALU.add), "blk_ready", x + 1)
            dve.wait_ge(S("cmp_hidden"), 2)
            h2 = ps[0:32, 4:6, 0:CMP_HIDDEN]
            step(dve.tensor_copy(hid_c[:], h2))
            step(dve.tensor_tensor(gel[:], hid_c[:], hid_c[:], ALU.mult))
            step(dve.tensor_scalar(gel[:], gel[:], 0.044715, 1.0, ALU.mult, ALU.add))
            step(dve.tensor_tensor(gel[:], gel[:], hid_c[:], ALU.mult))
            signal(dve, dve.tensor_scalar(gel[:], gel[:], -EXP_MAX / GELU, None, ALU.max), "cmp_gelu_arg")
            dve.wait_ge(S("cmp_gelu_sigmoid"), 1)
            signal(dve, dve.tensor_tensor(hid_c[:], hid_c[:], gel[:], ALU.mult), "cmp_gelu")
            dve.wait_ge(S("cmp_scores"), 1)
            bias = C("cmp_bias").rearrange("p (t h n) -> p t h n", t=2, h=NQH)
            for g in range(KVH):
                dve.tensor_tensor(s_cmp[:, :, g * GQA:(g + 1) * GQA, :],
                                  ps[:, 4 + g, 0:2 * GQA * CMP_PAD].rearrange("p (t h n) -> p t h n", t=2, h=GQA),
                                  bias[:, :, g * GQA:(g + 1) * GQA, :], ALU.add)
            own = C("cmp_own").rearrange("p (a c) -> p a c", a=GQA)
            vrep = vown_src
            step(dve.tensor_copy(vrep, ps[:, 3, 0:P]))
            step(dve.tensor_tensor(vown[:], own, vrep.unsqueeze(1).to_broadcast([P, GQA, P]), ALU.mult))
            flat_s = s_cmp[:].rearrange("p t h n -> p (t h) n")
            flat_m = mx_c[:].rearrange("p t h -> p (t h)")
            flat_d = den_c[:].rearrange("p t h -> p (t h)")
            wide = [P, 2 * NQH, CMP_PAD]
            step(dve.tensor_reduce(flat_m, flat_s, AX.X, ALU.max))
            signal(dve, dve.tensor_tensor(flat_s, flat_s, flat_m.unsqueeze(2).to_broadcast(wide), ALU.subtract),
                   "cmp_centred")
            dve.wait_ge(S("cmp_exps"), 1)
            step(dve.tensor_reduce(flat_d, flat_s, AX.X, ALU.add))
            step(dve.reciprocal(flat_d, flat_d))
            dve.wait_ge(S("nsa_values"), 1)
            gv = gates[:].rearrange("p t (h b) -> p t h b", b=3)
            step(dve.tensor_tensor(den_c[:], den_c[:], gv[:, :, :, 0], ALU.mult))
            step(dve.tensor_tensor(den_c[:], den_c[:], C("cmp_any").unsqueeze(2).to_broadcast([P, 2, NQH]),
                                   ALU.mult))
            signal(dve, dve.tensor_tensor(flat_s, flat_s, flat_d.unsqueeze(2).to_broadcast(wide), ALU.mult),
                   "cmp_probs")
            alibi = C("alibi").rearrange("p (g a k) -> p g a k", g=KVH, a=GQA)
            for a in range(GQA):
                dve.wait_ge(S("nsa_scores"), a + 1)
                if a > 0:
                    dve.wait_ge(S("nsa_probs_turned"), a)
                sv = s_nsa[:].rearrange("p (b g) k -> p b g k", b=2)
                pv = ps[:, 0:4, 0:P + SEQ].rearrange("p (b g) k -> p b g k", b=2)
                for br in range(2):
                    dve.tensor_tensor(sv[:, br, :, 0:P], pv[:, br, :, 0:P], alibi[:, :, a, P:SEQ], ALU.add)
                    ins = dve.tensor_tensor(sv[:, br, :, P:P + SEQ], pv[:, br, :, P:P + SEQ], alibi[:, :, a, :],
                                            ALU.add)
                step(ins)
                dve.tensor_reduce(mx_n[:, 0, :], s_nsa[:, :, 0:P], AX.X, ALU.max, negate=True)
                signal(dve, dve.tensor_reduce(mx_n[:, 1, :], s_nsa[:, :, P:P + SEQ], AX.X, ALU.max, negate=True),
                       "nsa_max", a + 1)
                dve.wait_ge(S("nsa_exps"), a + 1)
                step(dve.reciprocal(den_n[:], den_n[:]))
                for g in range(KVH):
                    ins = dve.tensor_tensor(den_n[:].rearrange("p t (b g) -> p t b g", b=2)[:, :, :, g],
                                            den_n[:].rearrange("p t (b g) -> p t b g", b=2)[:, :, :, g],
                                            gv[:, :, g * GQA + a, 1:3], ALU.mult)
                step(ins)
                for slot in range(4):
                    for t, (c0, n) in enumerate(((0, P), (P, SEQ))):
                        ins = dve.tensor_scalar(s_nsa[:, slot, c0:c0 + n], s_nsa[:, slot, c0:c0 + n],
                                                den_n[:, t, slot:slot + 1], None, ALU.mult)
                signal(dve, ins, "nsa_probs", a + 1)
                dve.wait_ge(S("nsa_out"), a + 1)
                signal(dve, dve.tensor_copy(yT[:, 4 + a, :], ps[:, 4 + a % 2, 0:SEQ]), "nsa_out_copied", a + 1)
            dve.wait_ge(S("rwkv_out"), 1)
            signal(dve, dve.memset(small[:, 7], 0.0), "y2_ready")

            add_output(2)
            normalise("norm_ff2", "norm5", META, SEQ)
            silu(2)
            add_down(2)
            dve.wait_ge(S("norm_root"), nth("norm6"))
            for k in range(KT):
                dve.scalar_tensor_tensor(yT[:, k, :], res[:, k, META:CTX], V("norm6", k), nrm[:, 1, 0:SEQ],
                                         ALU.mult, ALU.mult).then_inc(S("final_ready"), 1)




def tiles_in(w):
    n = w.shape[1]
    t = -(-n // P)
    w = np.concatenate([w, np.zeros((w.shape[0], t * P - n), w.dtype)], 1)
    return w.reshape(KT, P, t, P).transpose(2, 1, 0, 3).reshape(t, P, TILE)


def to_blocks(tiles):
    if len(tiles) % 2:
        tiles = np.concatenate([tiles, np.zeros_like(tiles[:1])])
    return tiles.reshape(-1, 2, P, TILE).transpose(0, 2, 1, 3).reshape(-1, P, BLOCK)


def ffn_blocks(gate, up, down):
    g, u = tiles_in(gate), tiles_in(up)
    both = np.stack([g, u], 1).reshape(-1, P, TILE)
    return [to_blocks(both), to_blocks(down.reshape(FT, P, TILE))]


def cols(v):
    return v.reshape(-1, P).T


def layout(i):
    f = np.float32
    i = {k: np.asarray(v) for k, v in i.items()}
    w = i["w_in"][0]
    u, qf, kf, vf, fl, qs, ks, vs = np.split(w, np.cumsum([256, 384, 384, 384, 6, 384, 384]), 1)
    w1 = np.concatenate([ks, qs, vs, vf, kf, qf, u, fl], 1)
    stream = [to_blocks(tiles_in(w1)), to_blocks(tiles_in(i["w_out"][0]))]
    stream += ffn_blocks(i["w_gate"][0], i["w_up"][0], i["w_down"][0])
    h = np.concatenate([i["meta_tokens"], i["x"][0]], 0)
    xT = h.T.reshape(KT, P, CTX).transpose(1, 0, 2).reshape(P, -1)
    vecs = {
        "norm1": cols(i["norm1"][0]), "norm2": cols(i["norm2"][0]), "norm3": cols(i["final_norm"]),
        "fox_gain": cols(i["fox_out_gain"][0]), "sb_gain": cols(i["sb_out_gain"][0]),
        "pool_scale": cols(i["pool_scale"][0]),
    }
    fb = np.zeros((P, 1), f)
    fb[0:6, 0] = i["forget_bias"][0]
    vecs["forget_bias"] = fb
    pw = np.zeros((P, 2, P), f)
    for g in range(4):
        r = HD * (g % 2)
        pw[r:r + HD, g // 2, r:r + HD] = i["pool_w"][0, g]
    vecs["pool_w"] = pw.reshape(P, -1)
    w = i["w_in_2"][0]
    rw, nsa = w[:, 0:SHIFTED * P], w[:, SHIFTED * P:]
    q, kvs, gl = nsa[:, 0:512], nsa[:, 512:1280], nsa[:, 1280:]
    q = q.reshape(D, KVH, GQA, HD).transpose(0, 2, 1, 3).reshape(D, -1)
    stream.append(to_blocks(tiles_in(np.concatenate([rw, q, kvs, gl], 1))))
    for n in ("nsa_cmp_k_w1_2", "nsa_cmp_v_w1_2"):
        stream.append(to_blocks(i[n][0].reshape(4, 4, P, CMP_HIDDEN).transpose(0, 2, 1, 3).reshape(4, P, TILE)))
    wo = i["w_out_2"][0]
    wn = wo[512:].reshape(KVH, GQA, HD, D).transpose(1, 0, 2, 3).reshape(512, D)
    stream.append(to_blocks(tiles_in(np.concatenate([wo[0:512], wn], 0))))
    stream += ffn_blocks(i["ffn_w_gate_2"][0], i["ffn_w_up_2"][0], i["ffn_w_down_2"][0])

    def by_head(v):
        return np.repeat(v.reshape(PAIRS, 2, HD).transpose(1, 0, 2).reshape(2, PAIRS * HD), CHUNK, 0)

    vecs |= {
        "norm4": cols(i["norm1_g_2"][0]), "norm5": cols(i["norm2_g_2"][0]), "norm6": cols(i["norm_f_g_2"]),
        "mu": cols(i["mu_shift_2"][0]), "w0": cols(i["rwkv_w0_2"][0]), "a0": cols(i["rwkv_a0_2"][0]),
        "k_k": cols(i["rwkv_k_k_2"][0]), "k_a": cols(i["rwkv_k_a_2"][0]), "r_k": cols(i["rwkv_r_k_2"][0]),
        "w2a2": np.concatenate([i["rwkv_w2_2"][0], i["rwkv_a2_2"][0]], 0),
        "g2": i["rwkv_g2_2"][0].reshape(P, PAIRS, 2, HD).transpose(0, 2, 1, 3).reshape(P, -1),
        "lnx_w": by_head(i["rwkv_lnx_w_2"][0]), "lnx_b": by_head(i["rwkv_lnx_b_2"][0]),
        "pe_k": i["nsa_pe_k_2"][0].reshape(CMP_PAIRS, P).T, "pe_v": i["nsa_pe_v_2"][0].reshape(CMP_PAIRS, P).T,
        "cmp_w2k": i["nsa_cmp_k_w2_2"][0].reshape(2, P, HD).transpose(1, 0, 2).reshape(P, -1),
        "cmp_w2v": i["nsa_cmp_v_w2_2"][0].reshape(2, P, HD).transpose(1, 0, 2).reshape(P, -1),
    }
    return {
        "xT": np.ascontiguousarray(xT), "weights": np.ascontiguousarray(np.concatenate(stream)),
        "consts": np.concatenate(list(constant_tables().values()), 1),
        "vecs": np.concatenate([vecs[k] for k in VEC_WIDTHS], 1),
    }


def kernel(**inputs):
    import concourse.bacc as bacc
    from concourse.bass_utils import run_bass_kernel_spmd

    nc = bacc.Bacc("TRN2", target_bir_lowering=False, num_devices=1)
    arrays, aps = {}, []
    for name, a in layout(inputs).items():
        a = np.ascontiguousarray(a)
        arrays[f"in_{name}"] = a
        aps.append(nc.dram_tensor(f"in_{name}", a.shape, mybir.dt.from_np(a.dtype), kind="ExternalInput").ap())
    out = nc.dram_tensor("out_features", (P, KT * SEQ), F32, kind="ExternalOutput").ap()
    build_program(nc, *aps, out)
    got = run_bass_kernel_spmd(nc, [arrays], core_ids=[0]).results[0]["out_features"]
    return got.reshape(P, KT, SEQ).transpose(2, 1, 0).reshape(1, SEQ, D)
```

```python
from contextlib import ExitStack

import numpy as np

import concourse.bass as bass
from concourse import mybir

P = 128
ALU = mybir.AluOpType
ACT = mybir.ActivationFunctionType
AX = mybir.AxisListType
F32 = mybir.dt.float32
F32R = mybir.dt.float32r

D = 1024
KT = D // P
SEQ = 256
META = 16
CTX = META + SEQ
HD = 64
EPS = 1e-6
NEG = -1e30
DFF = 2816
FT = DFF // P

HEADS1 = 6
KS0, QS0, VS0, VF0, KF0, QF0, U0, FL0 = 0, 3, 6, 9, 12, 15, 18, 20
TILES1 = 21
POOL_WINDOWS = (2, 4, 8, 16)
META_SLOT = (0, 2, 1)

R0, K0, V0, WA0, G0, Q0, KC0, VC0, KS1, VS1, KW1, VW1, GL0 = 0, 4, 8, 12, 13, 14, 18, 19, 20, 21, 22, 23, 24
SHIFTED = 14
TILES2 = 25
PAIRS = 4
CHUNK = 64
CHUNKS = SEQ // CHUNK
PACKS = PAIRS * CHUNKS
LEVELS = 6
DECAY = float(np.exp(-0.5))
GN_EPS = 64e-5
GQA, KVH = 4, 2
NQH = GQA * KVH
CMP_BLOCK, CMP_STRIDE = 32, 16
N_CMP = (SEQ - CMP_BLOCK) // CMP_STRIDE + 1
CMP_PAD = 16
CMP_PAIRS = CMP_BLOCK // 2
CMP_HIDDEN = 256
EXP_MAX = 43.0
GELU = 2.0 * float(np.sqrt(2.0 / np.pi))

TILE = KT * P
BLOCK = 2 * TILE
RING = 2
SLOTS = 4
UNROLL = 4


def blocks_of(tiles):
    return -(-tiles // 2)


B_IN1 = 0
B_OUT1 = B_IN1 + blocks_of(TILES1)
B_UP1 = B_OUT1 + KT // 2
B_DOWN1 = B_UP1 + FT
B_IN2 = B_DOWN1 + FT // 2
B_CMP = B_IN2 + blocks_of(TILES2)
B_OUT2 = B_CMP + 4
B_UP2 = B_OUT2 + KT // 2
B_DOWN2 = B_UP2 + FT

T_IN1 = 0
T_OUT1 = T_IN1 + TILES1
T_UP1 = T_OUT1 + KT
T_DOWN1 = T_UP1 + 2 * FT
T_IN2 = T_DOWN1 + FT
T_OUT2 = T_IN2 + TILES2
T_UP2 = T_OUT2 + KT
T_DOWN2 = T_UP2 + 2 * FT
T_END = T_DOWN2 + FT
PHASES = ((T_IN1, B_IN1), (T_OUT1, B_OUT1), (T_UP1, B_UP1), (T_DOWN1, B_DOWN1), (T_IN2, B_IN2),
          (T_OUT2, B_OUT2), (T_UP2, B_UP2), (T_DOWN2, B_DOWN2), (T_END, None))


def phase_of(t):
    return next(n for n in range(len(PHASES) - 1) if t < PHASES[n + 1][0])


def place(t):
    t0, b0 = PHASES[phase_of(t)]
    return b0 + (t - t0) // 2, (t - t0) % 2


def freed(t):
    n = phase_of(t)
    k, layer = t - PHASES[n][0], n // 4
    if n % 4 == 0:
        return f"proj{layer + 1}_ready", k + 1
    if n % 4 == 1:
        return "out_ready", layer * KT + k + 1
    if n % 4 == 2:
        return ("gate_ready", "up_ready")[k % 2], layer * FT + k // 2 + 1
    return ("down_ready", (layer + 1) * KT) if k == FT - 1 else ("down_used", layer * (FT - 1) + k + 1)

NORMS = ("norm1", "norm_ff1", "norm3", "norm4", "norm_ff2", "norm6")
FEEDING = ("norm1", "mixer1", "norm_ff1", "norm4", "mixer2", "norm_ff2")


def nth(name):
    return NORMS.index(name) + 1


def normed(name, k):
    return FEEDING.index(name) * KT + k + 1




def constant_tables():
    i = np.arange(P)
    c = {}
    c["ident"] = np.eye(P)
    c["ones"] = np.ones((P, P))
    c["neg_ones"] = -np.ones((P, P))
    c["neg_from"] = -(i[:, None] >= i[None, :]).astype(float)
    strict = i[:, None] < i[None, :]
    c["strict"] = strict.astype(float)
    c["strict_add"] = np.where(strict, 0.0, NEG)
    a = np.where(np.arange(META + P)[None, :] <= META + i[:, None], 0.0, NEG)
    b = np.where(np.arange(CTX)[None, :] <= META + P + i[:, None], 0.0, NEG)
    c["causal1"] = np.concatenate([a, b], 1)
    c["head_ones"] = np.kron(np.eye(2), np.ones((HD, HD)))
    sel = np.zeros((P, HEADS1, P))
    for h in range(HEADS1):
        sel[h, h] = 1.0
    c["pick_head"] = sel.reshape(P, -1)
    c["eps"] = np.full((P, 1), EPS)
    c["one"] = np.ones((P, 1))
    slopes = 2.0 ** (-8.0 * np.arange(1, NQH + 1) / NQH)
    k = np.arange(SEQ)
    dist = (P + i[:, None]) - k[None, :]
    c["alibi"] = np.where(dist[:, None, :] >= 0, -slopes[None, :, None] * dist[:, None, :], NEG).reshape(P, -1)
    end = np.arange(CMP_PAD) * CMP_STRIDE + CMP_BLOCK - 1
    t = i[:, None] + P * np.arange(2)[None, :]
    dist = t[:, :, None] - end
    ok = (dist >= 0) & (np.arange(CMP_PAD) < N_CMP)
    c["cmp_bias"] = np.where(ok[:, :, None, :], -slopes[None, None, :, None] * dist[:, :, None, :], NEG).reshape(P, -1)
    c["cmp_any"] = ok.any(-1).astype(float)
    rows = np.arange(P)
    c["cmp_spread"] = ((rows[None, :] % CMP_PAD == i[:, None]) & (i[:, None] < N_CMP)).astype(float)
    m = np.zeros((P, GQA, P))
    for r in rows:
        head = r // CMP_PAD
        m[r, head % GQA, HD * (head // GQA):HD * (head // GQA) + HD] = 1.0
    c["cmp_own"] = m.reshape(P, -1)
    same = i[:, None] // CHUNK == i[None, :] // CHUNK
    before = same & (i[:, None] < i[None, :])
    upto = same & (i[:, None] <= i[None, :])
    c["pack_masks"] = np.concatenate([before, upto, before, upto], 1).astype(float)
    lv = []
    for level in range(LEVELS):
        w = 2 << level
        lv.append((i[:, None] // w == i[None, :] // w) & (i[:, None] % w < w // 2) & (i[None, :] % w >= w // 2))
    c["join"] = np.concatenate(lv, 1).astype(float)
    c["join0_t"] = lv[0].T.astype(float)
    c["gn_eps"] = np.full((P, 1), GN_EPS)
    return {k: np.ascontiguousarray(v, np.float32) for k, v in c.items()}


def columns(widths):
    at, out = 0, {}
    for k, w in widths.items():
        out[k] = (at, w)
        at += w
    return out, at


CONST_AT, CONST_W = columns({k: v.shape[1] for k, v in constant_tables().items()})

VEC_WIDTHS = {
    "norm1": KT, "norm2": KT, "norm3": KT,
    "norm4": KT, "norm5": KT, "norm6": KT, "mu": SHIFTED, "w0": PAIRS, "a0": PAIRS, "k_k": PAIRS, "k_a": PAIRS,
    "r_k": PAIRS, "w2a2": PAIRS * P, "g2": PAIRS * P, "lnx_w": PAIRS * HD, "lnx_b": PAIRS * HD,
    "pe_k": CMP_PAIRS, "pe_v": CMP_PAIRS, "cmp_w2k": 2 * HD, "cmp_w2v": 2 * HD,
    "fox_gain": 3, "sb_gain": 3, "pool_scale": 2, "forget_bias": 1, "pool_w": 2 * P,
}
VEC_AT, VEC_W = columns(VEC_WIDTHS)


def build_program(nc, xT, weights, consts, vecs, out):
    ctx = ExitStack()
    sems = {}

    def S(name):
        if name not in sems:
            sems[name] = ctx.enter_context(nc.semaphore(name))
        return sems[name]

    def sb(name, shape):
        return ctx.enter_context(nc.sbuf_tensor(name, shape, F32))

    def parts(name, shape):
        return ctx.enter_context(nc.sbuf_tensor(name, shape, F32R))

    with ctx:
        ring = sb("ring", [P, RING, 2, KT, P])
        cst = sb("cst", [P, CONST_W])
        vec = sb("vec", [P, VEC_W])
        res = sb("res", [P, KT, CTX])
        act_in = sb("act_in", [P, KT, CTX])
        act_hi = parts("act_hi", [P, KT, CTX])
        act_lo = parts("act_lo", [P, KT, CTX])
        yT = sb("yT", [P, KT, SEQ])
        flat = sb("scratch", [P, 5632])
        nrm = sb("nrm", [P, 2, CTX])
        sig = sb("sig", [P, 2, SEQ])
        sig2 = sb("sig2", [P, 2, SEQ])
        state = sb("state", [P, PAIRS, HD])
        rhs_sa = sb("rhs_sa", [P, 2, PAIRS, HD])
        small = sb("small", [P, 8, 16])
        with ExitStack() as mixer:
            arena = mixer.enter_context(nc.sbuf_tensor("arena", [P, 12288], F32))
            proj = mixer.enter_context(nc.sbuf_tensor("proj", [P, 25, CTX], F32))
            vtok = mixer.enter_context(nc.sbuf_tensor("vtok", [P, 3, 12, HD], F32))
        w_hi = parts("w_hi", [P, SLOTS, KT, P])
        w_lo = parts("w_lo", [P, SLOTS, KT, P])
        hid_hi = parts("hid_hi", [P, FT, SEQ])
        hid_lo = parts("hid_lo", [P, FT, SEQ])
        ps = ctx.enter_context(nc.psum_tensor("ps", [P, 8, 512], F32))

        def C(name, parts=P):
            at, w = CONST_AT[name]
            return cst[0:parts, at:at + w]

        def V(name, j=0, n=1):
            at, _ = VEC_AT[name]
            return vec[:, at + j:at + j + n]

        landed = [S(f"weights_landed_{r}") for r in range(RING)]

        class Steps:

            def __init__(self, eng, name):
                self.eng, self.sem, self.n = eng, S(name), 0

            def __call__(self, ins):
                self.n += 1
                ins.then_inc(self.sem, 1)
                self.eng.wait_ge(self.sem, self.n)

        def signal(eng, ins, name, n=1):
            ins.then_inc(S(name), 1)
            eng.wait_ge(S(name), n)

        sq = act_in
        sb_nl = flat[:, 0:1152].rearrange("p (h c) -> p h c", h=3)
        sb_nlm = flat[0:META, 1152:1920].rearrange("p (h c) -> p h c", h=3)
        pT = flat[:, 1920:3072].rearrange("p (h c) -> p h c", h=3)
        pTm = flat[0:META, 3072:3840].rearrange("p (h c) -> p h c", h=3)
        s_row = flat[:, 3840:3840 + 1248].rearrange("p (h c) -> p h c", h=3)
        mx = flat[:, 5100:5106].rearrange("p (t h) -> p t h", t=2)
        den = flat[:, 5106:5112].rearrange("p (t h) -> p t h", t=2)
        rden = flat[:, 5112:5118].rearrange("p (t h) -> p t h", t=2)
        heads_out = act_in[:, :, :].rearrange("p a b -> p (a b)")[:, 0:6 * SEQ].rearrange("p (t q) -> p t q", t=6)
        def carve(at, *shape, parts=P):
            n = int(np.prod(shape))
            names = " ".join("abcd"[:len(shape)])
            return arena[0:parts, at:at + n].rearrange(f"p ({names}) -> p {names}",
                                                       **dict(zip("abcd", shape))), at + n

        negc, at = carve(2 * SLOTS * TILE, 1, CTX, parts=8)
        negc = negc[:, 0, :]
        fl_t, at = carve(at, 2, CTX, parts=8)
        pool_s, at = carve(at, 2, 2, CTX)
        hsq, at = carve(at, 3, SEQ)
        hr, at = carve(at, 3, SEQ)
        ar, at = carve(0, 2, PAIRS, 2, P)
        ar = arena[:, 0:2048].rearrange("p (m j x c) -> p m j x c", m=2, j=PAIRS, x=2)
        bf, at = carve(2048, 2, PAIRS, P)
        kf, at = carve(at, 2, PAIRS, P)
        wt, at = carve(at, 2, PAIRS, 4 * P)
        xi, at = carve(at, 2, PAIRS, P)
        xt, at = carve(at, 2, PAIRS, P)
        pb, at = carve(at, 2, PAIRS, P)
        nl, at = carve(at, 2, PAIRS, P)
        def feat(t, at):
            return t[:, at:at + PAIRS * SEQ].rearrange("p (j t) -> p j t", j=PAIRS)
        act_flat = act_in[:, :, :].rearrange("p a b -> p (a b)")
        vtok_flat = vtok[:, :, :, :].rearrange("p a b c -> p (a b c)")
        sigw, lsum, avec, kkn, scr = (feat(flat, 1024 * n) for n in range(5))
        sdg, lora_w = flat[:, 5120:5376], flat[0:HD, 5376:5632]
        p_inc, p_inv = feat(act_flat, 0), feat(act_flat, 1024)
        p_exc = yT[:, 4:8, :]
        reset = yT[:, 0:4, :]
        y_all = vtok_flat[:, 0:1024].rearrange("p (n v) -> p n v", n=PACKS)
        v_st = vtok_flat[:, 1024:2048].rearrange("p (n v) -> p n v", n=PACKS)
        s_nsa, at = carve(0, 4, P + SEQ)
        pt_nsa, at = carve(at, 4, P + SEQ)
        vt_nsa, at = carve(at, 2, 2, P)
        blk, at = carve(at, 2, CMP_PAIRS, 32)
        hid_c, at = carve(at, 2, CMP_HIDDEN, parts=32)
        gel, at = carve(at, 2, CMP_HIDDEN, parts=32)
        hid_t, at = carve(at, 2, 2, 32)
        kcmp, at = carve(at, 1, 32)
        vcmp, at = carve(at, 1, P, parts=CMP_PAD)
        vown, at = carve(at, GQA, P)
        s_cmp, at = carve(at, 2, NQH, CMP_PAD)
        pt_cmp, at = carve(at, 2, P)
        gates, at = carve(at, 2, 24)
        gl_t, at = carve(at, 1, SEQ, parts=24)
        coef, at = carve(at, 2, 3, NQH)
        vown_src, at = carve(at, 1, P)
        vown_src = vown_src[:, 0]
        mx_n, at = carve(at, 2, 4)
        den_n, at = carve(at, 2, 4)
        mx_c, at = carve(at, 2, NQH)
        den_c, at = carve(at, 2, NQH)

        def down_ahead(layer):
            return FT - 1 if layer == 1 else FT - SLOTS

        block = ctx.enter_context(nc.Block())

        @block.sync
        def _(sp):
            sp.dma_start(cst[:], consts).then_inc(S("consts_landed"), 16)
            sp.dma_start(vec[:], vecs).then_inc(S("vecs_landed"), 16)

            def load(b):
                if B_CMP <= b - RING < B_OUT2:
                    sp.wait_ge(S("cmp_block_used"), b - RING - B_CMP + 1)
                elif b >= RING:
                    last = max(t for t in range(T_END) if place(t)[0] == b - RING)
                    sp.wait_ge(S("w_split"), last + 1)
                sp.dma_start(ring[:, b % RING].rearrange("p a k c -> p (a k c)"), weights[b])\
                    .then_inc(landed[b % RING], 16)

            def load_up(b_up, t_up):
                with sp.Fori(0, (FT - RING) // UNROLL) as i:
                    for u in range(UNROLL):
                        b = b_up + RING + u
                        sp.wait_ge(S("w_split"), i * (2 * UNROLL) + (t_up + 2 * u + 2))
                        sp.dma_start(ring[:, b % RING].rearrange("p a k c -> p (a k c)"),
                                     weights[bass.ds(i * UNROLL + b, 1)].rearrange("o p c -> (o p) c"))\
                            .then_inc(landed[b % RING], 16)

            for b in range(B_IN1, B_UP1 + RING):
                load(b)
            load_up(B_UP1, T_UP1)
            for b in range(B_DOWN1, B_UP2 + RING):
                load(b)
            load_up(B_UP2, T_UP2)
            for b in range(B_DOWN2, B_DOWN2 + FT // 2):
                load(b)

        @block.gpsimd
        def _(pool):
            pool.dma_start(res[:].rearrange("p k t -> p (k t)"), xT).then_inc(S("x_landed"), 16)
            pool.wait_ge(S("normed"), normed("norm4", KT - 1))
            signal(pool, pool.memset(state[:], 0.0), "state_zeroed")
            pool.memset(reset, 1.0).then_inc(S("reset_ones"), 1)
            pool.wait_ge(S("reset_ones"), 1)
            signal(pool, pool.memset(reset.rearrange("p j (c t) -> p j c t", c=CHUNKS)[:, :, :, 0:1], 0.0),
                   "reset_ready")
            pool.wait_ge(S("proj2_ready"), TILES2)
            signal(pool, pool.memset(arena[:, 0:4096], 0.0), "packs_zeroed")
            for cp in range(0, CHUNKS, 2):
                for level in range(1, LEVELS):
                    for m in range(2):
                        c = cp + m
                        if level == 1:
                            pool.wait_ge(S("products_masked"), c + 1)
                        if level > 1:
                            pool.wait_ge(S(f"join_products_{m}"), (cp // 2) * (LEVELS - 1) + level - 1)
                        elif cp > 0:
                            pool.wait_ge(S("chunk_done"), c - 1)
                        pool.tensor_tensor(nl[:, m], wt[:, m, :, 0:P],
                                           C("join")[:, level * P:(level + 1) * P].unsqueeze(1)
                                           .to_broadcast([P, PAIRS, P]), ALU.mult)\
                            .then_inc(S(f"joins_{m}"), 1)
            pool.wait_ge(S("final_ready"), KT)
            pool.dma_start(out, yT[:].rearrange("p k t -> p (k t)")).then_inc(S("stored"), 16)
            pool.wait_ge(S("stored"), 16)

        @block.tensor
        def _(pe):
            def part_products(dst, slot, k, hi, lo, first, last):
                pe.matmul(dst, w_hi[:, slot, k, :], hi, start=first, stop=False, skip_group_check=True)
                pe.matmul(dst, w_hi[:, slot, k, :], lo, start=False, stop=False, skip_group_check=True)
                return pe.matmul(dst, w_lo[:, slot, k, :], hi, start=False, stop=last, skip_group_check=True)

            def tile_products(dst, slot, n, first=None):
                for k in range(KT):
                    if first is not None:
                        pe.wait_ge(S("normed"), normed(first, k))
                    mm = part_products(dst, slot, k, act_hi[:, k, 0:n], act_lo[:, k, 0:n], k == 0, k == KT - 1)
                return mm

            def have(b):
                pe.wait_ge(landed[b % RING], 16 * (b // RING + 1))

            def sum_squares(name, tokens):
                pe.wait_ge(S("norm_squares"), nth(name))
                for k in range(KT):
                    mm = pe.matmul(ps[:, 7, 0:tokens], C("ones"), sq[:, k, 0:tokens],
                                   start=(k == 0), stop=(k == KT - 1))
                mm.then_inc(S("norm_sums"), 1)

            def feed_forward(layer, t_up):
                t_down = t_up + 2 * FT

                def up(j, i=None):
                    step = 0 if i is None else i * UNROLL
                    t = t_up + 2 * j
                    if j >= 2:
                        pe.wait_ge(S("hid_full"), step + ((layer - 1) * FT + j - 1))
                    pe.wait_ge(S("w_split"), step * 2 + (t + 1))
                    tile_products(ps[:, 2 * (j % 2), 0:SEQ], t % SLOTS, SEQ, f"norm_ff{layer}" if j == 0 else None)\
                        .then_inc(S("gate_ready"), 1)
                    pe.wait_ge(S("w_split"), step * 2 + (t + 2))
                    tile_products(ps[:, 2 * (j % 2) + 1, 0:SEQ], (t + 1) % SLOTS, SEQ).then_inc(S("up_ready"), 1)

                up(0)
                up(1)
                with pe.Fori(0, (FT - 2) // UNROLL) as i:
                    for u in range(UNROLL):
                        up(2 + u, i)

                def down(d, i=None):
                    step = 0 if i is None else i * UNROLL
                    t = t_down + d
                    pe.wait_ge(S("w_split"), step + (t + 1))
                    pe.wait_ge(S("hid_ready"), step + ((layer - 1) * FT + d + 1))
                    last = d == FT - 1
                    if i is None:
                        hi, lo = hid_hi[:, d, :], hid_lo[:, d, :]
                    else:
                        hi, lo = (x[:, bass.ds(i * UNROLL + d, 1), :].rearrange("p o t -> p (o t)")
                                  for x in (hid_hi, hid_lo))
                    for f in range(KT):
                        mm = part_products(ps[:, 4 + f // 2, (f % 2) * SEQ:(f % 2 + 1) * SEQ], t % SLOTS, f,
                                           hi, lo, d == 0 and f % 2 == 0, last)
                        if last:
                            mm.then_inc(S("down_ready"), 1)
                    if not last:
                        mm.then_inc(S("down_used"), 1)

                down(0)
                with pe.Fori(0, (FT - 2) // UNROLL) as i:
                    for u in range(UNROLL):
                        down(1 + u, i)
                down(FT - 1)

            pe.wait_ge(S("consts_landed"), 16)
            sum_squares("norm1", CTX)
            for t in range(TILES1):
                pe.wait_ge(S("w_split"), T_IN1 + t + 1)
                if t >= 2:
                    pe.wait_ge(S("proj1_copied_" + "ab"[t % 2]), (t - 2) // 2 + 1)
                tile_products(ps[:, t % 2, 0:CTX], (T_IN1 + t) % SLOTS, CTX,
                              "norm1" if t == 0 else None).then_inc(S("proj1_ready"), 1)

            pe.wait_ge(S("proj1_copied_a"), 11)
            pe.wait_ge(S("proj1_copied_b"), 10)
            for kt, (t0, nt) in enumerate(((META, P), (META + P, P), (0, META))):
                for f in range(6):
                    mm = pe.transpose(ps[0:nt, 2 * kt + f // 4, (f % 4) * P:(f % 4 + 1) * P],
                                      proj[:, VS0 + f, t0:t0 + nt], C("ident"))
                mm.then_inc(S("v1_turned"), 1)

            def meta_dst(j):
                return ps[0:META, 3 + j % 2, (j // 2) * SEQ:(j // 2 + 1) * SEQ]

            def half_of(h):
                return slice(HD * (h % 2), HD * (h % 2) + HD)

            def weighted_values(src, srcm, g, v0, ready, done):
                pe.wait_ge(S(ready), g + 1)
                for j in range(3):
                    h = 3 * g + j
                    dst = ps[half_of(h), 5 + h // 2 - (3 * g) // 2, 0:SEQ]
                    vh = v0 + h
                    pe.matmul(dst, vtok[:, 0, vh, :], src[:, j, 0:SEQ], start=True, stop=False)
                    pe.matmul(dst, vtok[0:META, 2, vh, :], srcm[:, META_SLOT[j], :], start=False, stop=False)
                    mm = pe.matmul(dst[:, P:SEQ], vtok[:, 1, vh, :], src[:, j, SEQ:SEQ + P],
                                   start=False, stop=True)
                mm.then_inc(S(done), 1)

            pe.wait_ge(S("v1_copied"), 3)
            for g in range(2):
                if g == 1:
                    pe.wait_ge(S("sb_weights"), 1)
                for j in range(3):
                    h = 3 * g + j
                    hs = half_of(h)
                    q = proj[hs, QS0 + h // 2, META:CTX]
                    k = proj[hs, KS0 + h // 2, :]
                    pe.matmul(ps[:, j, 0:SEQ], k[:, META:META + P], q, start=True, stop=True,
                              skip_group_check=True)
                    pe.matmul(ps[:, j, SEQ:SEQ + P], k[:, META + P:CTX], q[:, P:SEQ], start=False, stop=True,
                              skip_group_check=True)
                    mm = pe.matmul(meta_dst(j), k[:, 0:META], q,
                                   start=(j < 2), stop=True, skip_group_check=True)
                mm.then_inc(S("sb_logits"), 1)
                pe.wait_ge(S("sb_logs"), g + 1)
                for j in range(3):
                    a_all = ps[:, j, 0:SEQ]
                    b_all = ps[:, j, SEQ:SEQ + P]
                    m_all = meta_dst(j)
                    nl_a, nl_b, nl_m = sb_nl[:, j, 0:SEQ], sb_nl[:, j, SEQ:SEQ + P], sb_nlm[:, META_SLOT[j], :]
                    kw = dict(start=False, stop=True, skip_group_check=True)
                    pe.matmul(a_all, C("neg_from"), nl_a, **kw)
                    pe.matmul(a_all[:, P:SEQ], C("neg_ones"), nl_b, **kw)
                    pe.matmul(a_all[:, 0:P], C("ident"), C("strict_add"), **kw)
                    pe.matmul(b_all, C("neg_from"), nl_b, **kw)
                    pe.matmul(b_all, C("ident"), C("strict_add"), **kw)
                    pe.matmul(m_all, C("neg_from")[0:META, 0:META], nl_m, **kw)
                    pe.matmul(m_all, C("neg_ones")[:, 0:META], nl_a, **kw)
                    mm = pe.matmul(m_all[:, P:SEQ], C("neg_ones")[:, 0:META], nl_b, **kw)
                mm.then_inc(S("sb_sums"), 1)
                if g == 1:
                    pe.wait_ge(S("sb_out_copied"), 1)
                weighted_values(pT, pTm, g, 0, "sb_weights", "sb_out")

            pe.wait_ge(S("sb_out_copied"), 2)
            pe.wait_ge(S("decay_sums"), 1)
            for g in range(2):
                if g == 1:
                    pe.wait_ge(S("fox_out_copied"), 1)
                for j in range(3):
                    h = 3 * g + j
                    hs = half_of(h)
                    q = proj[hs, QF0 + h // 2, META:CTX]
                    k = proj[hs, KF0 + h // 2, :]
                    for t, (c0, nk) in enumerate(((0, META + P), (META + P, CTX))):
                        pe.matmul(ps[:, 5 + j, c0:c0 + nk], q[:, t * P:(t + 1) * P], k[:, 0:nk],
                                  start=True, stop=False, skip_group_check=True)
                        mm = pe.matmul(ps[:, 5 + j, c0:c0 + nk],
                                       C("pick_head")[0:HEADS1, h * P:(h + 1) * P], negc[0:HEADS1, 0:nk],
                                       start=False, stop=True, skip_group_check=True)
                mm.then_inc(S("fox_scores"), 1)
                pe.wait_ge(S("fox_probs"), g + 1)
                if g == 1:
                    pe.wait_ge(S("fox_weights"), 1)
                for j in range(3):
                    row = s_row[:, j, :]
                    pe.transpose(ps[:, j, 0:P], row[:, META:META + P], C("ident"))
                    pe.transpose(ps[:, j, P:SEQ], row[:, P + 2 * META:2 * P + 2 * META], C("ident"))
                    pe.transpose(ps[:, j, SEQ:SEQ + P], row[:, 2 * P + 2 * META:3 * P + 2 * META], C("ident"))
                    pe.transpose(meta_dst(j)[:, 0:P], row[:, 0:META], C("ident"))
                    mm = pe.transpose(meta_dst(j)[:, P:SEQ],
                                      row[:, META + P:META + P + META], C("ident"))
                mm.then_inc(S("fox_turned"), 1)
                weighted_values(pT, pTm, g, 6, "fox_weights", "fox_out")

            for n, name in enumerate(("sb", "fox")):
                pe.wait_ge(S(f"{name}_head_squares"), 1)
                pe.matmul(ps[:, 2 * n, 0:512], C("head_ones"), hsq[:, 0:2, :].rearrange("p a b -> p (a b)"),
                          start=True, stop=True)
                pe.matmul(ps[:, 2 * n + 1, 0:SEQ], C("head_ones"), hsq[:, 2, :],
                          start=True, stop=True).then_inc(S(f"{name}_head_sums"), 1)
            pe.wait_ge(S("pool_diff"), 1)
            for t in range(2):
                mm = pe.matmul(ps[:, 4 + t, 0:SEQ], V("pool_w", t * P, P), pool_s[:, 0, t, META:CTX],
                               start=True, stop=True)
            mm.then_inc(S("pool_mixed"), 1)

            def output_product(layer, t0):
                for t in range(KT):
                    pe.wait_ge(S("w_split"), t0 + t + 1)
                    if t >= 4:
                        pe.wait_ge(S("out_added"), (layer - 1) * KT + t - 3)
                    tile_products(ps[:, t % 4, 0:SEQ], (t0 + t) % SLOTS, SEQ, f"mixer{layer}" if t == 0 else None)\
                        .then_inc(S("out_ready"), 1)

            output_product(1, T_OUT1)
            sum_squares("norm_ff1", SEQ)
            feed_forward(1, T_UP1)
            sum_squares("norm3", SEQ)

            sum_squares("norm4", SEQ)
            for t in range(TILES2):
                pe.wait_ge(S("w_split"), T_IN2 + t + 1)
                if t >= 2:
                    pe.wait_ge(S("proj2_copied_" + "ab"[t % 2]), (t - 2) // 2 + 1)
                tile_products(ps[:, t % 2, 0:SEQ], (T_IN2 + t) % SLOTS, SEQ,
                              "norm4" if t == 0 else None).then_inc(S("proj2_ready"), 1)

            pe.wait_ge(S("lora_w_ready"), 1)
            for f in range(PAIRS):
                pe.matmul(ps[:, f // 2, (f % 2) * SEQ:(f % 2 + 1) * SEQ], V("w2a2", f * P, P)[0:HD], lora_w,
                          start=True, stop=True)
            for f in range(PAIRS):
                mm = pe.matmul(ps[:, 2 + f // 2, (f % 2) * SEQ:(f % 2 + 1) * SEQ], V("w2a2", f * P, P)[HD:P],
                               proj[HD:P, WA0, 1:1 + SEQ], start=True, stop=True)
            mm.then_inc(S("lora_ready"), 1)
            pe.wait_ge(S("key_squares"), 1)
            for f in range(2):
                mm = pe.matmul(ps[:, 4 + f, :], C("head_ones"),
                               scr[:, 2 * f:2 * f + 2, :].rearrange("p a b -> p (a b)"), start=True, stop=True)
            mm.then_inc(S("key_sums"), 1)

            def tok(c):
                return slice(CHUNK * c, CHUNK * (c + 1))

            def halves():
                return ((h, slice(HD * h, HD * (h + 1))) for h in range(2))

            for c in range(CHUNKS):
                for j in range(PAIRS):
                    n = c * PAIRS + j
                    for h, hs in halves():
                        mm = pe.matmul(ps[hs, 6 + n // 8, (n % 8) * HD:(n % 8 + 1) * HD],
                                       proj[hs, V0 + j, 1 + CHUNK * c:1 + CHUNK * (c + 1)], C("ident")[hs, hs],
                                       start=True, stop=True)
            mm.then_inc(S("v_stacked"), 1)
            pe.wait_ge(S("rk_ready"), 1)
            for c in range(CHUNKS):
                for j in range(PAIRS):
                    for h, hs in halves():
                        mm = pe.matmul(ps[hs, 4, c * PAIRS + j:c * PAIRS + j + 1], scr[hs, j, tok(c)],
                                       C("ones")[hs, 0:1], start=True, stop=True)
            mm.then_inc(S("bonus_sums"), 1)

            for cp in range(0, CHUNKS, 2):
                pe.wait_ge(S("v_st_copied"), 1)
                pe.wait_ge(S("bonus_copied"), 1)
                for m in range(2):
                    c = cp + m
                    pe.wait_ge(S("packs_ready"), c + 1)
                    if c > 0:
                        pe.wait_ge(S("products_masked"), c)
                    if cp > 0:
                        pe.wait_ge(S("chunk_done"), c - 1)
                    for j in range(PAIRS):
                        both = ar[:, m, j, :, :].rearrange("p x c -> p (x c)")
                        pe.matmul(ps[:, j, 0:2 * P], bf[:, m, j, :], both, start=True, stop=True)
                        pe.matmul(ps[:, j, 2 * P:4 * P], kf[:, m, j, :], both, start=True, stop=True)
                        mm = pe.matmul(ps[:, 4 + m, j * P:(j + 1) * P], ar[:, m, j, 0, :], bf[:, m, j, :],
                                       start=True, stop=True)
                    mm.then_inc(S("products_ready"), 1)
                for level in range(1, LEVELS):
                    n = (cp // 2) * (LEVELS - 1) + level
                    for m in range(2):
                        if level == 1:
                            pe.wait_ge(S("products_masked"), cp + 2)
                        pe.wait_ge(S(f"joins_{m}"), n)
                        pe.wait_ge(S(f"inverse_grown_{m}"), n + cp // 2)
                        for j in range(PAIRS):
                            mm = pe.matmul(ps[:, 3 * m, j * P:(j + 1) * P], nl[:, m, j, :], xi[:, m, j, :],
                                           start=True, stop=True)
                        mm.then_inc(S(f"join_products_{m}"), 1)
                    for m in range(2):
                        pe.wait_ge(S(f"join_copied_{m}"), n)
                        for j in range(PAIRS):
                            if level < LEVELS - 1:
                                pe.matmul(ps[:, 3 * m + 1, j * P:(j + 1) * P], xt[:, m, j, :], pb[:, m, j, :],
                                          start=True, stop=True)
                            mm = pe.matmul(ps[:, 3 * m + 2, j * P:(j + 1) * P], pb[:, m, j, :], xt[:, m, j, :],
                                           start=True, stop=True)
                        mm.then_inc(S(f"inverse_terms_{m}"), 1)
                for m in range(2):
                    pe.wait_ge(S(f"inverse_grown_{m}"), (cp // 2 + 1) * LEVELS)
                    for j in range(PAIRS):
                        pe.transpose(ps[:, 3 * m, j * P:(j + 1) * P], bf[:, m, j, :], C("ident"))
                        mm = pe.transpose(ps[:, 3 * m + 1, j * P:(j + 1) * P], kf[:, m, j, :], C("ident"))
                    mm.then_inc(S("bk_turned"), 1)
                for m in range(2):
                    c = cp + m
                    if c == 0:
                        pe.wait_ge(S("state_zeroed"), 1)
                    else:
                        pe.wait_ge(S("chunk_done"), c)

                    def part(bank, j):
                        return ps[:, bank, j * HD:(j + 1) * HD]

                    kw = dict(stop=True, skip_group_check=True)
                    for j in range(PAIRS):
                        pe.matmul(part(6, j), ar[:, m, j, 0, :], state[:, j, :], start=(j == 0), **kw)
                        mm = pe.matmul(part(6, j), wt[:, m, j, 2 * P:3 * P], v_st[:, c * PAIRS + j, :],
                                       start=False, **kw)
                    mm.then_inc(S("rhs_ready"), 1)
                    pe.wait_ge(S("rhs_copied"), c + 1)
                    for j in range(PAIRS):
                        mm = pe.matmul(part(7, j), xt[:, m, j, :], rhs_sa[:, 0, j, :], start=(j == 0), **kw)
                    mm.then_inc(S("sa_ready"), 1)
                    for j in range(PAIRS):
                        pe.matmul(part(6, j), ar[:, m, j, 1, :], state[:, j, :], start=(j == 0), **kw)
                        pe.matmul(part(6, j), wt[:, m, j, 3 * P:4 * P], v_st[:, c * PAIRS + j, :],
                                  start=False, **kw)
                    pe.wait_ge(S("sa_copied"), c + 1)
                    pe.wait_ge(S("bk_copied"), c + 1)
                    for j in range(PAIRS):
                        pe.matmul(part(7, j), nl[:, m, j, :], v_st[:, c * PAIRS + j, :], start=(j == 0), **kw)
                        mm = pe.matmul(part(7, j), pb[:, m, j, :], rhs_sa[:, 1, j, :], start=False, **kw)
                    mm.then_inc(S("state_terms"), 1)
                    for j in range(PAIRS):
                        mm = pe.matmul(part(6, j), wt[:, m, j, P:2 * P], rhs_sa[:, 1, j, :], start=False, **kw)
                    mm.then_inc(S("y_terms"), 1)

            pe.wait_ge(S("chunk_done"), CHUNKS)
            for c in range(CHUNKS):
                for h, hs in halves():
                    mm = pe.matmul(ps[hs, c // 2, (c % 2) * 256:(c % 2 + 1) * 256], sdg[:, tok(c)],
                                   V("g2", h * 256, 256), start=True, stop=True)
            mm.then_inc(S("gates_ready"), 1)
            pe.wait_ge(S("rwkv_y"), 1)
            for c in range(CHUNKS):
                for j in range(PAIRS):
                    for h, hs in halves():
                        at = (j % 2) * SEQ + CHUNK * c
                        mm = pe.matmul(ps[hs, 2 + j // 2, at:at + CHUNK], y_all[hs, c * PAIRS + j, :],
                                       C("ident")[hs, hs], start=True, stop=True)
            mm.then_inc(S("rwkv_turned"), 1)

            def grp(g):
                return slice(HD * g, HD * (g + 1))

            for x in range(2):
                pe.wait_ge(S("blk_ready"), x + 1)
                for jp in range(CMP_PAIRS):
                    if jp % 8 == 0:
                        have(B_CMP + 2 * x + jp // 8)
                    b, r = B_CMP + 2 * x + jp // 8, jp % 8
                    w1 = ring[:, b % RING, r // 4, 2 * (r % 4):2 * (r % 4) + 2, :].rearrange("p a c -> p (a c)")
                    mm = pe.matmul(ps[0:32, 4 + x, 0:CMP_HIDDEN], blk[:, x, jp, :], w1,
                                   start=(jp == 0), stop=(jp == CMP_PAIRS - 1))
                    if jp % 8 == 7:
                        mm.then_inc(S("cmp_block_used"), 1)
            pe.wait_ge(S("gate_sigmoids"), 1)
            for t in range(2):
                pe.transpose(ps[:, 6, t * 24:(t + 1) * 24], gl_t[:, 0, t * P:(t + 1) * P], C("ident")[0:24, 0:24])
            for br, v in enumerate((VS1, VW1)):
                for t in range(2):
                    mm = pe.transpose(ps[:, 7, (2 * br + t) * P:(2 * br + t + 1) * P],
                                      proj[:, v, 1 + t * P:1 + (t + 1) * P], C("ident"))
            mm.then_inc(S("nsa_turned"), 1)
            pe.wait_ge(S("cmp_gelu"), 1)
            for x in range(2):
                for q in range(2):
                    mm = pe.transpose(ps[:, 0, (2 * x + q) * 32:(2 * x + q + 1) * 32],
                                      hid_c[:, x, q * P:(q + 1) * P], C("ident")[0:32, 0:32])
            mm.then_inc(S("cmp_turned"), 1)
            pe.wait_ge(S("hid_t_copied"), 1)
            for g in range(KVH):
                for q in range(2):
                    pe.matmul(ps[grp(g), 1, 0:CMP_PAD], V("cmp_w2k", q * HD, HD),
                              hid_t[:, 0, q, g * CMP_PAD:(g + 1) * CMP_PAD], start=(q == 0), stop=(q == 1))
            for g in range(KVH):
                for q in range(2):
                    mm = pe.matmul(ps[0:CMP_PAD, 2, g * HD:(g + 1) * HD], hid_t[:, 1, q, g * CMP_PAD:(g + 1) * CMP_PAD],
                                   V("cmp_w2v", q * HD, HD), start=(q == 0), stop=(q == 1))
            mm.then_inc(S("cmp_kv"), 1)
            pe.wait_ge(S("cmp_kv_copied"), 1)
            for g in range(KVH):
                for t in range(2):
                    for a in range(GQA):
                        at = (t * GQA + a) * CMP_PAD
                        pe.matmul(ps[:, 4 + g, at:at + CMP_PAD], proj[grp(g), Q0 + a, 1 + t * P:1 + (t + 1) * P],
                                  kcmp[grp(g), 0, 0:CMP_PAD], start=True, stop=True)
            pe.matmul(ps[:, 3, 0:P], C("cmp_spread")[0:CMP_PAD, :], vcmp[:, 0, :], start=True, stop=True)\
                .then_inc(S("cmp_scores"), 1)
            pe.wait_ge(S("cmp_probs"), 1)
            for t in range(2):
                mm = pe.transpose(ps[:, 6, t * P:(t + 1) * P], s_cmp[:, t].rearrange("p h n -> p (h n)"), C("ident"))
            mm.then_inc(S("cmp_probs_turned"), 1)

            for a in range(GQA):
                if a > 0:
                    pe.wait_ge(S("nsa_weights"), a)
                for br, k in enumerate((KS1, KW1)):
                    for g in range(KVH):
                        q = proj[grp(g), Q0 + a, 1:1 + SEQ]
                        kk = proj[grp(g), k, 1:1 + SEQ]
                        slot = 2 * br + g
                        pe.matmul(ps[:, slot, 0:P], q[:, 0:P], kk[:, 0:P], start=True, stop=True)
                        mm = pe.matmul(ps[:, slot, P:P + SEQ], q[:, P:SEQ], kk, start=True, stop=True)
                mm.then_inc(S("nsa_scores"), 1)
                pe.wait_ge(S("nsa_probs"), a + 1)
                for slot in range(4):
                    pe.transpose(ps[:, slot, 0:P], s_nsa[:, slot, 0:P], C("ident"))
                    pe.transpose(ps[:, slot, P:SEQ], s_nsa[:, slot, P:SEQ], C("ident"))
                    mm = pe.transpose(ps[:, slot, SEQ:SEQ + P], s_nsa[:, slot, SEQ:SEQ + P], C("ident"))
                mm.then_inc(S("nsa_probs_turned"), 1)
                if a == 0:
                    pe.wait_ge(S("pt_cmp_copied"), 1)
                if a >= 2:
                    pe.wait_ge(S("nsa_out_copied"), a - 1)
                dst = ps[:, 4 + a % 2, 0:SEQ]
                pe.matmul(dst, vown[:, a, :], pt_cmp[:].rearrange("p t q -> p (t q)"), start=True, stop=False,
                          skip_group_check=True)
                pe.wait_ge(S("nsa_weights"), a + 1)
                for br in range(2):
                    for g in range(KVH):
                        slot = 2 * br + g
                        w = pt_nsa[:, slot, :]
                        pe.matmul(dst[grp(g)], vt_nsa[:, br, 0, grp(g)], w[:, 0:SEQ], start=False, stop=False,
                                  skip_group_check=True)
                        mm = pe.matmul(dst[grp(g), P:SEQ], vt_nsa[:, br, 1, grp(g)], w[:, SEQ:SEQ + P],
                                       start=False, stop=(br == 1), skip_group_check=True)
                mm.then_inc(S("nsa_out"), 1)

            output_product(2, T_OUT2)
            sum_squares("norm_ff2", SEQ)
            feed_forward(2, T_UP2)
            sum_squares("norm6", SEQ)

        @block.scalar
        def _(act):
            step = Steps(act, "scalar_steps")
            act.preload_act_table_set("natural_log_exp_and_others")

            def norm_root(name, src_ready, n, src, tokens):
                act.wait_ge(S(src_ready), n)
                signal(act, act.activation(sq[:, :, 0:tokens], src, ACT.Square), "norm_squares", nth(name))
                act.wait_ge(S("norm_sums"), nth(name))
                step(act.activation(nrm[:, 0, 0:tokens], ps[:, 7, 0:tokens], ACT.Ln,
                                    bias=C("eps"), scale=1.0 / D))
                signal(act, act.activation(nrm[:, 1, 0:tokens], nrm[:, 0, 0:tokens], ACT.Exp, scale=-0.5),
                       "norm_root", nth(name))

            def split_hi(t, i=None, per_step=0, freed_by=None):
                b, half = place(t)
                step = 0 if i is None else i
                if half == 0 or t in (T_IN1,):
                    act.wait_ge(landed[b % RING], step * (16 * per_step // (2 * RING)) + 16 * (b // RING + 1))
                if t >= SLOTS:
                    name, n = freed(t - SLOTS)
                    act.wait_ge(S(name), n if i is None else i * (per_step // (2 if name in ("gate_ready", "up_ready")
                                                                              else 1)) + n)
                act.activation(w_hi[:, t % SLOTS].rearrange("p k c -> p (k c)"),
                               ring[:, b % RING, half].rearrange("p k c -> p (k c)"), ACT.Copy)\
                    .then_inc(S("w_rounded"), 1)

            def round_tiles(n, tokens, src):
                for k in range(KT):
                    if n is not None:
                        act.wait_ge(S("act_full"), n + k + 1)
                    act.activation(act_hi[:, k, 0:tokens], src[:, k, 0:tokens], ACT.Copy).then_inc(S("act_rounded"), 1)

            act.wait_ge(S("consts_landed"), 16)
            norm_root("norm1", "x_landed", 16, res[:, :, 0:CTX], CTX)
            for t in range(SLOTS):
                split_hi(T_IN1 + t)
            round_tiles(0, CTX, act_in)

            def scale_of(t):
                return HD ** -0.5 if QS0 <= t < QS0 + 3 or QF0 <= t < QF0 + 3 else 1.0

            for t in range(TILES1):
                if t % 2 == 0:
                    n = 6 if t == FL0 else P
                    act.wait_ge(S("proj1_ready"), t + 1)
                    act.activation(proj[0:n, t, :], ps[0:n, t % 2, 0:CTX], ACT.Copy, scale=scale_of(t))\
                        .then_inc(S("proj1_copied_a"), 1)
                split_hi(T_IN1 + t + SLOTS)
            act.wait_ge(S("forget_logit"), 1)
            step(act.activation(fl_t[0:6, 1, :], fl_t[0:6, 0, :], ACT.Abs))
            step(act.activation(fl_t[0:6, 1, :], fl_t[0:6, 1, :], ACT.Exp, scale=-1.0))
            signal(act, act.activation(fl_t[0:6, 1, :], fl_t[0:6, 1, :], ACT.Ln, bias=C("one", 6)),
                   "forget_log")

            for g in range(2):
                act.wait_ge(S("sb_logits"), g + 1)
                if g == 1:
                    act.wait_ge(S("sb_sums"), 1)
                zm = ps[0:META, 3:5, :].rearrange("p a b -> p (a b)")[:, 0:3 * SEQ]\
                    .rearrange("p (h q) -> p h q", h=3)
                z = ps[:, 0:3, 0:384]
                act.activation(sb_nl, z, ACT.Abs)
                step(act.activation(sb_nlm, zm, ACT.Abs))
                act.activation(sb_nl, sb_nl, ACT.Exp, scale=-1.0)
                step(act.activation(sb_nlm, sb_nlm, ACT.Exp, scale=-1.0))
                act.activation(sb_nl, sb_nl, ACT.Ln, bias=C("one"))
                signal(act, act.activation(sb_nlm, sb_nlm, ACT.Ln, bias=C("one", META)), "sb_softplus", g + 1)
                act.wait_ge(S("sb_sums"), g + 1)
                if g == 1:
                    act.wait_ge(S("sb_out"), 1)
                act.activation(pT, z, ACT.Exp)
                signal(act, act.activation(pTm, zm, ACT.Exp), "sb_weights", g + 1)

            act.wait_ge(S("sb_out_copied"), 2)
            signal(act, act.activation(hsq[:], heads_out[:, 3:6, :], ACT.Square), "sb_head_squares")

            for g in range(2):
                act.wait_ge(S("fox_max"), g + 1)
                for j in range(3):
                    for t, (c0, nk) in enumerate(((0, META + P), (META + P, CTX))):
                        ins = act.activation(s_row[:, j, c0:c0 + nk], s_row[:, j, c0:c0 + nk], ACT.Exp,
                                             bias=mx[:, t, j:j + 1], accum_out=den[:, t, j:j + 1])
                signal(act, ins, "fox_exps", g + 1)
                act.wait_ge(S("fox_turned"), g + 1)
                if g == 1:
                    act.wait_ge(S("fox_out"), 1)
                zm = ps[0:META, 3:5, :].rearrange("p a b -> p (a b)")[:, 0:3 * SEQ]\
                    .rearrange("p (h q) -> p h q", h=3)
                act.activation(pT, ps[:, 0:3, 0:384], ACT.Copy)
                signal(act, act.activation(pTm, zm, ACT.Copy), "fox_weights", g + 1)

            def head_root(name, n):
                act.wait_ge(S(f"{name}_head_sums"), 1)
                src = ps[:, 2 * n:2 * n + 2, :].rearrange("p a b -> p (a b)")[:, 0:3 * SEQ]
                dst = hr[:].rearrange("p a b -> p (a b)")
                step(act.activation(dst, src, ACT.Ln, bias=C("eps"), scale=1.0 / HD))
                signal(act, act.activation(dst, dst, ACT.Exp, scale=-0.5), f"{name}_head_root")

            head_root("sb", 0)
            act.wait_ge(S("fox_out_copied"), 2)
            signal(act, act.activation(hsq[:], heads_out[:, 0:3, :], ACT.Square), "fox_head_squares")
            act.wait_ge(S("sb_y"), 1)
            head_root("fox", 1)

            def feed_forward(layer, t_up):
                def one(j, i=None):
                    at = (layer - 1) * FT + j
                    step = 0 if i is None else i * UNROLL
                    m = j % 2
                    own = S("sigmoid_steps")
                    split_hi(t_up + 2 * j + SLOTS, i, 2 * UNROLL)
                    act.wait_ge(S("gate_kept"), step + (at + 1))
                    act.activation(sig[:, m, :], sig[:, m, :], ACT.Exp, scale=-1.0).then_inc(own, 1)
                    act.wait_ge(own, step * 2 + (2 * at + 1))
                    act.activation(sig[:, m, :], sig[:, m, :], ACT.Ln, bias=C("one")).then_inc(own, 1)
                    act.wait_ge(own, step * 2 + (2 * at + 2))
                    act.activation(sig[:, m, :], sig[:, m, :], ACT.Exp, scale=-1.0).then_inc(S("sigmoid"), 1)
                    split_hi(t_up + 2 * j + 1 + SLOTS, i, 2 * UNROLL)
                    act.wait_ge(S("hid_full"), step + (at + 1))
                    if i is None:
                        dst = hid_hi[:, j, :]
                    else:
                        dst = hid_hi[:, bass.ds(i * UNROLL + j, 1), :].rearrange("p o t -> p (o t)")
                    act.activation(dst, sig2[:, m, :], ACT.Copy).then_inc(S("hid_rounded"), 1)

                split_hi(t_up + SLOTS - 1)
                one(0)
                one(1)
                with act.Fori(0, (FT - 2) // UNROLL) as i:
                    for u in range(UNROLL):
                        one(2 + u, i)
                t_down = t_up + 2 * FT
                ahead = down_ahead(layer)
                split_hi(t_down + SLOTS)
                with act.Fori(0, (ahead - 1) // UNROLL) as i:
                    for u in range(UNROLL):
                        split_hi(t_down + SLOTS + 1 + u, i, UNROLL)
                for d in range(1 + (ahead - 1) // UNROLL * UNROLL, ahead):
                    split_hi(t_down + SLOTS + d)

            act.wait_ge(S("y1_ready"), 1)
            round_tiles(None, SEQ, yT)
            for t in range(KT - 1):
                split_hi(T_OUT1 + t + SLOTS)
            norm_root("norm_ff1", "out_added", KT, res[:, :, META:CTX], SEQ)
            round_tiles(KT, SEQ, act_in)
            feed_forward(1, T_UP1)
            norm_root("norm3", "down_added", KT, res[:, :, META:CTX], SEQ)

            norm_root("norm4", "norm3_ready", KT, res[:, :, META:CTX], SEQ)
            round_tiles(2 * KT, SEQ, act_in)
            split_hi(T_IN2 + SLOTS - 1)
            for t in range(TILES2):
                if t % 2 == 0:
                    n = 24 if t == GL0 else P
                    act.wait_ge(S("proj2_ready"), t + 1)
                    act.activation(proj[0:n, t, 1:1 + SEQ], ps[0:n, t % 2, 0:SEQ], ACT.Copy,
                                   scale=HD ** -0.5 if Q0 <= t < Q0 + 4 else 1.0).then_inc(S("proj2_copied_a"), 1)
                if t + SLOTS < TILES2:
                    split_hi(T_IN2 + t + SLOTS)

            def one_over_one_plus(dst):
                step(act.activation(dst, dst, ACT.Ln, bias=C("one", dst.shape[0])))
                return act.activation(dst, dst, ACT.Exp, scale=-1.0)

            act.wait_ge(S("shifted"), 1)
            step(act.activation(lora_w, lora_w, ACT.Exp, scale=2.0))
            signal(act, one_over_one_plus(lora_w), "lora_w_exp")
            step(act.activation(sdg, sdg, ACT.Exp, scale=-1.0))
            step(one_over_one_plus(sdg))
            act.wait_ge(S("key_scaled"), 1)
            signal(act, act.activation(scr, kkn, ACT.Square), "key_squares")
            for n, dst in enumerate((sigw, avec)):
                act.wait_ge(S("lora_biased"), n + 1)
                step(act.activation(dst, dst, ACT.Exp, scale=-1.0))
                signal(act, one_over_one_plus(dst), "decay_a_sigmoids", n + 1)
            act.wait_ge(S("key_sums_kept"), 1)
            step(act.activation(scr, scr, ACT.Ln))
            signal(act, act.activation(scr, scr, ACT.Exp, scale=-0.5), "key_root")
            act.wait_ge(S("decay_scanned"), 2)
            act.activation(p_exc, sigw, ACT.Exp, scale=-DECAY)
            act.activation(p_inc, lsum, ACT.Exp, scale=-DECAY)
            signal(act, act.activation(p_inv, lsum, ACT.Exp, scale=DECAY), "decay_powers")

            for cp in range(0, CHUNKS, 2):
                for level in range(1, LEVELS):
                    n = (cp // 2) * (LEVELS - 1) + level
                    for m in range(2):
                        if level == 1 and cp > 0:
                            act.wait_ge(S("chunk_done"), cp)
                        act.wait_ge(S(f"join_products_{m}"), n)
                        if level > 1:
                            act.wait_ge(S(f"inverse_terms_{m}"), n - 1)
                        act.activation(pb[:, m].rearrange("p j c -> p (j c)"), ps[:, 3 * m, :], ACT.Copy)\
                            .then_inc(S(f"join_copied_{m}"), 1)
                for m in range(2):
                    act.wait_ge(S("bk_turned"), cp + m + 1)
                    act.activation(pb[:, m].rearrange("p j c -> p (j c)"), ps[:, 3 * m, :], ACT.Copy)
                    signal(act, act.activation(nl[:, m].rearrange("p j c -> p (j c)"), ps[:, 3 * m + 1, :],
                                               ACT.Copy), "bk_copied", cp + m + 1)
                for m in range(2):
                    c = cp + m
                    act.wait_ge(S("rhs_ready"), c + 1)
                    signal(act, act.activation(rhs_sa[:, 0].rearrange("p j c -> p (j c)"), ps[:, 6, 0:256],
                                               ACT.Copy), "rhs_copied", c + 1)
                    act.wait_ge(S("sa_ready"), c + 1)
                    if c > 0:
                        act.wait_ge(S("y_terms"), c)
                    signal(act, act.activation(rhs_sa[:, 1].rearrange("p j c -> p (j c)"), ps[:, 7, 0:256],
                                               ACT.Copy), "sa_copied", c + 1)
            act.wait_ge(S("y_centred"), 1)
            signal(act, act.activation(scr.rearrange("p j t -> p (j t)"), y_all.rearrange("p n v -> p (n v)"),
                                       ACT.Square), "y_squares")
            act.wait_ge(S("y_vars"), 1)
            step(act.activation(small[:, 2], small[:, 2], ACT.Ln, bias=C("gn_eps"), scale=1.0 / HD))
            signal(act, act.activation(small[:, 2], small[:, 2], ACT.Exp, scale=-0.5), "y_root")
            act.wait_ge(S("rwkv_turned"), 1)
            signal(act, act.activation(yT[:, 0:4, :].rearrange("p j t -> p (j t)"),
                                       ps[:, 2:4, :].rearrange("p a b -> p (a b)"), ACT.Copy), "rwkv_out")

            act.wait_ge(S("blk_zeroed"), 1)
            for x, src in enumerate((KC0, VC0)):
                for g in range(KVH):
                    for q in range(2):
                        full = proj[HD * g:HD * (g + 1), src, 1 + q:1 + q + 255]
                        view = bass.AP(full.tensor, full.offset, [full.ap[0], [2, CMP_PAIRS], [CMP_STRIDE, N_CMP]])
                        ins = act.activation(blk[HD * q:HD * (q + 1), x, :, g * CMP_PAD:g * CMP_PAD + N_CMP],
                                             view, ACT.Copy)
                signal(act, ins, "blk_gathered", x + 1)
            step(act.activation(gl_t[:, 0], proj[0:24, GL0, 1:1 + SEQ], ACT.Exp, scale=-1.0))
            signal(act, one_over_one_plus(gl_t[:, 0]), "gate_sigmoids")
            act.wait_ge(S("cmp_gelu_arg"), 1)
            step(act.activation(gel[:], gel[:], ACT.Exp, scale=-GELU))
            signal(act, one_over_one_plus(gel[:]), "cmp_gelu_sigmoid")
            act.wait_ge(S("nsa_turned"), 1)
            act.activation(gates[:].rearrange("p t n -> p (t n)"), ps[:, 6, 0:48], ACT.Copy)
            signal(act, act.activation(vt_nsa[:].rearrange("p b t c -> p (b t c)"), ps[:, 7, :], ACT.Copy),
                   "nsa_values")
            act.wait_ge(S("cmp_turned"), 1)
            signal(act, act.activation(hid_t[:].rearrange("p a b c -> p (a b c)"), ps[:, 0, 0:128], ACT.Copy),
                   "hid_t_copied")
            act.wait_ge(S("cmp_kv"), 1)
            act.activation(kcmp[:, 0, 0:CMP_PAD], ps[:, 1, 0:CMP_PAD], ACT.Copy)
            signal(act, act.activation(vcmp[:, 0], ps[0:CMP_PAD, 2, 0:P], ACT.Copy), "cmp_kv_copied")
            act.wait_ge(S("cmp_centred"), 1)
            signal(act, act.activation(s_cmp[:], s_cmp[:], ACT.Exp), "cmp_exps")
            act.wait_ge(S("cmp_probs_turned"), 1)
            signal(act, act.activation(pt_cmp[:].rearrange("p t q -> p (t q)"), ps[:, 6, 0:SEQ], ACT.Copy),
                   "pt_cmp_copied")
            for a in range(GQA):
                act.wait_ge(S("nsa_max"), a + 1)
                for slot in range(4):
                    for t, (c0, n) in enumerate(((0, P), (P, SEQ))):
                        ins = act.activation(s_nsa[:, slot, c0:c0 + n], s_nsa[:, slot, c0:c0 + n], ACT.Exp,
                                             bias=mx_n[:, t, slot:slot + 1], accum_out=den_n[:, t, slot:slot + 1])
                signal(act, ins, "nsa_exps", a + 1)
                act.wait_ge(S("nsa_probs_turned"), a + 1)
                if a > 0:
                    act.wait_ge(S("nsa_out"), a)
                signal(act, act.activation(pt_nsa[:], ps[:, 0:4, 0:P + SEQ], ACT.Copy), "nsa_weights", a + 1)

            act.wait_ge(S("y2_ready"), 1)
            split_hi(T_OUT2)
            round_tiles(None, SEQ, yT)
            for t in range(1, SLOTS):
                split_hi(T_OUT2 + t)
            for t in range(KT - 1):
                split_hi(T_OUT2 + t + SLOTS)
            norm_root("norm_ff2", "out_added", 2 * KT, res[:, :, META:CTX], SEQ)
            round_tiles(3 * KT, SEQ, act_in)
            feed_forward(2, T_UP2)
            norm_root("norm6", "down_added", 2 * KT, res[:, :, META:CTX], SEQ)

        @block.vector
        def _(dve):
            step = Steps(dve, "vector_steps")

            def split_lo(t, i=None, per_step=0):
                b, half = place(t)
                dve.wait_ge(S("w_rounded"), t + 1 if i is None else i * per_step + (t + 1))
                dve.tensor_tensor(w_lo[:, t % SLOTS].rearrange("p k c -> p (k c)"),
                                  ring[:, b % RING, half].rearrange("p k c -> p (k c)"),
                                  w_hi[:, t % SLOTS].rearrange("p k c -> p (k c)").bitcast(F32), ALU.subtract)\
                    .then_inc(S("w_split"), 1)

            def rest(name, k, tokens, src):
                dve.wait_ge(S("act_rounded"), normed(name, k))
                dve.tensor_tensor(act_lo[:, k, 0:tokens], src[:, k, 0:tokens], act_hi[:, k, 0:tokens].bitcast(F32),
                                  ALU.subtract).then_inc(S("normed"), 1)

            def normalise(name, gain, t0, tokens):
                dve.wait_ge(S("norm_root"), nth(name))
                for k in range(KT + 1):
                    if k < KT:
                        dve.scalar_tensor_tensor(act_in[:, k, 0:tokens], res[:, k, t0:t0 + tokens],
                                                 V(gain, k), nrm[:, 1, 0:tokens], ALU.mult, ALU.mult)\
                            .then_inc(S("act_full"), 1)
                    if k > 0:
                        rest(name, k - 1, tokens, act_in)

            dve.wait_ge(S("vecs_landed"), 16)
            split_lo(T_IN1)
            split_lo(T_IN1 + 1)
            normalise("norm1", "norm1", 0, CTX)
            split_lo(T_IN1 + 2)
            split_lo(T_IN1 + 3)

            for t in range(TILES1):
                if t % 2:
                    dve.wait_ge(S("proj1_ready"), t + 1)
                    scale = HD ** -0.5 if QS0 <= t < QS0 + 3 or QF0 <= t < QF0 + 3 else 1.0
                    dve.tensor_scalar(proj[:, t, :], ps[:, t % 2, 0:CTX], scale, None, ALU.mult)\
                        .then_inc(S("proj1_copied_b"), 1)
                split_lo(T_IN1 + t + SLOTS)
            for kt, nt in enumerate((P, P, META)):
                dve.wait_ge(S("v1_turned"), kt + 1)
                src = ps[0:nt, 2 * kt:2 * kt + 2, :].rearrange("p a b -> p (a b)")[:, 0:12 * HD]
                dve.tensor_copy(vtok[0:nt, kt].rearrange("p h d -> p (h d)"), src).then_inc(S("v1_copied"), 1)

            dve.wait_ge(S("proj1_copied_a"), 11)
            signal(dve, dve.tensor_scalar(fl_t[0:6, 0, :], proj[0:6, FL0, :], V("forget_bias")[0:6], None, ALU.add),
                   "forget_logit")
            dve.wait_ge(S("forget_log"), 1)
            step(dve.scalar_tensor_tensor(fl_t[0:6, 0, :], fl_t[0:6, 0, :], 0.0, fl_t[0:6, 1, :],
                                          ALU.min, ALU.subtract))
            step(dve.memset(fl_t[0:6, 1, :], 1.0))
            signal(dve, dve.tensor_tensor_scan(negc[0:6, :], fl_t[0:6, 1, :], fl_t[0:6, 0, :], 0.0,
                                               ALU.mult, ALU.subtract), "decay_sums")

            dve.wait_ge(S("proj1_copied_b"), 10)
            u = proj[:, U0:U0 + 2, :]
            lo, hi = slice(0, HD), slice(HD, P)
            a, b = pool_s[:, 0], pool_s[:, 1]
            step(dve.tensor_tensor(a[:, :, 1:CTX], u[:, :, 1:CTX], u[:, :, 0:CTX - 1], ALU.add))
            step(dve.tensor_tensor(b[:, :, 3:CTX], a[:, :, 3:CTX], a[:, :, 1:CTX - 2], ALU.add))
            step(dve.scalar_tensor_tensor(a[lo, 0, META:CTX], a[lo, 0, META:CTX], 1 / 2, u[lo, 0, META:CTX],
                                          ALU.mult, ALU.subtract))
            step(dve.scalar_tensor_tensor(a[hi, 0, META:CTX], b[hi, 0, META:CTX], 1 / 4, u[hi, 0, META:CTX],
                                          ALU.mult, ALU.subtract))
            step(dve.tensor_tensor(a[:, 1, 7:CTX], b[:, 1, 7:CTX], b[:, 1, 3:CTX - 4], ALU.add))
            step(dve.tensor_tensor(b[:, 1, 15:CTX], a[:, 1, 15:CTX], a[:, 1, 7:CTX - 8], ALU.add))
            step(dve.scalar_tensor_tensor(a[lo, 1, META:CTX], a[lo, 1, META:CTX], 1 / 8, u[lo, 1, META:CTX],
                                          ALU.mult, ALU.subtract))
            signal(dve, dve.scalar_tensor_tensor(a[hi, 1, META:CTX], b[hi, 1, META:CTX], 1 / 16,
                                                 u[hi, 1, META:CTX], ALU.mult, ALU.subtract), "pool_diff")

            def copy_heads(g, t0, done):
                if g == 0:
                    dve.tensor_copy(heads_out[:, t0, :], ps[:, 5, 0:SEQ])
                    ins = dve.tensor_copy(heads_out[0:HD, t0 + 1, :], ps[0:HD, 6, 0:SEQ])
                else:
                    dve.tensor_copy(heads_out[HD:P, t0 + 1, :], ps[HD:P, 5, 0:SEQ])
                    ins = dve.tensor_copy(heads_out[:, t0 + 2, :], ps[:, 6, 0:SEQ])
                signal(dve, ins, done, g + 1)

            strict = C("strict").unsqueeze(1).to_broadcast([P, 3, P])
            for g in range(2):
                dve.wait_ge(S("sb_softplus"), g + 1)
                zm = ps[0:META, 3:5, :].rearrange("p a b -> p (a b)")[:, 0:3 * SEQ]\
                    .rearrange("p (h q) -> p h q", h=3)
                step(dve.scalar_tensor_tensor(sb_nl, ps[:, 0:3, 0:384], 0.0, sb_nl, ALU.max, ALU.add))
                dve.tensor_tensor(sb_nl[:, :, 0:P], sb_nl[:, :, 0:P], strict, ALU.mult)
                dve.tensor_tensor(sb_nl[:, :, SEQ:SEQ + P], sb_nl[:, :, SEQ:SEQ + P], strict, ALU.mult)
                signal(dve, dve.scalar_tensor_tensor(sb_nlm, zm, 0.0, sb_nlm, ALU.max, ALU.add),
                       "sb_logs", g + 1)
                dve.wait_ge(S("sb_out"), g + 1)
                copy_heads(g, 3, "sb_out_copied")

            causal = C("causal1").unsqueeze(1).to_broadcast([P, 3, META + P + CTX])
            for g in range(2):
                dve.wait_ge(S("fox_scores"), g + 1)
                step(dve.tensor_tensor(s_row, ps[:, 5:8, 0:META + P + CTX], causal, ALU.add))
                dve.tensor_reduce(mx[:, 0, :], s_row[:, :, 0:META + P], AX.X, ALU.max, negate=True)
                signal(dve, dve.tensor_reduce(mx[:, 1, :], s_row[:, :, META + P:META + P + CTX], AX.X, ALU.max,
                                              negate=True), "fox_max", g + 1)
                dve.wait_ge(S("fox_exps"), g + 1)
                step(dve.reciprocal(rden, den))
                for j in range(3):
                    for t, (c0, nk) in enumerate(((0, META + P), (META + P, CTX))):
                        ins = dve.tensor_scalar(s_row[:, j, c0:c0 + nk], s_row[:, j, c0:c0 + nk],
                                                rden[:, t, j:j + 1], None, ALU.mult)
                signal(dve, ins, "fox_probs", g + 1)
                dve.wait_ge(S("fox_out"), g + 1)
                copy_heads(g, 0, "fox_out_copied")

            for name, t0, y0, gain in (("sb", 3, 5, "sb_gain"), ("fox", 0, 2, "fox_gain")):
                dve.wait_ge(S(f"{name}_head_root"), 1)
                for t in range(3):
                    ins = dve.scalar_tensor_tensor(yT[:, y0 + t, :], heads_out[:, t0 + t, :], V(gain, t),
                                                   hr[:, t, :], ALU.mult, ALU.mult)
                signal(dve, ins, f"{name}_y")
            dve.wait_ge(S("pool_mixed"), 1)
            for t in range(2):
                ins = dve.tensor_scalar(yT[:, t, :], ps[:, 4 + t, 0:SEQ], V("pool_scale", t), None, ALU.mult)
            signal(dve, ins, "y1_ready")

            def mixer_output(layer, t_out):
                if layer == 2:
                    split_lo(t_out)
                for k in range(KT):
                    rest(f"mixer{layer}", k, SEQ, yT)
                if layer == 2:
                    for t in range(1, SLOTS):
                        split_lo(t_out + t)
                for t in range(KT):
                    dve.wait_ge(S("out_ready"), (layer - 1) * KT + t + 1)
                    dve.tensor_tensor(res[:, t, META:CTX], ps[:, t % 4, 0:SEQ], res[:, t, META:CTX], ALU.add)\
                        .then_inc(S("out_added"), 1)
                    if t < KT - 1:
                        split_lo(t_out + t + SLOTS)

            def feed_forward(layer, t_up):
                def one(j, i=None):
                    at = (layer - 1) * FT + j
                    step = 0 if i is None else i * UNROLL
                    m = j % 2
                    dve.wait_ge(S("gate_ready"), step + (at + 1))
                    dve.tensor_scalar(sig[:, m, :], ps[:, 2 * m, 0:SEQ], -EXP_MAX, None, ALU.max)\
                        .then_inc(S("gate_kept"), 1)
                    split_lo(t_up + 2 * j + SLOTS, i, 2 * UNROLL)
                    dve.wait_ge(S("sigmoid"), step + (at + 1))
                    if at >= 2:
                        dve.wait_ge(S("hid_ready"), step + (at - 1))
                    dve.tensor_tensor(sig2[:, m, :], ps[:, 2 * m, 0:SEQ], sig[:, m, :], ALU.mult)\
                        .then_inc(S("silu_steps"), 1)
                    dve.wait_ge(S("up_ready"), step + (at + 1))
                    dve.wait_ge(S("silu_steps"), step + (at + 1))
                    dve.tensor_tensor(sig2[:, m, :], ps[:, 2 * m + 1, 0:SEQ], sig2[:, m, :], ALU.mult)\
                        .then_inc(S("hid_full"), 1)
                    split_lo(t_up + 2 * j + 1 + SLOTS, i, 2 * UNROLL)
                    if i is None:
                        hi, lo = hid_hi[:, j, :], hid_lo[:, j, :]
                    else:
                        hi, lo = (x[:, bass.ds(i * UNROLL + j, 1), :].rearrange("p o t -> p (o t)")
                                  for x in (hid_hi, hid_lo))
                    dve.wait_ge(S("hid_rounded"), step + (at + 1))
                    dve.tensor_tensor(lo, sig2[:, m, :], hi.bitcast(F32), ALU.subtract).then_inc(S("hid_ready"), 1)

                split_lo(t_up + SLOTS - 1)
                one(0)
                one(1)
                with dve.Fori(0, (FT - 2) // UNROLL) as i:
                    for u in range(UNROLL):
                        one(2 + u, i)
                t_down = t_up + 2 * FT
                ahead = down_ahead(layer)
                split_lo(t_down + SLOTS)
                with dve.Fori(0, (ahead - 1) // UNROLL) as i:
                    for u in range(UNROLL):
                        split_lo(t_down + SLOTS + 1 + u, i, UNROLL)
                for d in range(1 + (ahead - 1) // UNROLL * UNROLL, ahead):
                    split_lo(t_down + SLOTS + d)

            def add_down(layer):
                dve.wait_ge(S("down_ready"), (layer - 1) * KT + KT)
                for t in range(KT):
                    dve.tensor_tensor(res[:, t, META:CTX], ps[:, 4 + t // 2, (t % 2) * SEQ:(t % 2 + 1) * SEQ],
                                      res[:, t, META:CTX], ALU.add).then_inc(S("down_added"), 1)

            mixer_output(1, T_OUT1)
            normalise("norm_ff1", "norm2", META, SEQ)
            feed_forward(1, T_UP1)
            add_down(1)
            dve.wait_ge(S("norm_root"), nth("norm3"))
            for k in range(KT):
                dve.scalar_tensor_tensor(res[:, k, META:CTX], res[:, k, META:CTX], V("norm3", k), nrm[:, 1, 0:SEQ],
                                         ALU.mult, ALU.mult).then_inc(S("norm3_ready"), 1)

            normalise("norm4", "norm4", META, SEQ)
            dve.wait_ge(S("normed"), normed("norm4", KT - 1))
            step(dve.memset(proj[:, 0:SHIFTED, 0:1], 0.0))
            split_lo(T_IN2 + SLOTS - 1)
            for t in range(TILES2):
                if t % 2:
                    dve.wait_ge(S("proj2_ready"), t + 1)
                    scale = HD ** -0.5 if Q0 <= t < Q0 + 4 else 1.0
                    dve.tensor_scalar(proj[:, t, 1:1 + SEQ], ps[:, t % 2, 0:SEQ], scale, None, ALU.mult)\
                        .then_inc(S("proj2_copied_b"), 1)
                if t + SLOTS < TILES2:
                    split_lo(T_IN2 + t + SLOTS)
            dve.wait_ge(S("proj2_copied_a"), 13)
            dve.wait_ge(S("proj2_copied_b"), 12)
            dve.wait_ge(S("norm_root"), nth("norm4"))
            diff = flat[:, 0:SHIFTED * SEQ].rearrange("p (a b) -> p a b", a=SHIFTED)
            step(dve.tensor_tensor(diff, proj[:, 0:SHIFTED, 0:SEQ], proj[:, 0:SHIFTED, 1:1 + SEQ], ALU.subtract))
            for t in range(SHIFTED):
                ins = dve.scalar_tensor_tensor(proj[:, t, 1:1 + SEQ], diff[:, t, :], V("mu", t),
                                               proj[:, t, 1:1 + SEQ], ALU.mult, ALU.add)
            step(ins)
            dve.tensor_scalar(lora_w, proj[0:HD, WA0, 1:1 + SEQ], EXP_MAX / 2, None, ALU.min)
            signal(dve, dve.tensor_scalar(sdg, proj[:, G0, 1:1 + SEQ], -EXP_MAX, None, ALU.max), "shifted")

            def per_pair(name):
                return V(name, 0, PAIRS).unsqueeze(2).to_broadcast([P, PAIRS, SEQ])

            rv, kv = proj[:, R0:R0 + 4, 1:1 + SEQ], proj[:, K0:K0 + 4, 1:1 + SEQ]
            signal(dve, dve.tensor_tensor(kkn, kv, per_pair("k_k"), ALU.mult), "key_scaled")
            dve.wait_ge(S("lora_w_exp"), 1)
            signal(dve, dve.tensor_scalar(lora_w, lora_w, -2.0, 1.0, ALU.mult, ALU.add), "lora_w_ready")
            dve.wait_ge(S("v_stacked"), 1)
            signal(dve, dve.tensor_copy(v_st.rearrange("p n v -> p (n v)"),
                                        ps[:, 6:8, :].rearrange("p a b -> p (a b)")), "v_st_copied")
            dve.wait_ge(S("key_sums"), 1)
            signal(dve, dve.tensor_scalar(scr.rearrange("p j t -> p (j t)"),
                                          ps[:, 4:6, :].rearrange("p a b -> p (a b)"), 1e-24, None, ALU.max),
                   "key_sums_kept")
            dve.wait_ge(S("lora_ready"), 1)
            for n, (name, dst) in enumerate((("w0", sigw), ("a0", avec))):
                for f in range(PAIRS):
                    ins = dve.tensor_scalar(dst[:, f, :],
                                            ps[:, 2 * n + f // 2, (f % 2) * SEQ:(f % 2 + 1) * SEQ],
                                            V(name, f), -EXP_MAX, ALU.add, ALU.max)
                signal(dve, ins, "lora_biased", n + 1)
            dve.wait_ge(S("reset_ready"), 1)
            dve.wait_ge(S("decay_a_sigmoids"), 1)
            one = "p j t -> p (j t)"
            signal(dve, dve.tensor_tensor_scan(lsum.rearrange(one), reset.rearrange(one), sigw.rearrange(one), 0.0,
                                               ALU.mult, ALU.add), "decay_scanned", 1)
            signal(dve, dve.tensor_tensor(sigw, lsum, sigw, ALU.subtract), "decay_scanned", 2)
            dve.wait_ge(S("key_root"), 1)
            step(dve.scalar_tensor_tensor(kkn, kkn, -1.0, scr, ALU.mult, ALU.mult))
            dve.wait_ge(S("decay_a_sigmoids"), 2)
            step(dve.scalar_tensor_tensor(scr, avec, -1.0, kv, ALU.add, ALU.mult))
            step(dve.tensor_tensor(scr, scr, per_pair("k_a"), ALU.mult))
            step(dve.tensor_tensor(kv, kv, scr, ALU.add))
            step(dve.scalar_tensor_tensor(avec, kkn, -1.0, avec, ALU.mult, ALU.mult))
            step(dve.tensor_tensor(scr, rv, kv, ALU.mult))
            signal(dve, dve.tensor_tensor(scr, scr, per_pair("r_k"), ALU.mult), "rk_ready")
            dve.wait_ge(S("bonus_sums"), 1)
            signal(dve, dve.tensor_copy(small[:, 0], ps[:, 4, 0:PACKS]), "bonus_copied")
            dve.wait_ge(S("decay_powers"), 1)
            dve.wait_ge(S("packs_zeroed"), 1)

            for cp in range(0, CHUNKS, 2):
                for m in range(2):
                    c = cp + m
                    if cp > 0:
                        dve.wait_ge(S("chunk_done"), c - 1)
                        dve.wait_ge(S("y_kept"), c - 1)
                    ts = slice(c * CHUNK, (c + 1) * CHUNK)
                    for dst, x, y in ((ar[:, m, :, 0], kkn, p_exc), (ar[:, m, :, 1], rv, p_inc),
                                      (bf[:, m], avec, p_inv), (kf[:, m], kv, p_inv)):
                        for h in range(2):
                            hs = slice(HD * h, HD * (h + 1))
                            ins = dve.tensor_tensor(dst[hs, :, CHUNK * h:CHUNK * (h + 1)], x[hs, :, ts],
                                                    y[hs, :, ts], ALU.mult)
                    signal(dve, ins, "packs_ready", c + 1)
                for m in range(2):
                    c = cp + m
                    dve.wait_ge(S("products_ready"), c + 1)
                    for j in range(PAIRS):
                        dve.tensor_tensor(wt[:, m, j], ps[:, j, :], C("pack_masks"), ALU.mult)
                    join0 = C("join")[:, 0:P].unsqueeze(1).to_broadcast([P, PAIRS, P])
                    join0_t = C("join0_t").unsqueeze(1).to_broadcast([P, PAIRS, P])
                    eye = C("ident").unsqueeze(1).to_broadcast([P, PAIRS, P])
                    ab = ps[:, 4 + m, :].rearrange("p (j c) -> p j c", j=PAIRS)
                    signal(dve, dve.tensor_tensor(xi[:, m], ab, join0_t, ALU.mult), "products_masked", c + 1)
                    step(dve.tensor_tensor(xt[:, m], wt[:, m, :, 0:P], join0, ALU.mult))
                    step(dve.tensor_tensor(xt[:, m], xt[:, m], eye, ALU.add))
                    signal(dve, dve.tensor_tensor(xi[:, m], xi[:, m], eye, ALU.add),
                           f"inverse_grown_{m}", (cp // 2) * LEVELS + 1)
                for level in range(1, LEVELS):
                    n = (cp // 2) * (LEVELS - 1) + level
                    for m in range(2):
                        dve.wait_ge(S(f"inverse_terms_{m}"), n)
                        flat2 = "p j c -> p (j c)"
                        if level < LEVELS - 1:
                            dve.tensor_tensor(xi[:, m].rearrange(flat2), ps[:, 3 * m + 1, :],
                                              xi[:, m].rearrange(flat2), ALU.add)
                        signal(dve, dve.tensor_tensor(xt[:, m].rearrange(flat2), ps[:, 3 * m + 2, :],
                                                      xt[:, m].rearrange(flat2), ALU.add),
                               f"inverse_grown_{m}", (cp // 2) * LEVELS + level + 1)
                for m in range(2):
                    c = cp + m
                    dve.wait_ge(S("state_terms"), c + 1)
                    st = "p j v -> p (j v)"
                    step(dve.tensor_tensor(state[:].rearrange(st), ps[:, 7, 0:256], state[:].rearrange(st), ALU.add))
                    end = p_inc[:, :, (c + 1) * CHUNK - 1:(c + 1) * CHUNK].to_broadcast([P, PAIRS, HD])
                    dve.wait_ge(S("y_terms"), c + 1)
                    signal(dve, dve.tensor_copy(y_all[:, c * PAIRS:(c + 1) * PAIRS, :].rearrange("p n v -> p (n v)"),
                                                ps[:, 6, 0:256]), "y_kept", c + 1)
                    signal(dve, dve.tensor_tensor(state[:], state[:], end, ALU.mult), "chunk_done", c + 1)

            def each(name):
                return small[:, name].unsqueeze(2).to_broadcast([P, PACKS, HD])

            def table(name):
                at, w = VEC_AT[name]
                return vec[:, at:at + w].unsqueeze(1).to_broadcast([P, CHUNKS, PAIRS * HD])

            by_chunk = y_all.rearrange("p (c j) v -> p c (j v)", c=CHUNKS)
            step(dve.tensor_reduce(small[:, 1], y_all, AX.X, ALU.add))
            step(dve.tensor_scalar(small[:, 1], small[:, 1], 1.0 / HD, None, ALU.mult))
            signal(dve, dve.tensor_tensor(y_all, y_all, each(1), ALU.subtract), "y_centred")
            dve.wait_ge(S("y_squares"), 1)
            signal(dve, dve.tensor_reduce(small[:, 2], scr.rearrange("p j t -> p (j t)")
                                          .rearrange("p (n v) -> p n v", n=PACKS), AX.X, ALU.add), "y_vars")
            dve.wait_ge(S("y_root"), 1)
            step(dve.tensor_tensor(y_all, y_all, each(2), ALU.mult))
            step(dve.tensor_tensor(by_chunk, by_chunk, table("lnx_w"), ALU.mult))
            step(dve.tensor_tensor(by_chunk, by_chunk, table("lnx_b"), ALU.add))
            step(dve.tensor_tensor(v_st, v_st, each(0), ALU.mult))
            step(dve.tensor_tensor(y_all, y_all, v_st, ALU.add))
            dve.wait_ge(S("gates_ready"), 1)
            signal(dve, dve.tensor_tensor(y_all.rearrange("p n v -> p (n v)"),
                                          ps[:, 0:2, :].rearrange("p a b -> p (a b)"),
                                          y_all.rearrange("p n v -> p (n v)"), ALU.mult), "rwkv_y")

            step(dve.memset(blk[:], 0.0))
            signal(dve, dve.memset(blk[:], 0.0), "blk_zeroed")
            for x in range(2):
                dve.wait_ge(S("blk_gathered"), x + 1)
                pe_add = V(("pe_k", "pe_v")[x], 0, CMP_PAIRS).unsqueeze(2).to_broadcast([P, CMP_PAIRS, 32])
                signal(dve, dve.tensor_tensor(blk[:, x], blk[:, x], pe_add, ALU.add), "blk_ready", x + 1)
            dve.wait_ge(S("cmp_block_used"), 4)
            h2 = ps[0:32, 4:6, 0:CMP_HIDDEN]
            step(dve.tensor_copy(hid_c[:], h2))
            step(dve.tensor_tensor(gel[:], hid_c[:], hid_c[:], ALU.mult))
            step(dve.tensor_scalar(gel[:], gel[:], 0.044715, 1.0, ALU.mult, ALU.add))
            step(dve.tensor_tensor(gel[:], gel[:], hid_c[:], ALU.mult))
            signal(dve, dve.tensor_scalar(gel[:], gel[:], -EXP_MAX / GELU, None, ALU.max), "cmp_gelu_arg")
            dve.wait_ge(S("cmp_gelu_sigmoid"), 1)
            signal(dve, dve.tensor_tensor(hid_c[:], hid_c[:], gel[:], ALU.mult), "cmp_gelu")
            dve.wait_ge(S("cmp_scores"), 1)
            bias = C("cmp_bias").rearrange("p (t h n) -> p t h n", t=2, h=NQH)
            for g in range(KVH):
                dve.tensor_tensor(s_cmp[:, :, g * GQA:(g + 1) * GQA, :],
                                  ps[:, 4 + g, 0:2 * GQA * CMP_PAD].rearrange("p (t h n) -> p t h n", t=2, h=GQA),
                                  bias[:, :, g * GQA:(g + 1) * GQA, :], ALU.add)
            own = C("cmp_own").rearrange("p (a c) -> p a c", a=GQA)
            vrep = vown_src
            step(dve.tensor_copy(vrep, ps[:, 3, 0:P]))
            step(dve.tensor_tensor(vown[:], own, vrep.unsqueeze(1).to_broadcast([P, GQA, P]), ALU.mult))
            flat_s = s_cmp[:].rearrange("p t h n -> p (t h) n")
            flat_m = mx_c[:].rearrange("p t h -> p (t h)")
            flat_d = den_c[:].rearrange("p t h -> p (t h)")
            wide = [P, 2 * NQH, CMP_PAD]
            step(dve.tensor_reduce(flat_m, flat_s, AX.X, ALU.max))
            signal(dve, dve.tensor_tensor(flat_s, flat_s, flat_m.unsqueeze(2).to_broadcast(wide), ALU.subtract),
                   "cmp_centred")
            dve.wait_ge(S("cmp_exps"), 1)
            step(dve.tensor_reduce(flat_d, flat_s, AX.X, ALU.add))
            step(dve.reciprocal(flat_d, flat_d))
            dve.wait_ge(S("nsa_values"), 1)
            gv = gates[:].rearrange("p t (h b) -> p t h b", b=3)
            step(dve.tensor_tensor(den_c[:], den_c[:], gv[:, :, :, 0], ALU.mult))
            step(dve.tensor_tensor(den_c[:], den_c[:], C("cmp_any").unsqueeze(2).to_broadcast([P, 2, NQH]),
                                   ALU.mult))
            signal(dve, dve.tensor_tensor(flat_s, flat_s, flat_d.unsqueeze(2).to_broadcast(wide), ALU.mult),
                   "cmp_probs")
            alibi = C("alibi").rearrange("p (g a k) -> p g a k", g=KVH, a=GQA)
            for a in range(GQA):
                dve.wait_ge(S("nsa_scores"), a + 1)
                if a > 0:
                    dve.wait_ge(S("nsa_probs_turned"), a)
                sv = s_nsa[:].rearrange("p (b g) k -> p b g k", b=2)
                pv = ps[:, 0:4, 0:P + SEQ].rearrange("p (b g) k -> p b g k", b=2)
                for br in range(2):
                    dve.tensor_tensor(sv[:, br, :, 0:P], pv[:, br, :, 0:P], alibi[:, :, a, P:SEQ], ALU.add)
                    ins = dve.tensor_tensor(sv[:, br, :, P:P + SEQ], pv[:, br, :, P:P + SEQ], alibi[:, :, a, :],
                                            ALU.add)
                step(ins)
                dve.tensor_reduce(mx_n[:, 0, :], s_nsa[:, :, 0:P], AX.X, ALU.max, negate=True)
                signal(dve, dve.tensor_reduce(mx_n[:, 1, :], s_nsa[:, :, P:P + SEQ], AX.X, ALU.max, negate=True),
                       "nsa_max", a + 1)
                dve.wait_ge(S("nsa_exps"), a + 1)
                step(dve.reciprocal(den_n[:], den_n[:]))
                for g in range(KVH):
                    ins = dve.tensor_tensor(den_n[:].rearrange("p t (b g) -> p t b g", b=2)[:, :, :, g],
                                            den_n[:].rearrange("p t (b g) -> p t b g", b=2)[:, :, :, g],
                                            gv[:, :, g * GQA + a, 1:3], ALU.mult)
                step(ins)
                for slot in range(4):
                    for t, (c0, n) in enumerate(((0, P), (P, SEQ))):
                        ins = dve.tensor_scalar(s_nsa[:, slot, c0:c0 + n], s_nsa[:, slot, c0:c0 + n],
                                                den_n[:, t, slot:slot + 1], None, ALU.mult)
                signal(dve, ins, "nsa_probs", a + 1)
                dve.wait_ge(S("nsa_out"), a + 1)
                signal(dve, dve.tensor_copy(yT[:, 4 + a, :], ps[:, 4 + a % 2, 0:SEQ]), "nsa_out_copied", a + 1)
            dve.wait_ge(S("rwkv_out"), 1)
            signal(dve, dve.memset(small[:, 7], 0.0), "y2_ready")

            mixer_output(2, T_OUT2)
            normalise("norm_ff2", "norm5", META, SEQ)
            feed_forward(2, T_UP2)
            add_down(2)
            dve.wait_ge(S("norm_root"), nth("norm6"))
            for k in range(KT):
                dve.scalar_tensor_tensor(yT[:, k, :], res[:, k, META:CTX], V("norm6", k), nrm[:, 1, 0:SEQ],
                                         ALU.mult, ALU.mult).then_inc(S("final_ready"), 1)




def tiles_in(w):
    n = w.shape[1]
    t = -(-n // P)
    w = np.concatenate([w, np.zeros((w.shape[0], t * P - n), w.dtype)], 1)
    return w.reshape(KT, P, t, P).transpose(2, 1, 0, 3).reshape(t, P, TILE)


def to_blocks(tiles):
    if len(tiles) % 2:
        tiles = np.concatenate([tiles, np.zeros_like(tiles[:1])])
    return tiles.reshape(-1, 2, P, TILE).transpose(0, 2, 1, 3).reshape(-1, P, BLOCK)


def ffn_blocks(gate, up, down):
    g, u = tiles_in(gate), tiles_in(up)
    both = np.stack([g, u], 1).reshape(-1, P, TILE)
    return [to_blocks(both), to_blocks(down.reshape(FT, P, TILE))]


def cols(v):
    return v.reshape(-1, P).T


def layout(i):
    f = np.float32
    i = {k: np.asarray(v) for k, v in i.items()}
    w = i["w_in"][0]
    u, qf, kf, vf, fl, qs, ks, vs = np.split(w, np.cumsum([256, 384, 384, 384, 6, 384, 384]), 1)
    w1 = np.concatenate([ks, qs, vs, vf, kf, qf, u, fl], 1)
    stream = [to_blocks(tiles_in(w1)), to_blocks(tiles_in(i["w_out"][0]))]
    stream += ffn_blocks(i["w_gate"][0], i["w_up"][0], i["w_down"][0])
    h = np.concatenate([i["meta_tokens"], i["x"][0]], 0)
    xT = h.T.reshape(KT, P, CTX).transpose(1, 0, 2).reshape(P, -1)
    vecs = {
        "norm1": cols(i["norm1"][0]), "norm2": cols(i["norm2"][0]), "norm3": cols(i["final_norm"]),
        "fox_gain": cols(i["fox_out_gain"][0]), "sb_gain": cols(i["sb_out_gain"][0]),
        "pool_scale": cols(i["pool_scale"][0]),
    }
    fb = np.zeros((P, 1), f)
    fb[0:6, 0] = i["forget_bias"][0]
    vecs["forget_bias"] = fb
    pw = np.zeros((P, 2, P), f)
    for g in range(4):
        r = HD * (g % 2)
        pw[r:r + HD, g // 2, r:r + HD] = i["pool_w"][0, g]
    vecs["pool_w"] = pw.reshape(P, -1)
    w = i["w_in_2"][0]
    rw, nsa = w[:, 0:SHIFTED * P], w[:, SHIFTED * P:]
    q, kvs, gl = nsa[:, 0:512], nsa[:, 512:1280], nsa[:, 1280:]
    q = q.reshape(D, KVH, GQA, HD).transpose(0, 2, 1, 3).reshape(D, -1)
    stream.append(to_blocks(tiles_in(np.concatenate([rw, q, kvs, gl], 1))))
    for n in ("nsa_cmp_k_w1_2", "nsa_cmp_v_w1_2"):
        stream.append(to_blocks(i[n][0].reshape(4, 4, P, CMP_HIDDEN).transpose(0, 2, 1, 3).reshape(4, P, TILE)))
    wo = i["w_out_2"][0]
    wn = wo[512:].reshape(KVH, GQA, HD, D).transpose(1, 0, 2, 3).reshape(512, D)
    stream.append(to_blocks(tiles_in(np.concatenate([wo[0:512], wn], 0))))
    stream += ffn_blocks(i["ffn_w_gate_2"][0], i["ffn_w_up_2"][0], i["ffn_w_down_2"][0])

    def by_head(v):
        return np.repeat(v.reshape(PAIRS, 2, HD).transpose(1, 0, 2).reshape(2, PAIRS * HD), CHUNK, 0)

    vecs |= {
        "norm4": cols(i["norm1_g_2"][0]), "norm5": cols(i["norm2_g_2"][0]), "norm6": cols(i["norm_f_g_2"]),
        "mu": cols(i["mu_shift_2"][0]), "w0": cols(i["rwkv_w0_2"][0]), "a0": cols(i["rwkv_a0_2"][0]),
        "k_k": cols(i["rwkv_k_k_2"][0]), "k_a": cols(i["rwkv_k_a_2"][0]), "r_k": cols(i["rwkv_r_k_2"][0]),
        "w2a2": np.concatenate([i["rwkv_w2_2"][0], i["rwkv_a2_2"][0]], 0),
        "g2": i["rwkv_g2_2"][0].reshape(P, PAIRS, 2, HD).transpose(0, 2, 1, 3).reshape(P, -1),
        "lnx_w": by_head(i["rwkv_lnx_w_2"][0]), "lnx_b": by_head(i["rwkv_lnx_b_2"][0]),
        "pe_k": i["nsa_pe_k_2"][0].reshape(CMP_PAIRS, P).T, "pe_v": i["nsa_pe_v_2"][0].reshape(CMP_PAIRS, P).T,
        "cmp_w2k": i["nsa_cmp_k_w2_2"][0].reshape(2, P, HD).transpose(1, 0, 2).reshape(P, -1),
        "cmp_w2v": i["nsa_cmp_v_w2_2"][0].reshape(2, P, HD).transpose(1, 0, 2).reshape(P, -1),
    }
    return {
        "xT": np.ascontiguousarray(xT), "weights": np.ascontiguousarray(np.concatenate(stream)),
        "consts": np.concatenate(list(constant_tables().values()), 1),
        "vecs": np.concatenate([vecs[k] for k in VEC_WIDTHS], 1),
    }


def kernel(**inputs):
    import concourse.bacc as bacc
    from concourse.bass_utils import run_bass_kernel_spmd

    nc = bacc.Bacc("TRN2", target_bir_lowering=False, num_devices=1)
    arrays, aps = {}, []
    for name, a in layout(inputs).items():
        a = np.ascontiguousarray(a)
        arrays[f"in_{name}"] = a
        aps.append(nc.dram_tensor(f"in_{name}", a.shape, mybir.dt.from_np(a.dtype), kind="ExternalInput").ap())
    out = nc.dram_tensor("out_features", (P, KT * SEQ), F32, kind="ExternalOutput").ap()
    build_program(nc, *aps, out)
    got = run_bass_kernel_spmd(nc, [arrays], core_ids=[0]).results[0]["out_features"]
    return got.reshape(P, KT, SEQ).transpose(2, 1, 0).reshape(1, SEQ, D)
```

```python
from contextlib import ExitStack

import numpy as np

import concourse.bass as bass
from concourse import mybir

P = 128
ALU = mybir.AluOpType
ACT = mybir.ActivationFunctionType
AX = mybir.AxisListType
F32 = mybir.dt.float32
F32R = mybir.dt.float32r

D = 1024
KT = D // P
SEQ = 256
META = 16
CTX = META + SEQ
HD = 64
EPS = 1e-6
NEG = -1e30
DFF = 2816
FT = DFF // P

HEADS1 = 6
KS0, QS0, VS0, VF0, FL0, KF0, QF0, U0 = 0, 3, 6, 9, 12, 13, 16, 19
TILES1 = 21
POOL_WINDOWS = (2, 4, 8, 16)

R0, K0, V0, WA0, G0, Q0, KC0, VC0, KS1, VS1, KW1, VW1, GL0 = 0, 4, 8, 12, 13, 14, 18, 19, 20, 21, 22, 23, 24
SHIFTED = 14
TILES2 = 25
PAIRS = 4
CHUNK = 64
CHUNKS = SEQ // CHUNK
PACKS = PAIRS * CHUNKS
LEVELS = 6
DECAY = float(np.exp(-0.5))
GN_EPS = 64e-5
GQA, KVH = 4, 2
NQH = GQA * KVH
CMP_BLOCK, CMP_STRIDE = 32, 16
N_CMP = (SEQ - CMP_BLOCK) // CMP_STRIDE + 1
CMP_PAD = 16
CMP_PAIRS = CMP_BLOCK // 2
CMP_HIDDEN = 256
EXP_MAX = 43.0
GELU = 2.0 * float(np.sqrt(2.0 / np.pi))

TILE = KT * P
BLOCK = 2 * TILE
RING = 2
SLOTS = 4
UNROLL = 4


def blocks_of(tiles):
    return -(-tiles // 2)


B_IN1 = 0
B_OUT1 = B_IN1 + blocks_of(TILES1)
B_UP1 = B_OUT1 + KT // 2
B_DOWN1 = B_UP1 + FT
B_IN2 = B_DOWN1 + FT // 2
B_CMP = B_IN2 + blocks_of(TILES2)
B_OUT2 = B_CMP + 4
B_UP2 = B_OUT2 + KT // 2
B_DOWN2 = B_UP2 + FT

T_IN1 = 0
T_OUT1 = T_IN1 + TILES1
T_UP1 = T_OUT1 + KT
T_DOWN1 = T_UP1 + 2 * FT
T_IN2 = T_DOWN1 + FT
T_OUT2 = T_IN2 + TILES2
T_UP2 = T_OUT2 + KT
T_DOWN2 = T_UP2 + 2 * FT
T_END = T_DOWN2 + FT
PHASES = ((T_IN1, B_IN1), (T_OUT1, B_OUT1), (T_UP1, B_UP1), (T_DOWN1, B_DOWN1), (T_IN2, B_IN2),
          (T_OUT2, B_OUT2), (T_UP2, B_UP2), (T_DOWN2, B_DOWN2), (T_END, None))


def phase_of(t):
    return next(n for n in range(len(PHASES) - 1) if t < PHASES[n + 1][0])


def place(t):
    t0, b0 = PHASES[phase_of(t)]
    return b0 + (t - t0) // 2, (t - t0) % 2


def freed(t):
    n = phase_of(t)
    k, layer = t - PHASES[n][0], n // 4
    if n % 4 == 0:
        return f"proj{layer + 1}_ready", k + 1
    if n % 4 == 1:
        return "out_ready", layer * KT + k + 1
    if n % 4 == 2:
        return ("gate_ready", "up_ready")[k % 2], layer * FT + k // 2 + 1
    return ("down_ready", (layer + 1) * KT) if k == FT - 1 else ("down_used", layer * (FT - 1) + k + 1)

NORMS = ("norm1", "norm_ff1", "norm3", "norm_ff2", "norm6")
FEEDING = ("norm1", "mixer1", "norm_ff1", "norm4", "mixer2", "norm_ff2")


MIXER_ORDER = {1: (0, 1, 5, 6, 7, 2, 3, 4), 2: (4, 5, 6, 7, 0, 1, 2, 3)}


def norm_bank(name):
    return 7 if name in ("norm1", "norm_ff1", "norm_ff2") else 3


UNITS = 2 * GQA
NSA_STEPS = [("hidden", 1), ("hidden", 2), ("hidden", 3)]
NSA_STEPS += [(name, 0) for name in ("gelu", "sigmoid", "hidden_turn", "compressed", "cmp_scores", "cmp_probs", "cmp_turn")]
NSA_STEPS += [(name, u) for u in range(UNITS) for name in ("scores", "probs", "turn")] + [("scores", UNITS)]


def nth(name):
    return NORMS.index(name) + 1


def normed(name, k):
    return FEEDING.index(name) * KT + k + 1




def constant_tables():
    i = np.arange(P)
    c = {}
    c["ones"] = np.ones((P, P))
    c["eps"] = np.full((P, 1), EPS)
    c["one"] = np.ones((P, 1))
    c["ident"] = np.eye(P)
    c["neg_ones"] = -np.ones((P, P))
    c["neg_from"] = -(i[:, None] >= i[None, :]).astype(float)
    strict = i[:, None] < i[None, :]
    c["strict"] = strict.astype(float)
    c["strict_add"] = np.where(strict, 0.0, NEG)
    a = np.where(np.arange(META + P)[None, :] <= META + i[:, None], 0.0, NEG)
    b = np.where(np.arange(CTX)[None, :] <= META + P + i[:, None], 0.0, NEG)
    c["causal1"] = np.concatenate([a, b], 1)
    c["head_ones"] = np.kron(np.eye(2), np.ones((HD, HD)))
    sel = np.zeros((P, HEADS1, P))
    for h in range(HEADS1):
        sel[h, h] = 1.0
    c["pick_head"] = sel.reshape(P, -1)
    slopes = 2.0 ** (-8.0 * np.arange(1, NQH + 1) / NQH)
    k = np.arange(SEQ)
    dist = (P + i[:, None]) - k[None, :]
    c["alibi"] = np.where(dist[:, None, :] >= 0, -slopes[None, :, None] * dist[:, None, :], NEG).reshape(P, -1)
    end = np.arange(CMP_PAD) * CMP_STRIDE + CMP_BLOCK - 1
    t = i[:, None] + P * np.arange(2)[None, :]
    dist = t[:, :, None] - end
    ok = (dist >= 0) & (np.arange(CMP_PAD) < N_CMP)
    c["cmp_bias"] = np.where(ok[:, :, None, :], -slopes[None, None, :, None] * dist[:, :, None, :], NEG).reshape(P, -1)
    c["cmp_any"] = ok.any(-1).astype(float)
    rows = np.arange(P)
    c["cmp_spread"] = ((rows[None, :] % CMP_PAD == i[:, None]) & (i[:, None] < N_CMP)).astype(float)
    m = np.zeros((P, GQA, P))
    for r in rows:
        head = r // CMP_PAD
        m[r, head % GQA, HD * (head // GQA):HD * (head // GQA) + HD] = 1.0
    c["cmp_own"] = m.reshape(P, -1)
    same = i[:, None] // CHUNK == i[None, :] // CHUNK
    before = same & (i[:, None] < i[None, :])
    upto = same & (i[:, None] <= i[None, :])
    c["pack_masks"] = np.concatenate([before, upto, before, upto], 1).astype(float)
    lv = []
    for level in range(LEVELS):
        w = 2 << level
        lv.append((i[:, None] // w == i[None, :] // w) & (i[:, None] % w < w // 2) & (i[None, :] % w >= w // 2))
    c["join"] = np.concatenate(lv, 1).astype(float)
    c["join0_t"] = lv[0].T.astype(float)
    c["gn_eps"] = np.full((P, 1), GN_EPS)
    return {k: np.ascontiguousarray(v, np.float32) for k, v in c.items()}


def columns(widths):
    at, out = 0, {}
    for k, w in widths.items():
        out[k] = (at, w)
        at += w
    return out, at


CONST_AT, CONST_W = columns({k: v.shape[1] for k, v in constant_tables().items()})

VEC_WIDTHS = {
    "norm1": KT, "norm2": KT, "norm3": KT,
    "norm4": KT, "norm5": KT, "norm6": KT, "mu": SHIFTED, "w0": PAIRS, "a0": PAIRS, "k_k": PAIRS, "k_a": PAIRS,
    "r_k": PAIRS, "w2a2": PAIRS * P, "g2": PAIRS * P, "lnx_w": PAIRS, "lnx_b": PAIRS,
    "pe_k": CMP_PAIRS, "pe_v": CMP_PAIRS, "cmp_w2k": 2 * HD, "cmp_w2v": 2 * HD,
    "fox_gain": 3, "sb_gain": 3, "pool_scale": 2, "forget_bias": 1, "pool_w": 2 * P,
}
VEC_AT, VEC_W = columns(VEC_WIDTHS)
CONST_FIRST, VEC_FIRST = CONST_AT["ident"][0], VEC_AT["mu"][0]


def build_program(nc, xT, weights, consts, vecs, out):
    ctx = ExitStack()
    sems = {}

    def S(name):
        if name not in sems:
            sems[name] = ctx.enter_context(nc.semaphore(name))
        return sems[name]

    def sb(name, shape):
        return ctx.enter_context(nc.sbuf_tensor(name, shape, F32))

    def parts(name, shape):
        return ctx.enter_context(nc.sbuf_tensor(name, shape, F32R))

    with ctx:
        ring = sb("ring", [P, RING, 2, KT, P])
        cst = sb("cst", [P, CONST_W])
        vec = sb("vec", [P, VEC_W])
        res = sb("res", [P, KT, CTX])
        act_in = sb("act_in", [P, KT, CTX])
        yT = sb("yT", [P, KT, SEQ])
        flat = sb("scratch", [P, 5632])
        nrm = sb("nrm", [P, 2, CTX])
        sig = sb("sig", [P, 2, SEQ])
        sig2 = sb("sig2", [P, 2, SEQ])
        state = sb("state", [P, PAIRS + 1, HD])
        rhs_sa = sb("rhs_sa", [P, 2, PAIRS + 1, HD])
        small = sb("small", [P, 8, 16])
        with ExitStack() as mixer:
            arena = mixer.enter_context(nc.sbuf_tensor("arena", [P, 12288], F32))
            proj = mixer.enter_context(nc.sbuf_tensor("proj", [P, 25, CTX], F32))
            vtok = mixer.enter_context(nc.sbuf_tensor("vtok", [P, 3, 12, HD], F32))
            nsa_mem = mixer.enter_context(nc.sbuf_tensor("nsa_mem", [P, 4880], F32))
        w_hi = parts("w_hi", [P, SLOTS, KT, P])
        w_lo = parts("w_lo", [P, SLOTS, KT, P])
        hid_hi = parts("hid_hi", [P, FT, SEQ])
        hid_lo = parts("hid_lo", [P, FT, SEQ])
        parts("gap", [P, 12288 + 25 * CTX + 2304 - 2 * SLOTS * TILE - 2 * FT * SEQ])
        act_hi = parts("act_hi", [P, KT, CTX])
        act_lo = parts("act_lo", [P, KT, CTX])
        ps = ctx.enter_context(nc.psum_tensor("ps", [P, 8, 512], F32))

        def C(name, parts=P):
            at, w = CONST_AT[name]
            return cst[0:parts, at:at + w]

        def V(name, j=0, n=1):
            at, _ = VEC_AT[name]
            return vec[:, at + j:at + j + n]

        landed = [S(f"weights_landed_{r}") for r in range(RING)]

        class Steps:

            def __init__(self, eng, name):
                self.eng, self.sem, self.n = eng, S(name), 0

            def __call__(self, ins):
                self.n += 1
                ins.then_inc(self.sem, 1)
                self.eng.wait_ge(self.sem, self.n)

        def signal(eng, ins, name, n=1):
            ins.then_inc(S(name), 1)
            eng.wait_ge(S(name), n)

        sq = act_in
        sq_gained = flat[:, 0:KT * SEQ].rearrange("p (k t) -> p k t", k=KT)
        gain34 = sb("gain34", [P, KT])
        def flat_view(at, heads, n, parts=P):
            return flat[0:parts, at:at + heads * n].rearrange("p (h c) -> p h c", h=heads)

        sb_nl, sb_nlm = flat_view(0, 2, 384), flat_view(768, 2, SEQ, META)
        sb_pT, sb_pTm = flat_view(1280, 2, 384), flat_view(2048, 2, SEQ, META)
        s_row = flat_view(2560, 2, META + P + CTX)
        fox_pT, fox_pTm = flat_view(3424, 2, 384), flat_view(4192, 2, SEQ, META)
        mx, den, rden = (flat_view(4704 + 4 * n, 2, 2) for n in range(3))
        heads_out = act_in[:, :, :].rearrange("p a b -> p (a b)")[:, 0:6 * SEQ].rearrange("p (t q) -> p t q", t=6)
        def carve(at, *shape, parts=P, mem=arena):
            n = int(np.prod(shape))
            names = " ".join("abcd"[:len(shape)])
            return mem[0:parts, at:at + n].rearrange(f"p ({names}) -> p {names}",
                                                       **dict(zip("abcd", shape))), at + n

        negc, at = carve(2 * SLOTS * TILE, 1, CTX, parts=8)
        negc = negc[:, 0, :]
        fl_t, at = carve(at, 2, CTX, parts=8)
        pool_s, at = carve(at, 2, 2, CTX)
        hsq, at = carve(at, 6, SEQ)
        ar, at = carve(0, 2, PAIRS, 2, P)
        ar = arena[:, 0:2048].rearrange("p (m j x c) -> p m j x c", m=2, j=PAIRS, x=2)
        bf, at = carve(2048, 2, PAIRS, P)
        kf, at = carve(at, 2, PAIRS, P)
        wt, at = carve(at, 2, PAIRS, 4 * P)
        xi, at = carve(at, 2, PAIRS, P)
        xt, at = carve(at, 2, PAIRS, P)
        pb, at = carve(at, 2, PAIRS, P)
        nl, at = carve(at, 2, PAIRS, P)
        def feat(t, at):
            return t[:, at:at + PAIRS * SEQ].rearrange("p (j t) -> p j t", j=PAIRS)
        act_flat = act_in[:, :, :].rearrange("p a b -> p (a b)")
        vtok_flat = vtok[:, :, :, :].rearrange("p a b c -> p (a b c)")
        sigw, lsum, avec, kkn, scr = (feat(flat, 1024 * n) for n in range(5))
        sdg, lora_w = flat[:, 5120:5376], flat[0:HD, 5376:5632]
        gate_t, p_inv = feat(act_flat, 0), feat(act_flat, 1024)
        p_inc, p_exc = lsum, sigw
        reset = yT[:, 0:4, :]
        y_all = vtok_flat[:, 0:1024].rearrange("p (n v) -> p n v", n=PACKS)
        v_st = vtok_flat[:, 1024:2048].rearrange("p (n v) -> p n v", n=PACKS)
        v_wide = vtok_flat[:, 1024:2048 + HD]
        def nsa_carve(at, *shape, parts=P):
            return carve(at, *shape, parts=parts, mem=nsa_mem)

        s_nsa, at = nsa_carve(0, 2, P + SEQ)
        pt_nsa, at = nsa_carve(at, 2, P + SEQ)
        vt_nsa, at = nsa_carve(at, 2, 2, P)
        blk, at = nsa_carve(at, 2, CMP_PAIRS, 32)
        hid_t, at = nsa_carve(at, 2, 2, 32)
        hid_c, _ = nsa_carve(0, 2, CMP_HIDDEN, parts=32)
        gel, _ = nsa_carve(2 * CMP_HIDDEN, 2, CMP_HIDDEN, parts=32)
        kcmp, at = nsa_carve(at, 1, 32)
        vcmp, at = nsa_carve(at, 1, P, parts=CMP_PAD)
        vown, at = nsa_carve(at, GQA, P)
        s_cmp, at = nsa_carve(at, 2, NQH, CMP_PAD)
        pt_cmp, at = nsa_carve(at, 2, P)
        gates, at = nsa_carve(at, 2, 24)
        gl_t, at = nsa_carve(at, 1, SEQ, parts=24)
        vown_src, at = nsa_carve(at, 1, P)
        vown_src = vown_src[:, 0]
        mx_n, at = nsa_carve(at, 2, 2)
        den_n, at = nsa_carve(at, 2, 2)
        mx_c, at = nsa_carve(at, 2, NQH)
        den_c, at = nsa_carve(at, 2, NQH)

        def down_ahead(layer):
            return FT - 1 if layer == 1 else FT - SLOTS

        def narrow(bank):
            return ps[:, bank, :].rearrange("p (j c) -> p j c", j=PAIRS)[:, :, 0:HD]

        block = ctx.enter_context(nc.Block())

        @block.sync
        def _(sp):
            half = KT * CTX // 2
            flat_res = res[:].rearrange("p k t -> p (k t)")
            sp.dma_start(flat_res[:, 0:half], xT[:, 0:half]).then_inc(S("x_landed_a"), 16)
            sp.dma_start(flat_res[:, half:2 * half], xT[:, half:2 * half]).then_inc(S("x_landed_b"), 16)
            sp.dma_start(cst[:, 0:CONST_FIRST], consts[:, 0:CONST_FIRST]).then_inc(S("consts_landed"), 16)
            sp.dma_start(vec[:, 0:VEC_FIRST], vecs[:, 0:VEC_FIRST]).then_inc(S("vecs_landed"), 16)

            def load(b):
                if B_CMP <= b - RING < B_OUT2:
                    sp.wait_ge(S("cmp_block_used"), b - RING - B_CMP + 1)
                elif b >= RING:
                    last = max(t for t in range(T_END) if place(t)[0] == b - RING)
                    sp.wait_ge(S("w_split"), last + 1)
                sp.dma_start(ring[:, b % RING].rearrange("p a k c -> p (a k c)"), weights[b])\
                    .then_inc(landed[b % RING], 16)

            def load_up(b_up, t_up):
                with sp.Fori(0, (FT - RING) // UNROLL) as i:
                    for u in range(UNROLL):
                        b = b_up + RING + u
                        sp.wait_ge(S("w_split"), i * (2 * UNROLL) + (t_up + 2 * u + 2))
                        sp.dma_start(ring[:, b % RING].rearrange("p a k c -> p (a k c)"),
                                     weights[bass.ds(i * UNROLL + b, 1)].rearrange("o p c -> (o p) c"))\
                            .then_inc(landed[b % RING], 16)

            for b in range(B_IN1, B_UP1 + RING):
                load(b)
            load_up(B_UP1, T_UP1)
            for b in range(B_DOWN1, B_UP2 + RING):
                load(b)
            load_up(B_UP2, T_UP2)
            for b in range(B_DOWN2, B_DOWN2 + FT // 2):
                load(b)
            for t in range(0, KT, 2):
                sp.wait_ge(S("final_ready"), t + 2)
                sp.dma_start(out[:, t * SEQ:(t + 2) * SEQ], yT[:, t:t + 2, :].rearrange("p k t -> p (k t)"))\
                    .then_inc(S("stored"), 16)
            sp.wait_ge(S("stored"), 16 * KT // 2)

        @block.gpsimd
        def _(pool):
            pool.wait_ge(S("norm_squares"), KT)
            pool.dma_start(cst[:, CONST_FIRST:CONST_W], consts[:, CONST_FIRST:CONST_W]).then_inc(S("tables_landed"), 16)
            pool.dma_start(vec[:, VEC_FIRST:VEC_W], vecs[:, VEC_FIRST:VEC_W]).then_inc(S("tables_landed"), 16)
            pool.wait_ge(S("normed"), normed("norm4", KT - 1))
            pool.memset(state[:], 0.0)
            pool.memset(vtok_flat[:, 2048:2048 + HD], 0.0)
            signal(pool, pool.memset(rhs_sa[:], 0.0), "state_zeroed")
            pool.memset(reset, 1.0).then_inc(S("reset_ones"), 1)
            pool.wait_ge(S("reset_ones"), 1)
            signal(pool, pool.memset(reset.rearrange("p j (c t) -> p j c t", c=CHUNKS)[:, :, :, 0:1], 0.0),
                   "reset_ready")
            pool.wait_ge(S("proj2_ready"), TILES2)
            signal(pool, pool.memset(blk[:], 0.0), "blk_zeroed")
            signal(pool, pool.memset(arena[:, 0:4096], 0.0), "packs_zeroed")
            for cp in range(0, CHUNKS, 2):
                for level in range(1, LEVELS):
                    for m in range(2):
                        c = cp + m
                        if level == 1:
                            pool.wait_ge(S("products_masked"), c + 1)
                        if level > 1:
                            pool.wait_ge(S(f"join_products_{m}"), (cp // 2) * (LEVELS - 1) + level - 1)
                        elif cp > 0:
                            pool.wait_ge(S("chunk_done"), c - 1)
                        pool.tensor_tensor(nl[:, m], wt[:, m, :, 0:P],
                                           C("join")[:, level * P:(level + 1) * P].unsqueeze(1)
                                           .to_broadcast([P, PAIRS, P]), ALU.mult)\
                            .then_inc(S(f"joins_{m}"), 1)

        @block.tensor
        def _(pe):
            def part_products(dst, slot, k, hi, lo, first, last):
                pe.matmul(dst, w_hi[:, slot, k, :], hi, start=first, stop=False, skip_group_check=True)
                pe.matmul(dst, w_hi[:, slot, k, :], lo, start=False, stop=False, skip_group_check=True)
                return pe.matmul(dst, w_lo[:, slot, k, :], hi, start=False, stop=last, skip_group_check=True)

            def tile_products(dst, slot, n, first=None, order=range(KT)):
                for at, k in enumerate(order):
                    if first is not None:
                        pe.wait_ge(S("normed"), normed(first, at))
                    mm = part_products(dst, slot, k, act_hi[:, k, 0:n], act_lo[:, k, 0:n], at == 0, at == KT - 1)
                return mm

            def have(b):
                pe.wait_ge(landed[b % RING], 16 * (b // RING + 1))

            def sum_squares(name, tokens):
                for k in range(KT):
                    pe.wait_ge(S("norm_squares"), (nth(name) - 1) * KT + k + 1)
                    mm = pe.matmul(ps[:, norm_bank(name), 0:tokens], C("ones"), sq[:, k, 0:tokens],
                                   start=(k == 0), stop=(k == KT - 1))
                mm.then_inc(S("norm_sums"), 1)

            def feed_forward(layer, t_up):
                t_down = t_up + 2 * FT

                def up(j, i=None):
                    step = 0 if i is None else i * UNROLL
                    t = t_up + 2 * j
                    if j >= 2:
                        pe.wait_ge(S("hid_full"), step + ((layer - 1) * FT + j - 1))
                    pe.wait_ge(S("w_split"), step * 2 + (t + 1))
                    tile_products(ps[:, 2 * (j % 2), 0:SEQ], t % SLOTS, SEQ, f"norm_ff{layer}" if j == 0 else None)\
                        .then_inc(S("gate_ready"), 1)
                    pe.wait_ge(S("w_split"), step * 2 + (t + 2))
                    tile_products(ps[:, 2 * (j % 2) + 1, 0:SEQ], (t + 1) % SLOTS, SEQ).then_inc(S("up_ready"), 1)

                up(0)
                up(1)
                with pe.Fori(0, (FT - 2) // UNROLL) as i:
                    for u in range(UNROLL):
                        up(2 + u, i)

                def down(d, i=None):
                    step = 0 if i is None else i * UNROLL
                    t = t_down + d
                    pe.wait_ge(S("w_split"), step + (t + 1))
                    pe.wait_ge(S("hid_ready"), step + ((layer - 1) * FT + d + 1))
                    last = d == FT - 1
                    if i is None:
                        hi, lo = hid_hi[:, d, :], hid_lo[:, d, :]
                    else:
                        hi, lo = (x[:, bass.ds(i * UNROLL + d, 1), :].rearrange("p o t -> p (o t)")
                                  for x in (hid_hi, hid_lo))
                    for f in range(KT):
                        mm = part_products(ps[:, 4 + f // 2, (f % 2) * SEQ:(f % 2 + 1) * SEQ], t % SLOTS, f,
                                           hi, lo, d == 0 and f % 2 == 0, last)
                        if last:
                            mm.then_inc(S("down_ready"), 1)
                    if not last:
                        mm.then_inc(S("down_used"), 1)

                down(0)
                with pe.Fori(0, (FT - 2) // UNROLL) as i:
                    for u in range(UNROLL):
                        down(1 + u, i)
                down(FT - 1)

            pe.wait_ge(S("consts_landed"), 16)
            sum_squares("norm1", CTX)
            def half_of(h):
                return slice(HD * (h % 2), HD * (h % 2) + HD)

            def sb_logits(r):
                for j in range(2):
                    hs = half_of(j)
                    q = proj[hs, QS0 + r, META:CTX]
                    k = proj[hs, KS0 + r, :]
                    kw = dict(stop=True, skip_group_check=True)
                    pe.matmul(ps[:, j, 0:SEQ], k[:, META:META + P], q, start=True, **kw)
                    pe.matmul(ps[:, j, SEQ:SEQ + P], k[:, META + P:CTX], q[:, P:SEQ], start=False, **kw)
                    mm = pe.matmul(ps[0:META, 2 + j, 0:SEQ], k[:, 0:META], q, start=True, **kw)
                mm.then_inc(S("sb_logits"), 1)

            def sb_sums(r):
                pe.wait_ge(S("sb_logs"), r + 1)
                for j in range(2):
                    a_all = ps[:, j, 0:SEQ]
                    b_all = ps[:, j, SEQ:SEQ + P]
                    m_all = ps[0:META, 2 + j, 0:SEQ]
                    nl_a, nl_b, nl_m = sb_nl[:, j, 0:SEQ], sb_nl[:, j, SEQ:SEQ + P], sb_nlm[:, j, :]
                    kw = dict(start=False, stop=True, skip_group_check=True)
                    pe.matmul(a_all, C("neg_from"), nl_a, **kw)
                    pe.matmul(a_all[:, P:SEQ], C("neg_ones"), nl_b, **kw)
                    pe.matmul(a_all[:, 0:P], C("ident"), C("strict_add"), **kw)
                    pe.matmul(b_all, C("neg_from"), nl_b, **kw)
                    pe.matmul(b_all, C("ident"), C("strict_add"), **kw)
                    pe.matmul(m_all, C("neg_from")[0:META, 0:META], nl_m, **kw)
                    pe.matmul(m_all, C("neg_ones")[:, 0:META], nl_a, **kw)
                    mm = pe.matmul(m_all[:, P:SEQ], C("neg_ones")[:, 0:META], nl_b, **kw)
                mm.then_inc(S("sb_sums"), 1)

            def fox_scores(r):
                for j in range(2):
                    h = 2 * r + j
                    hs = half_of(j)
                    q = proj[hs, QF0 + r, META:CTX]
                    k = proj[hs, KF0 + r, :]
                    for t, (c0, nk) in enumerate(((0, META + P), (META + P, CTX))):
                        pe.matmul(ps[:, 4 + j, c0:c0 + nk], q[:, t * P:(t + 1) * P], k[:, 0:nk],
                                  start=True, stop=False, skip_group_check=True)
                        mm = pe.matmul(ps[:, 4 + j, c0:c0 + nk],
                                       C("pick_head")[0:HEADS1, h * P:(h + 1) * P], negc[0:HEADS1, 0:nk],
                                       start=False, stop=True, skip_group_check=True)
                mm.then_inc(S("fox_scores"), 1)

            def fox_turn(r):
                pe.wait_ge(S("fox_probs"), r + 1)
                for j in range(2):
                    row = s_row[:, j, :]
                    pe.transpose(ps[:, 4 + j, 0:P], row[:, META:META + P], C("ident"))
                    pe.transpose(ps[:, 4 + j, P:SEQ], row[:, P + 2 * META:2 * P + 2 * META], C("ident"))
                    pe.transpose(ps[:, 4 + j, SEQ:SEQ + P], row[:, 2 * P + 2 * META:3 * P + 2 * META], C("ident"))
                    pe.transpose(ps[0:META, 6, j * SEQ:j * SEQ + P], row[:, 0:META], C("ident"))
                    mm = pe.transpose(ps[0:META, 6, j * SEQ + P:(j + 1) * SEQ],
                                      row[:, META + P:META + P + META], C("ident"))
                mm.then_inc(S("fox_turned"), 1)

            def weighted_values(r, src, srcm, v0, at, done):
                for j in range(2):
                    dst = ps[half_of(j), 7, at:at + SEQ]
                    vh = v0 + 2 * r + j
                    kw = dict(skip_group_check=True)
                    pe.matmul(dst, vtok[:, 0, vh, :], src[:, j, 0:SEQ], start=True, stop=False, **kw)
                    pe.matmul(dst, vtok[0:META, 2, vh, :], srcm[:, j, :], start=False, stop=False, **kw)
                    mm = pe.matmul(dst[:, P:SEQ], vtok[:, 1, vh, :], src[:, j, SEQ:SEQ + P],
                                   start=False, stop=True, **kw)
                mm.then_inc(S(done), 1)

            for t in range(TILES1):
                if t == VF0 + 4:
                    pe.wait_ge(S("tables_landed"), 32)
                    pe.wait_ge(S("proj1_copied_a"), (VF0 + 3) // 2)
                    pe.wait_ge(S("proj1_copied_b"), (VF0 + 3) // 2)
                    for kt, (t0, nt) in enumerate(((META, P), (META + P, P), (0, META))):
                        for f in range(6):
                            mm = pe.transpose(ps[0:nt, 2 * kt + f // 4, (f % 4) * P:(f % 4 + 1) * P],
                                              proj[:, VS0 + f, t0:t0 + nt], C("ident"))
                        mm.then_inc(S("v1_turned"), 1)
                if t == VF0 + 7:
                    pe.wait_ge(S("v1_copied"), 3)
                    sb_logits(0)
                if t == TILES1 - 1:
                    pe.wait_ge(S("proj1_copied_a"), (U0 + 1) // 2)
                    pe.wait_ge(S("proj1_copied_b"), U0 // 2)
                    pe.wait_ge(S("decay_sums"), 1)
                    fox_scores(0)
                pe.wait_ge(S("w_split"), T_IN1 + t + 1)
                if t >= 2:
                    pe.wait_ge(S("proj1_copied_" + "ab"[t % 2]), (t - 2) // 2 + 1)
                tile_products(ps[:, 6 + t % 2, 0:CTX], (T_IN1 + t) % SLOTS, CTX,
                              "norm1" if t == 0 else None).then_inc(S("proj1_ready"), 1)

            pe.wait_ge(S("proj1_copied_a"), (TILES1 + 1) // 2)
            pe.wait_ge(S("proj1_copied_b"), TILES1 // 2)
            for r in range(3):
                sb_sums(r)
                fox_turn(r)
                pe.wait_ge(S("sb_weights"), r + 1)
                if r > 0:
                    pe.wait_ge(S("fox_out_copied"), r)
                weighted_values(r, sb_pT, sb_pTm, 0, 0, "sb_out")
                if r < 2:
                    sb_logits(r + 1)
                pe.wait_ge(S("fox_weights"), r + 1)
                pe.wait_ge(S("sb_out_copied"), r + 1)
                weighted_values(r, fox_pT, fox_pTm, 6, SEQ, "fox_out")
                if r < 2:
                    fox_scores(r + 1)

            pe.wait_ge(S("pool_diff"), 1)
            for t in range(2):
                mm = pe.matmul(ps[:, 4 + t, 0:SEQ], V("pool_w", t * P, P), pool_s[:, 0, t, META:CTX],
                               start=True, stop=True)
            mm.then_inc(S("pool_mixed"), 1)
            pe.wait_ge(S("head_squares"), 1)
            for n in range(3):
                width = 2 * SEQ if n < 2 else SEQ
                mm = pe.matmul(ps[:, n, 0:width], C("head_ones"),
                               hsq[:, 2 * n:2 * n + width // SEQ, :].rearrange("p a b -> p (a b)"),
                               start=True, stop=True)
            mm.then_inc(S("head_sums"), 1)
            pe.wait_ge(S("head_squares"), 2)
            pe.matmul(ps[:, 3, 0:SEQ], C("head_ones"), hsq[:, 5, :], start=True, stop=True)\
                .then_inc(S("head_sums"), 1)

            def output_product(layer, t0):
                for t in range(KT):
                    pe.wait_ge(S("w_split"), t0 + t + 1)
                    if t >= 4:
                        pe.wait_ge(S("out_added"), (layer - 1) * KT + t - 3)
                    tile_products(ps[:, t % 4, 0:SEQ], (t0 + t) % SLOTS, SEQ, f"mixer{layer}" if t == 0 else None,
                                  MIXER_ORDER[layer])\
                        .then_inc(S("out_ready"), 1)

            output_product(1, T_OUT1)
            sum_squares("norm_ff1", SEQ)
            feed_forward(1, T_UP1)
            for k in range(KT):
                pe.wait_ge(S("norm_squares"), (nth("norm3") - 1) * KT + k + 1)
                kw = dict(stop=(k == KT - 1), skip_group_check=True)
                pe.matmul(ps[:, 3, 0:SEQ], C("ones"), sq[:, k, 0:SEQ], start=(k == 0), **kw)
                mm = pe.matmul(ps[:, 3, SEQ:2 * SEQ], C("ones"), sq_gained[:, k, :], start=False, **kw)
            mm.then_inc(S("norm_sums"), 1)

            for t in range(TILES2):
                if t == 12:
                    pe.wait_ge(S("key_squares"), 1)
                    for f in range(2):
                        mm = pe.matmul(ps[:, 6 + f, :], C("head_ones"),
                                       scr[:, 2 * f:2 * f + 2, :].rearrange("p a b -> p (a b)"),
                                       start=True, stop=True)
                    mm.then_inc(S("key_sums"), 1)
                if t == 18:
                    pe.wait_ge(S("lora_w_ready"), 1)
                    for f in range(PAIRS):
                        pe.matmul(ps[:, 2 + f // 2, (f % 2) * SEQ:(f % 2 + 1) * SEQ], V("w2a2", f * P, P)[0:HD],
                                  lora_w, start=True, stop=True)
                    for f in range(PAIRS):
                        mm = pe.matmul(ps[:, 4 + f // 2, (f % 2) * SEQ:(f % 2 + 1) * SEQ],
                                       V("w2a2", f * P, P)[HD:P], proj[HD:P, WA0, 1:1 + SEQ], start=True, stop=True)
                    mm.then_inc(S("lora_ready"), 1)
                    pe.wait_ge(S("key_sums_kept"), 1)
                    pe.wait_ge(S("gate_inputs"), 1)
                    for f in range(PAIRS):
                        mm = pe.matmul(ps[:, 6 + f // 2, (f % 2) * SEQ:(f % 2 + 1) * SEQ], V("g2", f * P, P),
                                       sdg, start=True, stop=True)
                    mm.then_inc(S("gates_ready"), 1)
                pe.wait_ge(S("w_split"), T_IN2 + t + 1)
                if t >= 2:
                    pe.wait_ge(S("proj2_copied_" + "ab"[t % 2]), (t - 2) // 2 + 1)
                tile_products(ps[:, t % 2, 0:SEQ], (T_IN2 + t) % SLOTS, SEQ,
                              "norm4" if t == 0 else None).then_inc(S("proj2_ready"), 1)

            def tok(c):
                return slice(CHUNK * c, CHUNK * (c + 1))

            def halves():
                return ((h, slice(HD * h, HD * (h + 1))) for h in range(2))

            def grp(g):
                return slice(HD * g, HD * (g + 1))

            pe.wait_ge(S("proj2_copied_a"), (TILES2 + 1) // 2)
            pe.wait_ge(S("proj2_copied_b"), TILES2 // 2)
            for c in range(CHUNKS):
                for j in range(PAIRS):
                    n = c * PAIRS + j
                    for h, hs in halves():
                        mm = pe.matmul(ps[hs, n // 8, (n % 8) * HD:(n % 8 + 1) * HD],
                                       proj[hs, V0 + j, 1 + CHUNK * c:1 + CHUNK * (c + 1)], C("ident")[hs, hs],
                                       start=True, stop=True)
            mm.then_inc(S("v_stacked"), 1)
            pe.wait_ge(S("gates_copied"), 1)

            def hidden(n):
                x, b = n // 2, B_CMP + n
                if n % 2 == 0:
                    pe.wait_ge(S("blk_ready"), x + 1)
                have(b)
                for r in range(8):
                    w1 = ring[:, b % RING, r // 4, 2 * (r % 4):2 * (r % 4) + 2, :].rearrange("p a c -> p (a c)")
                    mm = pe.matmul(ps[0:32, 6, x * CMP_HIDDEN:(x + 1) * CMP_HIDDEN], blk[:, x, n % 2 * 8 + r, :], w1,
                                   start=(n % 2 == 0 and r == 0), stop=(n % 2 == 1 and r == 7))
                mm.then_inc(S("cmp_block_used"), 1)

            hidden(0)

            def nsa_step(name, u):
                if name == "hidden":
                    hidden(u)
                elif name == "gelu":
                    pe.wait_ge(S("bonus_kept"), 1)
                    for br, v in enumerate((VS1, VW1)):
                        for t in range(2):
                            mm = pe.transpose(ps[:, 7, (2 * br + t) * P:(2 * br + t + 1) * P],
                                              proj[:, v, 1 + t * P:1 + (t + 1) * P], C("ident"))
                    mm.then_inc(S("nsa_turned"), 1)
                elif name == "hidden_turn":
                    pe.wait_ge(S("gate_sigmoids"), 1)
                    pe.wait_ge(S("cmp_gelu"), 1)
                    for x in range(2):
                        for q in range(2):
                            pe.transpose(ps[:, 6, (2 * x + q) * 32:(2 * x + q + 1) * 32],
                                         hid_c[:, x, q * P:(q + 1) * P], C("ident")[0:32, 0:32])
                    for t in range(2):
                        mm = pe.transpose(ps[:, 6, SEQ + t * 24:SEQ + (t + 1) * 24], gl_t[:, 0, t * P:(t + 1) * P],
                                          C("ident")[0:24, 0:24])
                    mm.then_inc(S("cmp_turned"), 1)
                elif name == "compressed":
                    pe.wait_ge(S("hid_t_copied"), 1)
                    pe.wait_ge(S("nsa_values"), 1)
                    for g in range(KVH):
                        for q in range(2):
                            pe.matmul(ps[grp(g), 6, 320:320 + CMP_PAD], V("cmp_w2k", q * HD, HD),
                                      hid_t[:, 0, q, g * CMP_PAD:(g + 1) * CMP_PAD], start=(q == 0), stop=(q == 1))
                    for g in range(KVH):
                        for q in range(2):
                            mm = pe.matmul(ps[0:CMP_PAD, 7, g * HD:(g + 1) * HD],
                                           hid_t[:, 1, q, g * CMP_PAD:(g + 1) * CMP_PAD],
                                           V("cmp_w2v", q * HD, HD), start=(q == 0), stop=(q == 1))
                    mm.then_inc(S("cmp_kv"), 1)
                elif name == "cmp_scores":
                    pe.wait_ge(S("cmp_kv_copied"), 1)
                    for g in range(KVH):
                        for t in range(2):
                            for a in range(GQA):
                                at = (t * GQA + a) * CMP_PAD
                                pe.matmul(ps[:, 6 + g, at:at + CMP_PAD],
                                          proj[grp(g), Q0 + a, 1 + t * P:1 + (t + 1) * P],
                                          kcmp[grp(g), 0, 0:CMP_PAD], start=True, stop=True)
                    pe.matmul(ps[:, 6, 384:384 + P], C("cmp_spread")[0:CMP_PAD, :], vcmp[:, 0, :],
                              start=True, stop=True).then_inc(S("cmp_scores"), 1)
                elif name == "cmp_turn":
                    pe.wait_ge(S("cmp_probs"), 1)
                    for t in range(2):
                        mm = pe.transpose(ps[:, 6, t * P:(t + 1) * P], s_cmp[:, t].rearrange("p h n -> p (h n)"),
                                          C("ident"))
                    mm.then_inc(S("cmp_probs_turned"), 1)
                elif name == "scores":
                    if u == 0:
                        pe.wait_ge(S("pt_cmp_copied"), 1)
                    else:
                        a, br = (u - 1) // 2, (u - 1) % 2
                        out_a, out_b = ps[:, 6, 384:384 + P], ps[:, 7, 384:384 + P]
                        kw = dict(skip_group_check=True)
                        pe.wait_ge(S("nsa_weights"), u)
                        if u > 1:
                            pe.wait_ge(S("nsa_out_copied"), u - 1)
                        if br == 0:
                            pe.matmul(out_a, vown[:, a, :], pt_cmp[:, 0, :], start=True, stop=False, **kw)
                            pe.matmul(out_b, vown[:, a, :], pt_cmp[:, 1, :], start=True, stop=False, **kw)
                        for g in range(KVH):
                            w = pt_nsa[:, g, :]
                            vt = [vt_nsa[:, br, t, grp(g)] for t in range(2)]
                            pe.matmul(out_a[grp(g)], vt[0], w[:, 0:P], start=(br == 1), stop=True, **kw)
                            pe.matmul(out_b[grp(g)], vt[0], w[:, P:SEQ], start=(br == 1), stop=False, **kw)
                            mm = pe.matmul(out_b[grp(g)], vt[1], w[:, SEQ:SEQ + P], start=False, stop=True, **kw)
                        mm.then_inc(S("nsa_out"), 1)
                    if u < UNITS:
                        a, br = u // 2, u % 2
                        for g in range(KVH):
                            q = proj[grp(g), Q0 + a, 1:1 + SEQ]
                            kk = proj[grp(g), (KS1, KW1)[br], 1:1 + SEQ]
                            pe.matmul(ps[:, 6 + g, 0:P], q[:, 0:P], kk[:, 0:P], start=True, stop=True)
                            mm = pe.matmul(ps[:, 6 + g, P:P + SEQ], q[:, P:SEQ], kk, start=True, stop=True)
                        mm.then_inc(S("nsa_scores"), 1)
                elif name == "turn":
                    pe.wait_ge(S("nsa_probs"), u + 1)
                    for g in range(KVH):
                        for n in range(3):
                            mm = pe.transpose(ps[:, 6 + g, n * P:(n + 1) * P], s_nsa[:, g, n * P:(n + 1) * P],
                                              C("ident"))
                    mm.then_inc(S("nsa_probs_turned"), 1)

            nsa_steps = iter(NSA_STEPS)

            def nsa():
                nsa_step(*next(nsa_steps, ("", 0)))

            def turn_outputs(cp):
                pe.wait_ge(S("rwkv_y"), cp // 2 + 1)
                for m in range(2):
                    for j in range(PAIRS):
                        for h, hs in halves():
                            mm = pe.matmul(ps[hs, 4 + m, SEQ + j * CHUNK:SEQ + (j + 1) * CHUNK],
                                           y_all[hs, (cp + m) * PAIRS + j, :], C("ident")[hs, hs],
                                           start=True, stop=True)
                mm.then_inc(S("rwkv_turned"), 1)

            for cp in range(0, CHUNKS, 2):
                pe.wait_ge(S("v_st_copied"), 1)
                for m in range(2):
                    c = cp + m
                    pe.wait_ge(S("packs_ready"), c + 1)
                    if c > 0:
                        pe.wait_ge(S("products_masked"), c)
                    if c == 1:
                        pe.wait_ge(S("bonus_kept"), 1)
                    if cp > 0:
                        pe.wait_ge(S("chunk_done"), cp)
                    for j in range(PAIRS):
                        both = ar[:, m, j, :, :].rearrange("p x c -> p (x c)")
                        pe.matmul(ps[:, j, 0:2 * P], bf[:, m, j, :], both, start=True, stop=True)
                        pe.matmul(ps[:, j, 2 * P:4 * P], kf[:, m, j, :], both, start=True, stop=True)
                        mm = pe.matmul(ps[:, 4 + m, j * P:(j + 1) * P], ar[:, m, j, 0, :], bf[:, m, j, :],
                                       start=True, stop=True)
                    mm.then_inc(S("products_ready"), 1)
                    if c == 0:
                        pe.wait_ge(S("rk_ready"), 1)
                        for n, bank in enumerate((7, 5)):
                            mm = pe.matmul(ps[:, bank, :], C("head_ones"),
                                           scr[:, 2 * n:2 * n + 2, :].rearrange("p a b -> p (a b)"),
                                           start=True, stop=True)
                        mm.then_inc(S("bonus_sums"), 1)
                    nsa()
                for level in range(1, LEVELS):
                    n = (cp // 2) * (LEVELS - 1) + level
                    for m in range(2):
                        if level == 1:
                            pe.wait_ge(S("products_masked"), cp + 2)
                        pe.wait_ge(S(f"joins_{m}"), n)
                        pe.wait_ge(S(f"inverse_grown_{m}"), n + cp // 2)
                        for j in range(PAIRS):
                            mm = pe.matmul(ps[:, 2 * m, j * P:(j + 1) * P], nl[:, m, j, :], xi[:, m, j, :],
                                           start=True, stop=True)
                        mm.then_inc(S(f"join_products_{m}"), 1)
                    nsa()
                    if cp > 0 and level == 1:
                        turn_outputs(cp - 2)
                    for m in range(2):
                        pe.wait_ge(S(f"join_copied_{m}"), n)
                        for j in range(PAIRS):
                            mm = pe.matmul(ps[:, 2 * m + 1, j * P:(j + 1) * P], pb[:, m, j, :], xt[:, m, j, :],
                                           start=True, stop=True)
                            if level < LEVELS - 1:
                                mm = pe.matmul(ps[:, 2 * m, j * P:(j + 1) * P], xt[:, m, j, :], pb[:, m, j, :],
                                               start=True, stop=True)
                        mm.then_inc(S(f"inverse_terms_{m}"), 1)
                    nsa()
                for m in range(2):
                    pe.wait_ge(S(f"inverse_grown_{m}"), (cp // 2 + 1) * LEVELS)
                    for j in range(PAIRS):
                        pe.transpose(ps[:, 2 * m, j * P:(j + 1) * P], bf[:, m, j, :], C("ident"))
                        mm = pe.transpose(ps[:, 2 * m + 1, j * P:(j + 1) * P], kf[:, m, j, :], C("ident"))
                    mm.then_inc(S("bk_turned"), 1)
                nsa()
                for m in range(2):
                    c = cp + m
                    if c == 0:
                        pe.wait_ge(S("state_zeroed"), 1)
                    else:
                        pe.wait_ge(S("chunk_done"), c)

                    def part(bank, j):
                        return ps[:, bank, j * P:(j + 1) * P]

                    def wide(src, j):
                        return src.rearrange("p j v -> p (j v)")[:, j * HD:j * HD + P]

                    kw = dict(stop=True, skip_group_check=True)
                    for j in range(PAIRS):
                        pe.matmul(part(4, j), ar[:, m, j, 0, :], wide(state[:], j), start=(j == 0), **kw)
                        mm = pe.matmul(part(4, j), wt[:, m, j, 2 * P:3 * P], v_wide[:, (c * PAIRS + j) * HD:(c * PAIRS + j) * HD + P],
                                       start=False, **kw)
                    mm.then_inc(S("rhs_ready"), 1)
                    nsa()
                    pe.wait_ge(S("rhs_copied"), c + 1)
                    for j in range(PAIRS):
                        mm = pe.matmul(part(5, j), xt[:, m, j, :], wide(rhs_sa[:, 0], j), start=(j == 0), **kw)
                    mm.then_inc(S("sa_ready"), 1)
                    for j in range(PAIRS):
                        pe.matmul(part(4, j), ar[:, m, j, 1, :], wide(state[:], j), start=(j == 0), **kw)
                        pe.matmul(part(4, j), wt[:, m, j, 3 * P:4 * P], v_wide[:, (c * PAIRS + j) * HD:(c * PAIRS + j) * HD + P],
                                  start=False, **kw)
                    pe.wait_ge(S("sa_copied"), c + 1)
                    pe.wait_ge(S("bk_copied"), c + 1)
                    for j in range(PAIRS):
                        pe.matmul(part(5, j), nl[:, m, j, :], v_wide[:, (c * PAIRS + j) * HD:(c * PAIRS + j) * HD + P], start=(j == 0), **kw)
                        mm = pe.matmul(part(5, j), pb[:, m, j, :], wide(rhs_sa[:, 1], j), start=False, **kw)
                    mm.then_inc(S("state_terms"), 1)
                    for j in range(PAIRS):
                        mm = pe.matmul(part(4, j), wt[:, m, j, P:2 * P], wide(rhs_sa[:, 1], j), start=False, **kw)
                    mm.then_inc(S("y_terms"), 1)
                    nsa()
            for name, u in nsa_steps:
                nsa_step(name, u)
            turn_outputs(CHUNKS - 2)

            output_product(2, T_OUT2)
            sum_squares("norm_ff2", SEQ)
            feed_forward(2, T_UP2)
            sum_squares("norm6", SEQ)

        @block.scalar
        def _(act):
            step = Steps(act, "scalar_steps")
            act.preload_act_table_set("natural_log_exp_and_others")

            def norm_root(name, src_ready, n, src, tokens, ahead=()):
                for k in range(KT):
                    act.wait_ge(S(src_ready[k // 4] if name == "norm1" else src_ready), n if name == "norm1" else n - KT + k + 1)
                    act.activation(sq[:, k, 0:tokens], src[:, k, :], ACT.Square).then_inc(S("norm_squares"), 1)
                for t in ahead:
                    split_hi(t)
                act.wait_ge(S("norm_squares"), nth(name) * KT)
                act.wait_ge(S("norm_sums"), nth(name))
                step(act.activation(nrm[:, 0, 0:tokens], ps[:, norm_bank(name), 0:tokens], ACT.Ln,
                                    bias=C("eps"), scale=1.0 / D))
                signal(act, act.activation(nrm[:, 1, 0:tokens], nrm[:, 0, 0:tokens], ACT.Exp, scale=-0.5),
                       "norm_root", nth(name))

            def split_hi(t, i=None, per_step=0):
                b, half = place(t)
                step = 0 if i is None else i
                if half == 0 or t in (T_IN1,):
                    act.wait_ge(landed[b % RING], step * (16 * per_step // (2 * RING)) + 16 * (b // RING + 1))
                if t >= SLOTS:
                    name, n = freed(t - SLOTS)
                    act.wait_ge(S(name), n if i is None else i * (per_step // (2 if name in ("gate_ready", "up_ready")
                                                                              else 1)) + n)
                act.activation(w_hi[:, t % SLOTS].rearrange("p k c -> p (k c)"),
                               ring[:, b % RING, half].rearrange("p k c -> p (k c)"), ACT.Copy)\
                    .then_inc(S("w_rounded"), 1)

            def round_tiles(n, tokens, src, tiles=range(KT)):
                for k in tiles:
                    if n is not None:
                        act.wait_ge(S("act_full"), n + k + 1)
                    act.activation(act_hi[:, k, 0:tokens], src[:, k, 0:tokens], ACT.Copy).then_inc(S("act_rounded"), 1)

            act.wait_ge(S("consts_landed"), 16)
            norm_root("norm1", ("x_landed_a", "x_landed_b"), 16, res[:, :, 0:CTX], CTX, range(T_IN1, T_IN1 + SLOTS))
            round_tiles(0, CTX, act_in)

            def scale_of(t):
                return HD ** -0.5 if QS0 <= t < QS0 + 3 or QF0 <= t < QF0 + 3 else 1.0

            def sb_logarithms(r):
                act.wait_ge(S("sb_logits"), r + 1)
                act.activation(sb_nl, ps[:, 0:2, 0:384], ACT.Abs)
                step(act.activation(sb_nlm, ps[0:META, 2:4, 0:SEQ], ACT.Abs))
                act.activation(sb_nl, sb_nl, ACT.Exp, scale=-1.0)
                step(act.activation(sb_nlm, sb_nlm, ACT.Exp, scale=-1.0))
                act.activation(sb_nl, sb_nl, ACT.Ln, bias=C("one"))
                signal(act, act.activation(sb_nlm, sb_nlm, ACT.Ln, bias=C("one", META)), "sb_softplus", r + 1)

            for t in range(TILES1):
                if t % 2 == 0:
                    n = 6 if t == FL0 else P
                    act.wait_ge(S("proj1_ready"), t + 1)
                    act.activation(proj[0:n, t, :], ps[0:n, 6 + t % 2, 0:CTX], ACT.Copy, scale=scale_of(t))\
                        .then_inc(S("proj1_copied_a"), 1)
                split_hi(T_IN1 + t + SLOTS)
                if t == VF0 + 6:
                    act.wait_ge(S("forget_logit"), 1)
                    step(act.activation(fl_t[0:6, 1, :], fl_t[0:6, 0, :], ACT.Abs))
                    step(act.activation(fl_t[0:6, 1, :], fl_t[0:6, 1, :], ACT.Exp, scale=-1.0))
                    signal(act, act.activation(fl_t[0:6, 1, :], fl_t[0:6, 1, :], ACT.Ln, bias=C("one", 6)),
                           "forget_log")
                if t == VF0 + 7:
                    sb_logarithms(0)
            act.wait_ge(S("tables_landed"), 32)
            def fox_exps(r):
                act.wait_ge(S("fox_max"), r + 1)
                for j in range(2):
                    for t, (c0, nk) in enumerate(((0, META + P), (META + P, CTX))):
                        ins = act.activation(s_row[:, j, c0:c0 + nk], s_row[:, j, c0:c0 + nk], ACT.Exp,
                                             bias=mx[:, t, j:j + 1], accum_out=den[:, t, j:j + 1])
                signal(act, ins, "fox_exps", r + 1)

            for r in range(3):
                fox_exps(r)
                act.wait_ge(S("sb_sums"), r + 1)
                if r > 0:
                    act.wait_ge(S("sb_out"), r)
                act.activation(sb_pT, ps[:, 0:2, 0:384], ACT.Exp)
                signal(act, act.activation(sb_pTm, ps[0:META, 2:4, 0:SEQ], ACT.Exp), "sb_weights", r + 1)
                act.wait_ge(S("fox_turned"), r + 1)
                if r > 0:
                    act.wait_ge(S("fox_out"), r)
                act.activation(fox_pT, ps[:, 4:6, 0:384], ACT.Copy)
                signal(act, act.activation(fox_pTm, ps[0:META, 6, :].rearrange("p (h q) -> p h q", h=2), ACT.Copy),
                       "fox_weights", r + 1)
                if r < 2:
                    sb_logarithms(r + 1)

            for n, (t0, t1) in enumerate(((0, 5), (5, 6))):
                if n == 0:
                    act.wait_ge(S("sb_out_copied"), 3)
                    act.wait_ge(S("fox_out_copied"), 2)
                else:
                    act.wait_ge(S("fox_out_copied"), 3)
                signal(act, act.activation(hsq[:, t0:t1, :], heads_out[:, t0:t1, :], ACT.Square), "head_squares",
                       n + 1)
            round_tiles_after = (("pool_y", 1, 0, 2), ("heads_y", 1, 2, 7), ("heads_y", 2, 7, 8))
            for n, (t0, t1) in enumerate(((0, 5), (5, 6))):
                act.wait_ge(S("head_sums"), n + 1)
                src = ps[:, 0:3, :].rearrange("p a b -> p (a b)")[:, 0:5 * SEQ] if n == 0 else ps[:, 3, 0:SEQ]
                dst = hsq[:, t0:t1, :].rearrange("p a b -> p (a b)")
                step(act.activation(dst, src, ACT.Ln, bias=C("eps"), scale=1.0 / HD))
                signal(act, act.activation(dst, dst, ACT.Exp, scale=-0.5), "head_root", n + 1)

            def feed_forward(layer, t_up):
                def one(j, i=None):
                    at = (layer - 1) * FT + j
                    step = 0 if i is None else i * UNROLL
                    m = j % 2
                    own = S("sigmoid_steps")
                    split_hi(t_up + 2 * j + SLOTS, i, 2 * UNROLL)
                    act.wait_ge(S("gate_kept"), step + (at + 1))
                    act.activation(sig[:, m, :], sig[:, m, :], ACT.Exp, scale=-1.0).then_inc(own, 1)
                    act.wait_ge(own, step * 2 + (2 * at + 1))
                    act.activation(sig[:, m, :], sig[:, m, :], ACT.Ln, bias=C("one")).then_inc(own, 1)
                    act.wait_ge(own, step * 2 + (2 * at + 2))
                    act.activation(sig[:, m, :], sig[:, m, :], ACT.Exp, scale=-1.0).then_inc(S("sigmoid"), 1)
                    split_hi(t_up + 2 * j + 1 + SLOTS, i, 2 * UNROLL)
                    act.wait_ge(S("hid_full"), step + (at + 1))
                    if i is None:
                        dst = hid_hi[:, j, :]
                    else:
                        dst = hid_hi[:, bass.ds(i * UNROLL + j, 1), :].rearrange("p o t -> p (o t)")
                    act.activation(dst, sig2[:, m, :], ACT.Copy).then_inc(S("hid_rounded"), 1)

                one(0)
                one(1)
                with act.Fori(0, (FT - 2) // UNROLL) as i:
                    for u in range(UNROLL):
                        one(2 + u, i)
                t_down = t_up + 2 * FT
                ahead = down_ahead(layer)
                split_hi(t_down + SLOTS)
                with act.Fori(0, (ahead - 1) // UNROLL) as i:
                    for u in range(UNROLL):
                        split_hi(t_down + SLOTS + 1 + u, i, UNROLL)
                for d in range(1 + (ahead - 1) // UNROLL * UNROLL, ahead):
                    split_hi(t_down + SLOTS + d)

            for name, n, k0, k1 in round_tiles_after:
                act.wait_ge(S(name), n)
                round_tiles(None, SEQ, yT, MIXER_ORDER[1][k0:k1])
            for t in range(KT - 1):
                split_hi(T_OUT1 + t + SLOTS)
            norm_root("norm_ff1", "out_added", KT, res[:, :, META:CTX], SEQ, (T_UP1 + SLOTS - 1,))
            round_tiles(KT, SEQ, act_in)
            feed_forward(1, T_UP1)
            for k in range(KT):
                act.wait_ge(S("down_added"), k + 1)
                act.activation(sq[:, k, 0:SEQ], res[:, k, META:CTX], ACT.Square)
                act.activation(sq_gained[:, k, :], res[:, k, META:CTX], ACT.Square, scale=V("norm3", k))\
                    .then_inc(S("norm_squares"), 1)
            split_hi(T_IN2 + SLOTS - 1)
            act.wait_ge(S("norm_squares"), nth("norm3") * KT)
            act.wait_ge(S("norm_sums"), nth("norm3"))
            step(act.activation(nrm[:, 0, 0:SEQ], ps[:, 3, 0:SEQ], ACT.Ln, bias=C("eps"), scale=1.0 / D))
            act.activation(nrm[:, 1, 0:SEQ], nrm[:, 0, 0:SEQ], ACT.Exp, scale=-0.5)
            signal(act, act.activation(nrm[:, 0, 0:SEQ], nrm[:, 0, 0:SEQ], ACT.Exp, scale=-1.0), "norm_root",
                   nth("norm3"))
            act.wait_ge(S("norm4_mean"), 1)
            step(act.activation(nrm[:, 0, 0:SEQ], nrm[:, 0, 0:SEQ], ACT.Ln, bias=C("eps"), scale=1.0 / D))
            signal(act, act.activation(nrm[:, 0, 0:SEQ], nrm[:, 0, 0:SEQ], ACT.Exp, scale=-0.5), "norm4_root")

            def one_over_one_plus(dst):
                step(act.activation(dst, dst, ACT.Ln, bias=C("one", dst.shape[0])))
                return act.activation(dst, dst, ACT.Exp, scale=-1.0)

            round_tiles(2 * KT, SEQ, act_in)
            for t in range(TILES2):
                if t % 2 == 0:
                    n = 24 if t == GL0 else P
                    act.wait_ge(S("proj2_ready"), t + 1)
                    act.activation(proj[0:n, t, 1:1 + SEQ], ps[0:n, t % 2, 0:SEQ], ACT.Copy,
                                   scale=HD ** -0.5 if Q0 <= t < Q0 + 4 else 1.0).then_inc(S("proj2_copied_a"), 1)
                if t + SLOTS < TILES2:
                    split_hi(T_IN2 + t + SLOTS)
                if t == 10:
                    act.wait_ge(S("key_scaled"), 1)
                    signal(act, act.activation(scr, kkn, ACT.Square), "key_squares")
                if t == 13:
                    act.wait_ge(S("key_sums_kept"), 1)
                    step(act.activation(scr, scr, ACT.Ln))
                    signal(act, act.activation(scr, scr, ACT.Exp, scale=-0.5), "key_root")
                if t == 15:
                    act.wait_ge(S("shifted"), 1)
                    step(act.activation(lora_w, lora_w, ACT.Exp, scale=2.0))
                    signal(act, one_over_one_plus(lora_w), "lora_w_exp")
                    step(act.activation(sdg, sdg, ACT.Exp, scale=-1.0))
                    signal(act, one_over_one_plus(sdg), "gate_inputs")
                if t in (19, 21):
                    n, dst = ((1, sigw), (2, avec))[t == 21]
                    act.wait_ge(S("lora_biased"), n)
                    step(act.activation(dst, dst, ACT.Exp, scale=-1.0))
                    signal(act, one_over_one_plus(dst), "decay_a_sigmoids", n)
                if t == 22:
                    act.wait_ge(S("gates_ready"), 1)
                    signal(act, act.activation(gate_t.rearrange("p j t -> p (j t)"),
                                               ps[:, 6:8, :].rearrange("p a b -> p (a b)"), ACT.Copy), "gates_copied")

            act.wait_ge(S("blk_zeroed"), 1)
            act.wait_ge(S("proj2_copied_b"), TILES2 // 2)

            def gather_blocks(x):
                for g in range(KVH):
                    for q in range(2):
                        full = proj[HD * g:HD * (g + 1), (KC0, VC0)[x], 1 + q:1 + q + 255]
                        view = bass.AP(full.tensor, full.offset, [full.ap[0], [2, CMP_PAIRS], [CMP_STRIDE, N_CMP]])
                        ins = act.activation(blk[HD * q:HD * (q + 1), x, :, g * CMP_PAD:g * CMP_PAD + N_CMP],
                                             view, ACT.Copy)
                signal(act, ins, "blk_gathered", x + 1)

            gather_blocks(0)
            act.wait_ge(S("decay_scanned"), 2)
            step(act.activation(p_inv, lsum, ACT.Exp, scale=DECAY))
            act.activation(p_exc, sigw, ACT.Exp, scale=-DECAY)
            signal(act, act.activation(p_inc, lsum, ACT.Exp, scale=-DECAY), "decay_powers")
            gather_blocks(1)
            act.wait_ge(S("v_stacked"), 1)
            signal(act, act.activation(v_st.rearrange("p n v -> p (n v)"),
                                       ps[:, 0:2, :].rearrange("p a b -> p (a b)"), ACT.Copy), "v_st_copied")
            step(act.activation(gl_t[:, 0], proj[0:24, GL0, 1:1 + SEQ], ACT.Exp, scale=-1.0))
            signal(act, one_over_one_plus(gl_t[:, 0]), "gate_sigmoids")

            def nsa_step(name, u):
                if name == "sigmoid":
                    act.wait_ge(S("cmp_gelu_arg"), 1)
                    step(act.activation(gel[:], gel[:], ACT.Exp, scale=-GELU))
                    signal(act, one_over_one_plus(gel[:]), "cmp_gelu_sigmoid")
                    act.wait_ge(S("nsa_turned"), 1)
                    signal(act, act.activation(vt_nsa[:].rearrange("p b t c -> p (b t c)"), ps[:, 7, :], ACT.Copy),
                           "nsa_values")
                elif name == "hidden_turn":
                    act.wait_ge(S("cmp_turned"), 1)
                    act.activation(gates[:].rearrange("p t n -> p (t n)"), ps[:, 6, SEQ:SEQ + 48], ACT.Copy)
                    signal(act, act.activation(hid_t[:].rearrange("p a b c -> p (a b c)"), ps[:, 6, 0:128],
                                               ACT.Copy), "hid_t_copied")
                elif name == "compressed":
                    act.wait_ge(S("cmp_kv"), 1)
                    act.activation(kcmp[:, 0, 0:CMP_PAD], ps[:, 6, 320:320 + CMP_PAD], ACT.Copy)
                    signal(act, act.activation(vcmp[:, 0], ps[0:CMP_PAD, 7, 0:P], ACT.Copy), "cmp_kv_copied")
                elif name == "cmp_scores":
                    act.wait_ge(S("cmp_centred"), 1)
                    signal(act, act.activation(s_cmp[:], s_cmp[:], ACT.Exp), "cmp_exps")
                elif name == "cmp_turn":
                    act.wait_ge(S("cmp_probs_turned"), 1)
                    signal(act, act.activation(pt_cmp[:].rearrange("p t q -> p (t q)"), ps[:, 6, 0:SEQ], ACT.Copy),
                           "pt_cmp_copied")
                elif name == "probs":
                    act.wait_ge(S("nsa_max"), u + 1)
                    for g in range(KVH):
                        for t, (c0, n) in enumerate(((0, P), (P, SEQ))):
                            ins = act.activation(s_nsa[:, g, c0:c0 + n], s_nsa[:, g, c0:c0 + n], ACT.Exp,
                                                 bias=mx_n[:, t, g:g + 1], accum_out=den_n[:, t, g:g + 1])
                    signal(act, ins, "nsa_exps", u + 1)
                elif name == "turn":
                    act.wait_ge(S("nsa_probs_turned"), u + 1)
                    if u > 0:
                        act.wait_ge(S("nsa_out"), u)
                    signal(act, act.activation(pt_nsa[:], ps[:, 6:8, 0:P + SEQ], ACT.Copy), "nsa_weights", u + 1)

            nsa_steps = iter(NSA_STEPS)

            def nsa():
                nsa_step(*next(nsa_steps, ("", 0)))

            def output_root(cp):
                act.wait_ge(S("y_vars"), cp + 2)
                v = small[:, 2, cp * PAIRS:(cp + 2) * PAIRS]
                step(act.activation(v, v, ACT.Ln, bias=C("gn_eps"), scale=1.0 / HD))
                signal(act, act.activation(v, v, ACT.Exp, scale=-0.5), "y_root", cp // 2 + 1)

            for cp in range(0, CHUNKS, 2):
                for m in range(2):
                    nsa()
                if cp > 0:
                    output_root(cp - 2)
                for level in range(1, LEVELS):
                    n = (cp // 2) * (LEVELS - 1) + level
                    for m in range(2):
                        if level == 1 and cp > 0:
                            act.wait_ge(S("chunk_done"), cp)
                        act.wait_ge(S(f"join_products_{m}"), n)
                        if level > 1:
                            act.wait_ge(S(f"inverse_terms_{m}"), n - 1)
                        act.activation(pb[:, m].rearrange("p j c -> p (j c)"), ps[:, 2 * m, :], ACT.Copy)\
                            .then_inc(S(f"join_copied_{m}"), 1)
                    nsa()
                    nsa()
                for m in range(2):
                    act.wait_ge(S("bk_turned"), cp + m + 1)
                    act.activation(pb[:, m].rearrange("p j c -> p (j c)"), ps[:, 2 * m, :], ACT.Copy)
                    signal(act, act.activation(nl[:, m].rearrange("p j c -> p (j c)"), ps[:, 2 * m + 1, :],
                                               ACT.Copy), "bk_copied", cp + m + 1)
                nsa()
                for m in range(2):
                    c = cp + m
                    act.wait_ge(S("rhs_ready"), c + 1)
                    signal(act, act.activation(rhs_sa[:, 0, 0:PAIRS], narrow(4),
                                               ACT.Copy), "rhs_copied", c + 1)
                    nsa()
                    act.wait_ge(S("sa_ready"), c + 1)
                    if c > 0:
                        act.wait_ge(S("y_terms"), c)
                    signal(act, act.activation(rhs_sa[:, 1, 0:PAIRS], narrow(5),
                                               ACT.Copy), "sa_copied", c + 1)
                    nsa()
            output_root(CHUNKS - 2)
            for name, u in nsa_steps:
                nsa_step(name, u)

            act.wait_ge(S("chunk_done"), CHUNKS)
            split_hi(T_OUT2)
            act.wait_ge(S("nsa_out_copied"), UNITS)
            round_tiles(None, SEQ, yT, MIXER_ORDER[2][0:4])
            split_hi(T_OUT2 + 1)
            act.wait_ge(S("rwkv_finished"), 2)
            round_tiles(None, SEQ, yT, MIXER_ORDER[2][4:8])
            for t in range(2, SLOTS):
                split_hi(T_OUT2 + t)
            for t in range(KT - 1):
                split_hi(T_OUT2 + t + SLOTS)
            norm_root("norm_ff2", "out_added", 2 * KT, res[:, :, META:CTX], SEQ, (T_UP2 + SLOTS - 1,))
            round_tiles(3 * KT, SEQ, act_in)
            feed_forward(2, T_UP2)
            norm_root("norm6", "down_added", 2 * KT, res[:, :, META:CTX], SEQ)

        @block.vector
        def _(dve):
            step = Steps(dve, "vector_steps")

            def split_lo(t, i=None, per_step=0):
                b, half = place(t)
                dve.wait_ge(S("w_rounded"), t + 1 if i is None else i * per_step + (t + 1))
                dve.tensor_tensor(w_lo[:, t % SLOTS].rearrange("p k c -> p (k c)"),
                                  ring[:, b % RING, half].rearrange("p k c -> p (k c)"),
                                  w_hi[:, t % SLOTS].rearrange("p k c -> p (k c)").bitcast(F32), ALU.subtract)\
                    .then_inc(S("w_split"), 1)

            def rest(name, k, tokens, src, at=None):
                dve.wait_ge(S("act_rounded"), normed(name, k if at is None else at))
                dve.tensor_tensor(act_lo[:, k, 0:tokens], src[:, k, 0:tokens], act_hi[:, k, 0:tokens].bitcast(F32),
                                  ALU.subtract).then_inc(S("normed"), 1)

            def normalise(name, gain, t0, tokens):
                dve.wait_ge(S("norm_root"), nth(name))
                for k in range(KT + 1):
                    if k < KT:
                        dve.scalar_tensor_tensor(act_in[:, k, 0:tokens], res[:, k, t0:t0 + tokens],
                                                 V(gain, k), nrm[:, 1, 0:tokens], ALU.mult, ALU.mult)\
                            .then_inc(S("act_full"), 1)
                    if k > 0:
                        rest(name, k - 1, tokens, act_in)

            dve.wait_ge(S("vecs_landed"), 16)
            for t in range(3):
                split_lo(T_IN1 + t)
            normalise("norm1", "norm1", 0, CTX)
            split_lo(T_IN1 + 3)

            strict = C("strict").unsqueeze(1).to_broadcast([P, 2, P])

            def sb_negated_logs(r):
                dve.wait_ge(S("tables_landed"), 32)
                dve.wait_ge(S("sb_softplus"), r + 1)
                step(dve.scalar_tensor_tensor(sb_nl, ps[:, 0:2, 0:384], 0.0, sb_nl, ALU.max, ALU.add))
                dve.tensor_tensor(sb_nl[:, :, 0:P], sb_nl[:, :, 0:P], strict, ALU.mult)
                dve.tensor_tensor(sb_nl[:, :, SEQ:SEQ + P], sb_nl[:, :, SEQ:SEQ + P], strict, ALU.mult)
                signal(dve, dve.scalar_tensor_tensor(sb_nlm, ps[0:META, 2:4, 0:SEQ], 0.0, sb_nlm, ALU.max, ALU.add),
                       "sb_logs", r + 1)

            causal = C("causal1").unsqueeze(1).to_broadcast([P, 2, META + P + CTX])

            def fox_maxima(r):
                dve.wait_ge(S("fox_scores"), r + 1)
                step(dve.tensor_tensor(s_row, ps[:, 4:6, 0:META + P + CTX], causal, ALU.add))
                dve.tensor_reduce(mx[:, 0, :], s_row[:, :, 0:META + P], AX.X, ALU.max, negate=True)
                signal(dve, dve.tensor_reduce(mx[:, 1, :], s_row[:, :, META + P:META + P + CTX], AX.X, ALU.max,
                                              negate=True), "fox_max", r + 1)

            for t in range(TILES1):
                if t % 2:
                    dve.wait_ge(S("proj1_ready"), t + 1)
                    scale = HD ** -0.5 if QS0 <= t < QS0 + 3 or QF0 <= t < QF0 + 3 else 1.0
                    dve.tensor_scalar(proj[:, t, :], ps[:, 6 + t % 2, 0:CTX], scale, None, ALU.mult)\
                        .then_inc(S("proj1_copied_b"), 1)
                split_lo(T_IN1 + t + SLOTS)
                if t == VF0 + 4:
                    dve.wait_ge(S("tables_landed"), 32)
                    for kt, nt in enumerate((P, P, META)):
                        dve.wait_ge(S("v1_turned"), kt + 1)
                        src = ps[0:nt, 2 * kt:2 * kt + 2, :].rearrange("p a b -> p (a b)")[:, 0:12 * HD]
                        dve.tensor_copy(vtok[0:nt, kt].rearrange("p h d -> p (h d)"), src)\
                            .then_inc(S("v1_copied"), 1)
                if t == VF0 + 5:
                    dve.wait_ge(S("proj1_copied_a"), FL0 // 2 + 1)
                    signal(dve, dve.tensor_scalar(fl_t[0:6, 0, :], proj[0:6, FL0, :], V("forget_bias")[0:6], None,
                                                  ALU.add), "forget_logit")
                if t == VF0 + 7:
                    dve.wait_ge(S("forget_log"), 1)
                    step(dve.scalar_tensor_tensor(fl_t[0:6, 0, :], fl_t[0:6, 0, :], 0.0, fl_t[0:6, 1, :],
                                                  ALU.min, ALU.subtract))
                    step(dve.memset(fl_t[0:6, 1, :], 1.0))
                    signal(dve, dve.tensor_tensor_scan(negc[0:6, :], fl_t[0:6, 1, :], fl_t[0:6, 0, :], 0.0,
                                                       ALU.mult, ALU.subtract), "decay_sums")
                if t == VF0 + 8:
                    sb_negated_logs(0)
            fox_maxima(0)

            def pool_windows():
                dve.wait_ge(S("proj1_copied_a"), 11)
                dve.wait_ge(S("proj1_copied_b"), 10)
                u = proj[:, U0:U0 + 2, :]
                lo, hi = slice(0, HD), slice(HD, P)
                a, b = pool_s[:, 0], pool_s[:, 1]
                step(dve.tensor_tensor(a[:, :, 1:CTX], u[:, :, 1:CTX], u[:, :, 0:CTX - 1], ALU.add))
                step(dve.tensor_tensor(b[:, :, 3:CTX], a[:, :, 3:CTX], a[:, :, 1:CTX - 2], ALU.add))
                step(dve.scalar_tensor_tensor(a[lo, 0, META:CTX], a[lo, 0, META:CTX], 1 / 2, u[lo, 0, META:CTX],
                                              ALU.mult, ALU.subtract))
                step(dve.scalar_tensor_tensor(a[hi, 0, META:CTX], b[hi, 0, META:CTX], 1 / 4, u[hi, 0, META:CTX],
                                              ALU.mult, ALU.subtract))
                step(dve.tensor_tensor(a[:, 1, 7:CTX], b[:, 1, 7:CTX], b[:, 1, 3:CTX - 4], ALU.add))
                step(dve.tensor_tensor(b[:, 1, 15:CTX], a[:, 1, 15:CTX], a[:, 1, 7:CTX - 8], ALU.add))
                step(dve.scalar_tensor_tensor(a[lo, 1, META:CTX], a[lo, 1, META:CTX], 1 / 8, u[lo, 1, META:CTX],
                                              ALU.mult, ALU.subtract))
                signal(dve, dve.scalar_tensor_tensor(a[hi, 1, META:CTX], b[hi, 1, META:CTX], 1 / 16,
                                                     u[hi, 1, META:CTX], ALU.mult, ALU.subtract), "pool_diff")

            for r in range(3):
                if r > 0:
                    sb_negated_logs(r)
                    dve.wait_ge(S("fox_out"), r)
                    signal(dve, dve.tensor_copy(heads_out[:, 2 + r, :], ps[:, 7, SEQ:2 * SEQ]), "fox_out_copied", r)
                    fox_maxima(r)
                else:
                    pool_windows()
                dve.wait_ge(S("fox_exps"), r + 1)
                step(dve.reciprocal(rden, den))
                for j in range(2):
                    for t, (c0, nk) in enumerate(((0, META + P), (META + P, CTX))):
                        ins = dve.tensor_scalar(s_row[:, j, c0:c0 + nk], s_row[:, j, c0:c0 + nk],
                                                rden[:, t, j:j + 1], None, ALU.mult)
                signal(dve, ins, "fox_probs", r + 1)
                dve.wait_ge(S("sb_out"), r + 1)
                signal(dve, dve.tensor_copy(heads_out[:, r, :], ps[:, 7, 0:SEQ]), "sb_out_copied", r + 1)
            dve.wait_ge(S("fox_out"), 3)
            signal(dve, dve.tensor_copy(heads_out[:, 5, :], ps[:, 7, SEQ:2 * SEQ]), "fox_out_copied", 3)

            dve.wait_ge(S("pool_mixed"), 1)
            for t in range(2):
                ins = dve.tensor_scalar(yT[:, t, :], ps[:, 4 + t, 0:SEQ], V("pool_scale", t), None, ALU.mult)
            signal(dve, ins, "pool_y")
            for n, (t0, t1) in enumerate(((0, 5), (5, 6))):
                dve.wait_ge(S("head_root"), n + 1)
                for t in range(t0, t1):
                    gain, y = (V("sb_gain", t), 5 + t) if t < 3 else (V("fox_gain", t - 3), t - 1)
                    ins = dve.scalar_tensor_tensor(yT[:, y, :], heads_out[:, t, :], gain, hsq[:, t, :],
                                                   ALU.mult, ALU.mult)
                signal(dve, ins, "heads_y", n + 1)

            def mixer_output(layer, t_out):
                for at, k in enumerate(MIXER_ORDER[layer]):
                    if not (layer == 2 and at < 4):
                        rest(f"mixer{layer}", k, SEQ, yT, at)
                for t in range(KT):
                    dve.wait_ge(S("out_ready"), (layer - 1) * KT + t + 1)
                    dve.tensor_tensor(res[:, t, META:CTX], ps[:, t % 4, 0:SEQ], res[:, t, META:CTX], ALU.add)\
                        .then_inc(S("out_added"), 1)
                    if t < KT - 1:
                        split_lo(t_out + t + SLOTS)

            def feed_forward(layer, t_up):
                def one(j, i=None):
                    at = (layer - 1) * FT + j
                    step = 0 if i is None else i * UNROLL
                    m = j % 2
                    dve.wait_ge(S("gate_ready"), step + (at + 1))
                    dve.tensor_scalar(sig[:, m, :], ps[:, 2 * m, 0:SEQ], -EXP_MAX, None, ALU.max)\
                        .then_inc(S("gate_kept"), 1)
                    split_lo(t_up + 2 * j + SLOTS, i, 2 * UNROLL)
                    dve.wait_ge(S("sigmoid"), step + (at + 1))
                    if at >= 2:
                        dve.wait_ge(S("hid_ready"), step + (at - 1))
                    dve.tensor_tensor(sig2[:, m, :], ps[:, 2 * m, 0:SEQ], sig[:, m, :], ALU.mult)\
                        .then_inc(S("silu_steps"), 1)
                    dve.wait_ge(S("up_ready"), step + (at + 1))
                    dve.wait_ge(S("silu_steps"), step + (at + 1))
                    dve.tensor_tensor(sig2[:, m, :], ps[:, 2 * m + 1, 0:SEQ], sig2[:, m, :], ALU.mult)\
                        .then_inc(S("hid_full"), 1)
                    split_lo(t_up + 2 * j + 1 + SLOTS, i, 2 * UNROLL)
                    if i is None:
                        hi, lo = hid_hi[:, j, :], hid_lo[:, j, :]
                    else:
                        hi, lo = (x[:, bass.ds(i * UNROLL + j, 1), :].rearrange("p o t -> p (o t)")
                                  for x in (hid_hi, hid_lo))
                    dve.wait_ge(S("hid_rounded"), step + (at + 1))
                    dve.tensor_tensor(lo, sig2[:, m, :], hi.bitcast(F32), ALU.subtract).then_inc(S("hid_ready"), 1)

                one(0)
                one(1)
                with dve.Fori(0, (FT - 2) // UNROLL) as i:
                    for u in range(UNROLL):
                        one(2 + u, i)
                t_down = t_up + 2 * FT
                ahead = down_ahead(layer)
                split_lo(t_down + SLOTS)
                with dve.Fori(0, (ahead - 1) // UNROLL) as i:
                    for u in range(UNROLL):
                        split_lo(t_down + SLOTS + 1 + u, i, UNROLL)
                for d in range(1 + (ahead - 1) // UNROLL * UNROLL, ahead):
                    split_lo(t_down + SLOTS + d)

            def add_down(layer):
                for t in range(KT):
                    dve.wait_ge(S("down_ready"), (layer - 1) * KT + t // 2 * 2 + 2)
                    dve.tensor_tensor(res[:, t, META:CTX], ps[:, 4 + t // 2, (t % 2) * SEQ:(t % 2 + 1) * SEQ],
                                      res[:, t, META:CTX], ALU.add).then_inc(S("down_added"), 1)

            mixer_output(1, T_OUT1)
            split_lo(T_UP1 + SLOTS - 1)
            normalise("norm_ff1", "norm2", META, SEQ)
            feed_forward(1, T_UP1)
            add_down(1)
            split_lo(T_IN2 + SLOTS - 1)
            step(dve.tensor_tensor(gain34[:], V("norm3", 0, KT), V("norm4", 0, KT), ALU.mult))
            dve.wait_ge(S("norm_root"), nth("norm3"))
            signal(dve, dve.tensor_tensor(nrm[:, 0, 0:SEQ], ps[:, 3, SEQ:2 * SEQ], nrm[:, 0, 0:SEQ], ALU.mult),
                   "norm4_mean")
            dve.wait_ge(S("norm4_root"), 1)
            step(dve.tensor_tensor(nrm[:, 0, 0:SEQ], nrm[:, 0, 0:SEQ], nrm[:, 1, 0:SEQ], ALU.mult))
            for k in range(KT + 1):
                if k < KT:
                    dve.scalar_tensor_tensor(act_in[:, k, 0:SEQ], res[:, k, META:CTX], gain34[:, k:k + 1],
                                             nrm[:, 0, 0:SEQ], ALU.mult, ALU.mult).then_inc(S("act_full"), 1)
                if k > 0:
                    rest("norm4", k - 1, SEQ, act_in)
            for k in range(KT):
                dve.scalar_tensor_tensor(res[:, k, META:CTX], res[:, k, META:CTX], V("norm3", k), nrm[:, 1, 0:SEQ],
                                         ALU.mult, ALU.mult).then_inc(S("norm3_ready"), 1)

            dve.wait_ge(S("normed"), normed("norm4", KT - 1))
            step(dve.memset(proj[:, 0:SHIFTED, 0:1], 0.0))
            def per_pair(name):
                return V(name, 0, PAIRS).unsqueeze(2).to_broadcast([P, PAIRS, SEQ])

            rv, kv = proj[:, R0:R0 + 4, 1:1 + SEQ], proj[:, K0:K0 + 4, 1:1 + SEQ]

            def shift(t):
                if t % 2 == 0:
                    dve.wait_ge(S("proj2_copied_a"), t // 2 + 1)
                else:
                    dve.wait_ge(S("proj2_copied_b"), t // 2 + 1)
                diff = act_in[:, t % 2, 0:SEQ]
                step(dve.tensor_tensor(diff, proj[:, t, 0:SEQ], proj[:, t, 1:1 + SEQ], ALU.subtract))
                step(dve.scalar_tensor_tensor(proj[:, t, 1:1 + SEQ], diff, V("mu", t), proj[:, t, 1:1 + SEQ],
                                              ALU.mult, ALU.add))

            def add_bias(n):
                name, dst = (("w0", sigw), ("a0", avec))[n]
                for f in range(PAIRS):
                    ins = dve.tensor_scalar(dst[:, f, :],
                                            ps[:, 2 + 2 * n + f // 2, (f % 2) * SEQ:(f % 2 + 1) * SEQ],
                                            V(name, f), -EXP_MAX, ALU.add, ALU.max)
                signal(dve, ins, "lora_biased", n + 1)

            for t in range(TILES2):
                if t % 2:
                    dve.wait_ge(S("proj2_ready"), t + 1)
                    scale = HD ** -0.5 if Q0 <= t < Q0 + 4 else 1.0
                    dve.tensor_scalar(proj[:, t, 1:1 + SEQ], ps[:, t % 2, 0:SEQ], scale, None, ALU.mult)\
                        .then_inc(S("proj2_copied_b"), 1)
                if t + SLOTS < TILES2:
                    split_lo(T_IN2 + t + SLOTS)
                if 1 <= t <= SHIFTED:
                    shift(t - 1)
                if t == K0 + 5:
                    signal(dve, dve.tensor_tensor(kkn, kv, per_pair("k_k"), ALU.mult), "key_scaled")
                if t == 12:
                    dve.wait_ge(S("key_sums"), 1)
                    signal(dve, dve.tensor_scalar(scr.rearrange("p j t -> p (j t)"),
                                                  ps[:, 6:8, :].rearrange("p a b -> p (a b)"), 1e-24, None,
                                                  ALU.max), "key_sums_kept")
                if t == SHIFTED:
                    dve.tensor_scalar(lora_w, proj[0:HD, WA0, 1:1 + SEQ], EXP_MAX / 2, None, ALU.min)
                    signal(dve, dve.tensor_scalar(sdg, proj[:, G0, 1:1 + SEQ], -EXP_MAX, None, ALU.max), "shifted")
                if t == 15:
                    dve.wait_ge(S("key_root"), 1)
                    step(dve.scalar_tensor_tensor(kkn, kkn, -1.0, scr, ALU.mult, ALU.mult))
                if t == 16:
                    dve.wait_ge(S("lora_w_exp"), 1)
                    signal(dve, dve.tensor_scalar(lora_w, lora_w, -2.0, 1.0, ALU.mult, ALU.add), "lora_w_ready")
                if t == 18:
                    dve.wait_ge(S("lora_ready"), 1)
                    add_bias(0)
                if t == 19:
                    add_bias(1)
                if t == 21:
                    dve.wait_ge(S("reset_ready"), 1)
                    dve.wait_ge(S("decay_a_sigmoids"), 1)
                    one = "p j t -> p (j t)"
                    signal(dve, dve.tensor_tensor_scan(lsum.rearrange(one), reset.rearrange(one),
                                                       sigw.rearrange(one), 0.0, ALU.mult, ALU.add),
                           "decay_scanned", 1)
                    signal(dve, dve.tensor_tensor(sigw, lsum, sigw, ALU.subtract), "decay_scanned", 2)
            dve.wait_ge(S("decay_a_sigmoids"), 2)
            step(dve.scalar_tensor_tensor(scr, avec, -1.0, kv, ALU.add, ALU.mult))
            step(dve.tensor_tensor(scr, scr, per_pair("k_a"), ALU.mult))

            def block_positions(x):
                dve.wait_ge(S("blk_gathered"), x + 1)
                pe_add = V(("pe_k", "pe_v")[x], 0, CMP_PAIRS).unsqueeze(2).to_broadcast([P, CMP_PAIRS, 32])
                signal(dve, dve.tensor_tensor(blk[:, x], blk[:, x], pe_add, ALU.add), "blk_ready", x + 1)

            block_positions(0)
            step(dve.tensor_tensor(kv, kv, scr, ALU.add))
            step(dve.scalar_tensor_tensor(avec, kkn, -1.0, avec, ALU.mult, ALU.mult))

            gv = gates[:].rearrange("p t (g a b) -> p t g a b", g=KVH, a=GQA)
            alibi = C("alibi").rearrange("p (g a k) -> p g a k", g=KVH, a=GQA)
            flat_s = s_cmp[:].rearrange("p t h n -> p (t h) n")
            flat_d = den_c[:].rearrange("p t h -> p (t h)")
            wide = [P, 2 * NQH, CMP_PAD]

            def nsa_step(name, u):
                if name == "gelu":
                    dve.wait_ge(S("cmp_block_used"), 4)
                    step(dve.tensor_copy(hid_c[:].rearrange("p x h -> p (x h)"), ps[0:32, 6, :]))
                    step(dve.tensor_tensor(gel[:], hid_c[:], hid_c[:], ALU.mult))
                    step(dve.tensor_scalar(gel[:], gel[:], 0.044715, 1.0, ALU.mult, ALU.add))
                    step(dve.tensor_tensor(gel[:], gel[:], hid_c[:], ALU.mult))
                    signal(dve, dve.tensor_scalar(gel[:], gel[:], -EXP_MAX / GELU, None, ALU.max), "cmp_gelu_arg")
                elif name == "hidden_turn":
                    dve.wait_ge(S("cmp_gelu_sigmoid"), 1)
                    signal(dve, dve.tensor_tensor(hid_c[:], hid_c[:], gel[:], ALU.mult), "cmp_gelu")
                elif name == "cmp_scores":
                    dve.wait_ge(S("cmp_scores"), 1)
                    bias = C("cmp_bias").rearrange("p (t h n) -> p t h n", t=2, h=NQH)
                    for g in range(KVH):
                        dve.tensor_tensor(s_cmp[:, :, g * GQA:(g + 1) * GQA, :],
                                          ps[:, 6 + g, 0:2 * GQA * CMP_PAD]
                                          .rearrange("p (t h n) -> p t h n", t=2, h=GQA),
                                          bias[:, :, g * GQA:(g + 1) * GQA, :], ALU.add)
                    own = C("cmp_own").rearrange("p (a c) -> p a c", a=GQA)
                    vrep = vown_src
                    step(dve.tensor_copy(vrep, ps[:, 6, 384:384 + P]))
                    step(dve.tensor_tensor(vown[:], own, vrep.unsqueeze(1).to_broadcast([P, GQA, P]), ALU.mult))
                    flat_m = mx_c[:].rearrange("p t h -> p (t h)")
                    step(dve.tensor_reduce(flat_m, flat_s, AX.X, ALU.max))
                    signal(dve, dve.tensor_tensor(flat_s, flat_s, flat_m.unsqueeze(2).to_broadcast(wide),
                                                  ALU.subtract), "cmp_centred")
                elif name == "cmp_probs":
                    dve.wait_ge(S("cmp_exps"), 1)
                    step(dve.tensor_reduce(flat_d, flat_s, AX.X, ALU.add))
                    step(dve.reciprocal(flat_d, flat_d))
                    dve.wait_ge(S("hid_t_copied"), 1)
                    for g in range(KVH):
                        ins = dve.tensor_tensor(den_c[:, :, g * GQA:(g + 1) * GQA], den_c[:, :, g * GQA:(g + 1) * GQA],
                                                gv[:, :, g, :, 0], ALU.mult)
                    step(ins)
                    step(dve.tensor_tensor(den_c[:], den_c[:], C("cmp_any").unsqueeze(2).to_broadcast([P, 2, NQH]),
                                           ALU.mult))
                    signal(dve, dve.tensor_tensor(flat_s, flat_s, flat_d.unsqueeze(2).to_broadcast(wide),
                                                  ALU.mult), "cmp_probs")
                elif name == "scores":
                    if u < UNITS:
                        a = u // 2
                        dve.wait_ge(S("nsa_scores"), u + 1)
                        if u > 0:
                            dve.wait_ge(S("nsa_probs_turned"), u)
                        dve.tensor_tensor(s_nsa[:, :, 0:P], ps[:, 6:8, 0:P], alibi[:, :, a, P:SEQ], ALU.add)
                        step(dve.tensor_tensor(s_nsa[:, :, P:P + SEQ], ps[:, 6:8, P:P + SEQ], alibi[:, :, a, :],
                                               ALU.add))
                        dve.tensor_reduce(mx_n[:, 0, :], s_nsa[:, :, 0:P], AX.X, ALU.max, negate=True)
                        signal(dve, dve.tensor_reduce(mx_n[:, 1, :], s_nsa[:, :, P:P + SEQ], AX.X, ALU.max,
                                                      negate=True), "nsa_max", u + 1)
                    if u > 0:
                        a = (u - 1) // 2
                        dst = yT[:, 4 + a, :].rearrange("p (t q) -> p t q", t=2)
                        dve.wait_ge(S("nsa_out"), u)
                        if u % 2:
                            ins = dve.tensor_copy(dst, ps[:, 6:8, 384:384 + P])
                        else:
                            ins = dve.tensor_tensor(dst, ps[:, 6:8, 384:384 + P], dst, ALU.add)
                        signal(dve, ins, "nsa_out_copied", u)
                elif name == "probs":
                    a, br = u // 2, u % 2
                    dve.wait_ge(S("nsa_exps"), u + 1)
                    step(dve.reciprocal(den_n[:], den_n[:]))
                    step(dve.tensor_tensor(den_n[:], den_n[:], gv[:, :, :, a, 1 + br], ALU.mult))
                    for g in range(KVH):
                        for t, (c0, n) in enumerate(((0, P), (P, SEQ))):
                            ins = dve.tensor_scalar(s_nsa[:, g, c0:c0 + n], s_nsa[:, g, c0:c0 + n],
                                                    den_n[:, t, g:g + 1], None, ALU.mult)
                    signal(dve, ins, "nsa_probs", u + 1)

            nsa_steps = iter(NSA_STEPS)

            def nsa():
                nsa_step(*next(nsa_steps, ("", 0)))

            def make_packs(c):
                m = c % 2
                ts = slice(c * CHUNK, (c + 1) * CHUNK)
                for dst, x, y in ((ar[:, m, :, 0], kkn, p_exc), (ar[:, m, :, 1], rv, p_inc),
                                  (bf[:, m], avec, p_inv), (kf[:, m], kv, p_inv)):
                    for h in range(2):
                        hs = slice(HD * h, HD * (h + 1))
                        ins = dve.tensor_tensor(dst[hs, :, CHUNK * h:CHUNK * (h + 1)], x[hs, :, ts],
                                                y[hs, :, ts], ALU.mult)
                signal(dve, ins, "packs_ready", c + 1)

            dve.wait_ge(S("decay_powers"), 1)
            dve.wait_ge(S("packs_zeroed"), 1)
            make_packs(0)
            block_positions(1)
            step(dve.tensor_tensor(scr, rv, kv, ALU.mult))
            signal(dve, dve.tensor_tensor(scr, scr, per_pair("r_k"), ALU.mult), "rk_ready")
            make_packs(1)

            def centre_outputs(c):
                n = slice(c * PAIRS, (c + 1) * PAIRS)
                y = y_all[:, n, :]
                squares = scr[:, 0, :].rearrange("p (j v) -> p j v", j=PAIRS)
                step(dve.tensor_reduce(small[:, 1, n], y, AX.X, ALU.add))
                step(dve.tensor_scalar(small[:, 1, n], small[:, 1, n], 1.0 / HD, None, ALU.mult))
                step(dve.tensor_tensor(y, y, small[:, 1, n].unsqueeze(2).to_broadcast([P, PAIRS, HD]), ALU.subtract))
                step(dve.tensor_tensor(squares, y, y, ALU.mult))
                signal(dve, dve.tensor_reduce(small[:, 2, n], squares, AX.X, ALU.add), "y_vars", c + 1)

            def scale_outputs(cp):
                dve.wait_ge(S("y_root"), cp // 2 + 1)
                n = slice(cp * PAIRS, (cp + 2) * PAIRS)
                signal(dve, dve.tensor_tensor(y_all[:, n, :], y_all[:, n, :],
                                              small[:, 2, n].unsqueeze(2).to_broadcast([P, 2 * PAIRS, HD]),
                                              ALU.mult), "rwkv_y", cp // 2 + 1)

            def finish_outputs(cp):
                ts = slice(cp * CHUNK, (cp + 2) * CHUNK)
                dve.wait_ge(S("rwkv_turned"), cp // 2 + 1)
                for j in range(PAIRS):
                    y = yT[:, j, ts].rearrange("p (c t) -> p c t", c=2)
                    ins = dve.scalar_tensor_tensor(y, ps[:, 4:6, SEQ + j * CHUNK:SEQ + (j + 1) * CHUNK],
                                                   V("lnx_w", j), y, ALU.mult, ALU.add)
                step(ins)
                signal(dve, dve.tensor_tensor(yT[:, 0:4, ts], yT[:, 0:4, ts], gate_t[:, :, ts], ALU.mult),
                       "rwkv_finished", cp // 2 + 1)

            for cp in range(0, CHUNKS, 2):
                for m in range(2):
                    c = cp + m
                    dve.wait_ge(S("products_ready"), c + 1)
                    for j in range(PAIRS):
                        dve.tensor_tensor(wt[:, m, j], ps[:, j, :], C("pack_masks"), ALU.mult)
                    join0 = C("join")[:, 0:P].unsqueeze(1).to_broadcast([P, PAIRS, P])
                    join0_t = C("join0_t").unsqueeze(1).to_broadcast([P, PAIRS, P])
                    eye = C("ident").unsqueeze(1).to_broadcast([P, PAIRS, P])
                    ab = ps[:, 4 + m, :].rearrange("p (j c) -> p j c", j=PAIRS)
                    signal(dve, dve.tensor_tensor(xi[:, m], ab, join0_t, ALU.mult), "products_masked", c + 1)
                    if c == 0:
                        dve.wait_ge(S("bonus_sums"), 1)
                        for n, bank in enumerate((7, 5)):
                            ins = dve.tensor_tensor(yT[:, 2 * n:2 * n + 2, :],
                                                    ps[:, bank, :].rearrange("p (a b) -> p a b", a=2),
                                                    proj[:, V0 + 2 * n:V0 + 2 * n + 2, 1:1 + SEQ], ALU.mult)
                        signal(dve, ins, "bonus_kept")
                    step(dve.tensor_tensor(xt[:, m], wt[:, m, :, 0:P], join0, ALU.mult))
                    step(dve.tensor_tensor(xt[:, m], xt[:, m], eye, ALU.add))
                    signal(dve, dve.tensor_tensor(xi[:, m], xi[:, m], eye, ALU.add),
                           f"inverse_grown_{m}", (cp // 2) * LEVELS + 1)
                    if c == 2:
                        centre_outputs(1)
                    nsa()
                if cp > 0:
                    scale_outputs(cp - 2)
                for level in range(1, LEVELS):
                    n = (cp // 2) * (LEVELS - 1) + level
                    nsa()
                    for m in range(2):
                        dve.wait_ge(S(f"inverse_terms_{m}"), n)
                        flat2 = "p j c -> p (j c)"
                        if level < LEVELS - 1:
                            dve.tensor_tensor(xi[:, m].rearrange(flat2), ps[:, 2 * m, :],
                                              xi[:, m].rearrange(flat2), ALU.add)
                        signal(dve, dve.tensor_tensor(xt[:, m].rearrange(flat2), ps[:, 2 * m + 1, :],
                                                      xt[:, m].rearrange(flat2), ALU.add),
                               f"inverse_grown_{m}", (cp // 2) * LEVELS + level + 1)
                    nsa()
                    if cp == 0 and level == 2:
                        for j in range(PAIRS):
                            ins = dve.tensor_scalar(yT[:, j, :], yT[:, j, :], V("lnx_b", j), None, ALU.add)
                        step(ins)
                    if cp > 0 and level == 2:
                        finish_outputs(cp - 2)
                nsa()
                for m in range(2):
                    c = cp + m
                    nsa()
                    dve.wait_ge(S("state_terms"), c + 1)
                    step(dve.tensor_tensor(state[:, 0:PAIRS], narrow(5), state[:, 0:PAIRS], ALU.add))
                    end = p_inc[:, :, (c + 1) * CHUNK - 1:(c + 1) * CHUNK].to_broadcast([P, PAIRS, HD])
                    dve.wait_ge(S("y_terms"), c + 1)
                    signal(dve, dve.tensor_copy(y_all[:, c * PAIRS:(c + 1) * PAIRS, :], narrow(4)), "y_kept", c + 1)
                    signal(dve, dve.tensor_tensor(state[:, 0:PAIRS], state[:, 0:PAIRS], end, ALU.mult),
                           "chunk_done", c + 1)
                    nsa()
                    if c + 2 < CHUNKS:
                        make_packs(c + 2)
                    if c != 1:
                        centre_outputs(c)
            scale_outputs(CHUNKS - 2)
            for name, u in nsa_steps:
                nsa_step(name, u)
            split_lo(T_OUT2)
            for at in range(4):
                rest("mixer2", MIXER_ORDER[2][at], SEQ, yT, at)
            finish_outputs(CHUNKS - 2)
            for t in range(1, SLOTS):
                split_lo(T_OUT2 + t)

            mixer_output(2, T_OUT2)
            split_lo(T_UP2 + SLOTS - 1)
            normalise("norm_ff2", "norm5", META, SEQ)
            feed_forward(2, T_UP2)
            add_down(2)
            dve.wait_ge(S("norm_root"), nth("norm6"))
            for k in range(KT):
                dve.scalar_tensor_tensor(yT[:, k, :], res[:, k, META:CTX], V("norm6", k), nrm[:, 1, 0:SEQ],
                                         ALU.mult, ALU.mult).then_inc(S("final_ready"), 1)




def tiles_in(w):
    n = w.shape[1]
    t = -(-n // P)
    w = np.concatenate([w, np.zeros((w.shape[0], t * P - n), w.dtype)], 1)
    return w.reshape(KT, P, t, P).transpose(2, 1, 0, 3).reshape(t, P, TILE)


def to_blocks(tiles):
    if len(tiles) % 2:
        tiles = np.concatenate([tiles, np.zeros_like(tiles[:1])])
    return tiles.reshape(-1, 2, P, TILE).transpose(0, 2, 1, 3).reshape(-1, P, BLOCK)


def ffn_blocks(gate, up, down):
    g, u = tiles_in(gate), tiles_in(up)
    both = np.stack([g, u], 1).reshape(-1, P, TILE)
    return [to_blocks(both), to_blocks(down.reshape(FT, P, TILE))]


def cols(v):
    return v.reshape(-1, P).T


def layout(i):
    f = np.float32
    i = {k: np.asarray(v) for k, v in i.items()}
    w = i["w_in"][0]
    u, qf, kf, vf, fl, qs, ks, vs = np.split(w, np.cumsum([256, 384, 384, 384, 6, 384, 384]), 1)
    fl = np.concatenate([fl, np.zeros((D, P - fl.shape[1]), fl.dtype)], 1)
    w1 = np.concatenate([ks, qs, vs, vf, fl, kf, qf, u], 1)
    stream = [to_blocks(tiles_in(w1)), to_blocks(tiles_in(i["w_out"][0]))]
    stream += ffn_blocks(i["w_gate"][0], i["w_up"][0], i["w_down"][0])
    h = np.concatenate([i["meta_tokens"], i["x"][0]], 0)
    xT = h.T.reshape(KT, P, CTX).transpose(1, 0, 2).reshape(P, -1)
    vecs = {
        "norm1": cols(i["norm1"][0]), "norm2": cols(i["norm2"][0]), "norm3": cols(i["final_norm"]),
        "fox_gain": cols(i["fox_out_gain"][0]), "sb_gain": cols(i["sb_out_gain"][0]),
        "pool_scale": cols(i["pool_scale"][0]),
    }
    fb = np.zeros((P, 1), f)
    fb[0:6, 0] = i["forget_bias"][0]
    vecs["forget_bias"] = fb
    pw = np.zeros((P, 2, P), f)
    for g in range(4):
        r = HD * (g % 2)
        pw[r:r + HD, g // 2, r:r + HD] = i["pool_w"][0, g]
    vecs["pool_w"] = pw.reshape(P, -1)
    w = i["w_in_2"][0]
    rw, nsa = w[:, 0:SHIFTED * P], w[:, SHIFTED * P:]
    q, kvs, gl = nsa[:, 0:512], nsa[:, 512:1280], nsa[:, 1280:]
    q = q.reshape(D, KVH, GQA, HD).transpose(0, 2, 1, 3).reshape(D, -1)
    stream.append(to_blocks(tiles_in(np.concatenate([rw, q, kvs, gl], 1))))
    for n in ("nsa_cmp_k_w1_2", "nsa_cmp_v_w1_2"):
        stream.append(to_blocks(i[n][0].reshape(4, 4, P, CMP_HIDDEN).transpose(0, 2, 1, 3).reshape(4, P, TILE)))
    wo = i["w_out_2"][0]
    wn = wo[512:].reshape(KVH, GQA, HD, D).transpose(1, 0, 2, 3).reshape(512, D)
    stream.append(to_blocks(tiles_in(np.concatenate([wo[0:512], wn], 0))))
    stream += ffn_blocks(i["ffn_w_gate_2"][0], i["ffn_w_up_2"][0], i["ffn_w_down_2"][0])

    vecs |= {
        "norm4": cols(i["norm1_g_2"][0]), "norm5": cols(i["norm2_g_2"][0]), "norm6": cols(i["norm_f_g_2"]),
        "mu": cols(i["mu_shift_2"][0]), "w0": cols(i["rwkv_w0_2"][0]), "a0": cols(i["rwkv_a0_2"][0]),
        "k_k": cols(i["rwkv_k_k_2"][0]), "k_a": cols(i["rwkv_k_a_2"][0]), "r_k": cols(i["rwkv_r_k_2"][0]),
        "w2a2": np.concatenate([i["rwkv_w2_2"][0], i["rwkv_a2_2"][0]], 0),
        "g2": i["rwkv_g2_2"][0], "lnx_w": cols(i["rwkv_lnx_w_2"][0]), "lnx_b": cols(i["rwkv_lnx_b_2"][0]),
        "pe_k": i["nsa_pe_k_2"][0].reshape(CMP_PAIRS, P).T, "pe_v": i["nsa_pe_v_2"][0].reshape(CMP_PAIRS, P).T,
        "cmp_w2k": i["nsa_cmp_k_w2_2"][0].reshape(2, P, HD).transpose(1, 0, 2).reshape(P, -1),
        "cmp_w2v": i["nsa_cmp_v_w2_2"][0].reshape(2, P, HD).transpose(1, 0, 2).reshape(P, -1),
    }
    return {
        "xT": np.ascontiguousarray(xT), "weights": np.ascontiguousarray(np.concatenate(stream)),
        "consts": np.concatenate(list(constant_tables().values()), 1),
        "vecs": np.concatenate([vecs[k] for k in VEC_WIDTHS], 1),
    }


def kernel(**inputs):
    import concourse.bacc as bacc
    from concourse.bass_utils import run_bass_kernel_spmd

    nc = bacc.Bacc("TRN2", target_bir_lowering=False, num_devices=1)
    arrays, aps = {}, []
    for name, a in layout(inputs).items():
        a = np.ascontiguousarray(a)
        arrays[f"in_{name}"] = a
        aps.append(nc.dram_tensor(f"in_{name}", a.shape, mybir.dt.from_np(a.dtype), kind="ExternalInput").ap())
    out = nc.dram_tensor("out_features", (P, KT * SEQ), F32, kind="ExternalOutput").ap()
    build_program(nc, *aps, out)
    got = run_bass_kernel_spmd(nc, [arrays], core_ids=[0]).results[0]["out_features"]
    return got.reshape(P, KT, SEQ).transpose(2, 1, 0).reshape(1, SEQ, D)
```
